# Optimizing a Trainium2 kernel written in Bass

```python
import math
import jax, jax.numpy as jnp
from jax import lax
import numpy as np

D_MODEL = 1024
BATCH = 1
SEQ = 256
DEPTH = 1

MEM_LEN = 256
ROPE_THETA = 500000.0
EPS = 1e-6
NEG = -1e30
Q_BLOCK = 128
N_BRANCH = 3
BRANCH_WIDTH = 512
A_HEADS = 8
A_HEAD_DIM = 64
A_ROT = A_HEAD_DIM // 4
IDX_HEADS = 8
IDX_DIM = 64
IDX_ROT = IDX_DIM // 4
TOPK_MAX = 256
B_HEADS = 8
B_NOPE = 64
B_ROPE = 32
B_VDIM = 64
B_QK = B_NOPE + B_ROPE
B_Q_RANK = 384
B_KV_RANK = 256
M_HEADS = 4
M_HEAD_DIM = 128

SPLITS = (
    A_HEADS * A_HEAD_DIM,
    A_HEADS * A_HEAD_DIM,
    A_HEADS * A_HEAD_DIM,
    IDX_HEADS * IDX_DIM,
    IDX_DIM,
    IDX_HEADS,
    BRANCH_WIDTH,
    B_Q_RANK,
    B_KV_RANK,
    B_ROPE,
    BRANCH_WIDTH,
    M_HEADS * M_HEAD_DIM,
    BRANCH_WIDTH,
    N_BRANCH * D_MODEL,
)
D_IN = (4 * A_HEADS * A_HEAD_DIM + IDX_DIM + IDX_HEADS + BRANCH_WIDTH
        + B_Q_RANK + B_KV_RANK + B_ROPE + BRANCH_WIDTH
        + M_HEADS * M_HEAD_DIM + BRANCH_WIDTH + N_BRANCH * D_MODEL)


def rms_norm(x, g):
    xf = x.astype(jnp.float32)
    y = xf * lax.rsqrt(jnp.mean(xf * xf, axis=-1, keepdims=True) + EPS)
    return (y * g.astype(jnp.float32)).astype(x.dtype)

def rope_tables(positions, rot_dim):
    inv_freq = ROPE_THETA ** (-(jnp.arange(0, rot_dim, 2, dtype=jnp.float32) / rot_dim))
    ang = positions.astype(jnp.float32)[..., None] * inv_freq
    return jnp.cos(ang), jnp.sin(ang)

def rotate(x, cos, sin):
    half = x.shape[-1] // 2
    x1 = x[..., :half].astype(jnp.float32)
    x2 = x[..., half:].astype(jnp.float32)
    return jnp.concatenate([x1 * cos - x2 * sin, x2 * cos + x1 * sin], axis=-1).astype(x.dtype)

def partial_rope(x, cos, sin):
    rd = 2 * cos.shape[-1]
    return jnp.concatenate([rotate(x[..., :rd], cos, sin), x[..., rd:]], axis=-1)

def to_blocks(t, nb):
    b = t.shape[0]
    return jnp.moveaxis(t.reshape((b, nb, Q_BLOCK) + t.shape[2:]), 1, 0)

def from_blocks(t):
    t = jnp.moveaxis(t, 0, 1)
    return t.reshape((t.shape[0], t.shape[1] * t.shape[2]) + t.shape[3:])

def dsa_attention(q, k, v, qi, ki, wi):
    b, s, h, d = q.shape
    nb = s // Q_BLOCK
    topk = min(TOPK_MAX, s // 4)
    key_pos = jnp.arange(s)
    ki_f = ki.astype(jnp.float32)
    scale = d ** -0.5

    def one_block(args):
        qb, qib, wib, start = args
        q_pos = start + jnp.arange(Q_BLOCK)
        causal = key_pos[None, :] <= q_pos[:, None]
        dots = jnp.einsum('bqhc,bsc->bhqs', qib.astype(jnp.float32), ki_f) * (IDX_DIM ** -0.5)
        index = jnp.einsum('bhqs,bqh->bqs', jax.nn.relu(dots),
                           wib.astype(jnp.float32) * (IDX_HEADS ** -0.5))
        index = jnp.where(causal[None], index, NEG)
        _, idx = lax.top_k(index, topk)
        valid = idx <= q_pos[None, :, None]
        k_sel = jax.vmap(lambda kb, ib: kb[ib])(k, idx)
        v_sel = jax.vmap(lambda vb, ib: vb[ib])(v, idx)
        sc = jnp.einsum('bqhd,bqkhd->bhqk', qb, k_sel).astype(jnp.float32) * scale
        sc = jnp.where(valid[:, None], sc, NEG)
        p = jax.nn.softmax(sc, axis=-1).astype(v.dtype)
        return jnp.einsum('bhqk,bqkhd->bqhd', p, v_sel)

    starts = jnp.arange(nb) * Q_BLOCK
    out = lax.map(one_block, (to_blocks(q, nb), to_blocks(qi, nb), to_blocks(wi, nb), starts))
    return from_blocks(out)

def causal_attention(q, k, v):
    b, s, h, dq = q.shape
    nb = s // Q_BLOCK
    key_pos = jnp.arange(s)
    scale = dq ** -0.5

    def one_block(args):
        qb, start = args
        q_pos = start + jnp.arange(Q_BLOCK)
        sc = jnp.einsum('bqhd,bkhd->bhqk', qb, k).astype(jnp.float32) * scale
        sc = jnp.where((key_pos[None, :] <= q_pos[:, None])[None, None], sc, NEG)
        p = jax.nn.softmax(sc, axis=-1).astype(v.dtype)
        return jnp.einsum('bhqk,bkhd->bqhd', p, v)

    starts = jnp.arange(nb) * Q_BLOCK
    return from_blocks(lax.map(one_block, (to_blocks(q, nb), starts)))

def first_inputs(seed: int = 0) -> dict:
    key = jax.random.key(seed)
    ks = jax.random.split(key, 24)
    f32 = jnp.float32

    def w(k, shape, fan_in):
        return jax.random.normal(k, shape, f32) * (fan_in ** -0.5)

    def gain(k, shape):
        return 1.0 + 0.02 * jax.random.normal(k, shape, f32)

    x = jax.random.normal(ks[0], (BATCH, SEQ, D_MODEL), f32)
    mem = jax.random.normal(ks[1], (BATCH, MEM_LEN, D_MODEL), f32)
    offsets = jax.random.randint(ks[2], (BATCH, 1), 0, 4096, dtype=jnp.int32)
    positions = offsets + jnp.arange(SEQ, dtype=jnp.int32)[None, :]
    return {
        "x": x,
        "mem": mem,
        "positions": positions,
        "g_norm": gain(ks[3], (DEPTH, D_MODEL)),
        "w_in": w(ks[4], (DEPTH, D_MODEL, D_IN), D_MODEL),
        "g_qn_a": gain(ks[5], (DEPTH, A_HEAD_DIM)),
        "g_kn_a": gain(ks[6], (DEPTH, A_HEAD_DIM)),
        "g_cq": gain(ks[7], (DEPTH, B_Q_RANK)),
        "g_ckv": gain(ks[8], (DEPTH, B_KV_RANK)),
        "w_uq": w(ks[9], (DEPTH, B_Q_RANK, B_HEADS * B_QK), B_Q_RANK),
        "w_ukv": w(ks[10], (DEPTH, B_KV_RANK, B_HEADS * (B_NOPE + B_VDIM)), B_KV_RANK),
        "g_qn_b": gain(ks[11], (DEPTH, B_QK)),
        "g_kn_b": gain(ks[12], (DEPTH, B_QK)),
        "g_mem": gain(ks[13], (DEPTH, D_MODEL)),
        "w_mem_kv": w(ks[14], (DEPTH, D_MODEL, 2 * M_HEADS * M_HEAD_DIM), D_MODEL),
        "g_qn_m": gain(ks[15], (DEPTH, M_HEAD_DIM)),
        "g_kn_m": gain(ks[16], (DEPTH, M_HEAD_DIM)),
        "w_branch": w(ks[17], (DEPTH, N_BRANCH, BRANCH_WIDTH, D_MODEL), BRANCH_WIDTH),
        "w_out": w(ks[18], (DEPTH, D_MODEL, D_MODEL), D_MODEL),
    }

def first_block(x, mem, positions, g_norm, w_in, g_qn_a, g_kn_a, g_cq, g_ckv, w_uq, w_ukv,
              g_qn_b, g_kn_b, g_mem, w_mem_kv, g_qn_m, g_kn_m, w_branch, w_out):
    b, s, _ = x.shape
    m_len = mem.shape[1]
    cos_a, sin_a = rope_tables(positions, A_ROT)
    cos_b, sin_b = rope_tables(positions, B_ROPE)
    split_at = [int(o) for o in np.cumsum(SPLITS)[:-1]]

    for layer in range(DEPTH):
        h = rms_norm(x, g_norm[layer])
        proj = h @ w_in[layer]
        (q_a, k_a, v_a, q_i, k_i, w_i, z_a, c_q, c_kv, k_rope, z_b, q_m, z_m,
         gate_logits) = jnp.split(proj, split_at, axis=-1)

        q_a = partial_rope(rms_norm(q_a.reshape(b, s, A_HEADS, A_HEAD_DIM), g_qn_a[layer]),
                           cos_a[:, :, None], sin_a[:, :, None])
        k_a = partial_rope(rms_norm(k_a.reshape(b, s, A_HEADS, A_HEAD_DIM), g_kn_a[layer]),
                           cos_a[:, :, None], sin_a[:, :, None])
        v_a = v_a.reshape(b, s, A_HEADS, A_HEAD_DIM)
        q_i = partial_rope(q_i.reshape(b, s, IDX_HEADS, IDX_DIM), cos_a[:, :, None], sin_a[:, :, None])
        k_i = partial_rope(k_i, cos_a, sin_a)
        o_a = dsa_attention(q_a, k_a, v_a, q_i, k_i, w_i)

        q_b = (rms_norm(c_q, g_cq[layer]) @ w_uq[layer]).reshape(b, s, B_HEADS, B_QK)
        kv_b = (rms_norm(c_kv, g_ckv[layer]) @ w_ukv[layer]).reshape(b, s, B_HEADS, B_NOPE + B_VDIM)
        k_nope, v_b = kv_b[..., :B_NOPE], kv_b[..., B_NOPE:]
        k_b = jnp.concatenate(
            [k_nope, jnp.broadcast_to(k_rope[:, :, None, :], (b, s, B_HEADS, B_ROPE))], axis=-1)
        q_b = rms_norm(q_b, g_qn_b[layer])
        k_b = rms_norm(k_b, g_kn_b[layer])
        q_b = jnp.concatenate(
            [q_b[..., :B_NOPE], rotate(q_b[..., B_NOPE:], cos_b[:, :, None], sin_b[:, :, None])], axis=-1)
        k_b = jnp.concatenate(
            [k_b[..., :B_NOPE], rotate(k_b[..., B_NOPE:], cos_b[:, :, None], sin_b[:, :, None])], axis=-1)
        o_b = causal_attention(q_b, k_b, v_b)

        kv_m = (rms_norm(mem, g_mem[layer]) @ w_mem_kv[layer]).reshape(b, m_len, 2, M_HEADS, M_HEAD_DIM)
        k_m = rms_norm(kv_m[:, :, 0], g_kn_m[layer])
        v_m = kv_m[:, :, 1]
        q_m = rms_norm(q_m.reshape(b, s, M_HEADS, M_HEAD_DIM), g_qn_m[layer])
        sc_m = jnp.einsum('bqhd,bmhd->bhqm', q_m, k_m).astype(jnp.float32) * (M_HEAD_DIM ** -0.5)
        p_m = jax.nn.softmax(sc_m, axis=-1).astype(v_m.dtype)
        o_m = jnp.einsum('bhqm,bmhd->bqhd', p_m, v_m)

        ys = jnp.stack([
            o_a.reshape(b, s, BRANCH_WIDTH) * jax.nn.silu(z_a),
            o_b.reshape(b, s, BRANCH_WIDTH) * jax.nn.silu(z_b),
            o_m.reshape(b, s, BRANCH_WIDTH) * jax.nn.silu(z_m),
        ], axis=0)
        branch = jnp.einsum('nbsw,nwd->nbsd', ys, w_branch[layer])
        gates = jax.nn.sigmoid(
            gate_logits.reshape(b, s, N_BRANCH, D_MODEL).astype(jnp.float32)).astype(x.dtype)
        merged = jnp.einsum('bsnd,nbsd->bsd', gates, branch)
        x = x + merged @ w_out[layer]
    return x


CHUNK = 64

DA_HEADS = 4
DA_QK_DIM = D_MODEL // 16
DA_V_DIM = 2 * DA_QK_DIM
DA_QK_COLS = DA_HEADS * 2 * DA_QK_DIM
DA_WIDTH = DA_HEADS * DA_V_DIM

GLA_HEADS = 4
GLA_K_DIM = D_MODEL // 16
GLA_V_DIM = D_MODEL // 8
GLA_QK_COLS = GLA_HEADS * GLA_K_DIM
GLA_WIDTH = GLA_HEADS * GLA_V_DIM
GLA_GATE_RANK = 16
GLA_TAU = 16.0

MIX_WIDTH = DA_WIDTH + GLA_WIDTH
IN_WIDTH = 2 * DA_QK_COLS + DA_WIDTH + 2 * GLA_QK_COLS + 2 * GLA_WIDTH + GLA_GATE_RANK

CROSS_HEADS = 4
CROSS_DIM = D_MODEL // CROSS_HEADS

N_GROUPS = 4
EXPERTS_PER_GROUP = 8
N_EXPERTS = N_GROUPS * EXPERTS_PER_GROUP
TOP_K = 2
D_EXPERT = D_MODEL // 2
EXPERT_BLOCK = 128


def _rmsnorm(t, g):
    tf = t.astype(jnp.float32)
    tf = tf * lax.rsqrt(jnp.mean(tf * tf, axis=-1, keepdims=True) + EPS)
    return (tf * g.astype(jnp.float32)).astype(t.dtype)

def _split_heads(t, n):
    b, s, _ = t.shape
    return t.reshape(b, s, n, -1).transpose(0, 2, 1, 3)

def _merge_heads(t):
    b, h, s, d = t.shape
    return t.transpose(0, 2, 1, 3).reshape(b, s, h * d)

def _diff_attention(q1, q2, k1, k2, v, lam):
    b, h, s, d = q1.shape
    n_blocks = s // Q_BLOCK
    scale = d ** -0.5
    key_chunk = jnp.arange(s) // CHUNK

    def to_blocks(t):
        return t.reshape(b, h, n_blocks, Q_BLOCK, d).transpose(2, 0, 1, 3, 4)

    def one_block(args):
        qb1, qb2, bi = args
        q_chunk = (bi * Q_BLOCK + jnp.arange(Q_BLOCK)) // CHUNK
        mask = key_chunk[None, :] <= q_chunk[:, None]

        def probs(qb, kk):
            sc = jnp.einsum('bhqd,bhkd->bhqk', qb, kk).astype(jnp.float32) * scale
            return jax.nn.softmax(jnp.where(mask, sc, -jnp.inf), axis=-1)

        p = probs(qb1, k1) - lam * probs(qb2, k2)
        return jnp.einsum('bhqk,bhkv->bhqv', p.astype(v.dtype), v)

    o = lax.map(one_block, (to_blocks(q1), to_blocks(q2), jnp.arange(n_blocks)))
    return o.transpose(1, 2, 0, 3, 4).reshape(b, h, s, v.shape[-1])

def _gla_chunked(q, k, v, log_a):
    b, h, s, dk = q.shape
    dv = v.shape[-1]
    nc = s // CHUNK
    q = q.reshape(b, h, nc, CHUNK, dk)
    k = k.reshape(b, h, nc, CHUNK, dk)
    v = v.reshape(b, h, nc, CHUNK, dv)
    L = jnp.cumsum(log_a.reshape(b, h, nc, CHUNK, dk), axis=3)
    L_end = L[:, :, :, -1, :]
    Lc = L - L[:, :, :, CHUNK // 2 - 1:CHUNK // 2, :]
    e_pos, e_neg = jnp.exp(Lc), jnp.exp(-Lc)
    a_past = jnp.einsum('bhnid,bhnjd->bhnij', q * e_pos, k * e_neg)
    a_fut = jnp.einsum('bhnid,bhnjd->bhnij', q * e_neg, k * e_pos)
    lower = jnp.tril(jnp.ones((CHUNK, CHUNK), dtype=bool))
    a = jnp.where(lower, a_past, a_fut)
    o_intra = jnp.einsum('bhnij,bhnjv->bhniv', a, v)
    u = jnp.einsum('bhnjd,bhnjv->bhndv', k * jnp.exp(L_end[:, :, :, None, :] - L), v)
    decay = jnp.exp(L_end)

    def step(state, inp):
        d_c, u_c = inp
        return state * d_c[..., None] + u_c, state

    _, s_prev = lax.scan(step, jnp.zeros((b, h, dk, dv), jnp.float32),
                         (jnp.moveaxis(decay, 2, 0), jnp.moveaxis(u, 2, 0)))
    s_prev = jnp.moveaxis(s_prev, 0, 2)
    o_inter = jnp.einsum('bhnid,bhndv->bhniv', q * jnp.exp(L), s_prev)
    return (o_intra + o_inter).reshape(b, h, s, dv)

def _mixer(h, norm_g, w_in, da_qn, da_kn, lq1, lk1, lq2, lk2, da_on, gate_w, gate_b, gla_on, w_o, lam_init):
    b, s, _ = h.shape
    f32 = jnp.float32
    u = _rmsnorm(h, norm_g)
    p = u @ w_in
    widths = (DA_QK_COLS, DA_QK_COLS, DA_WIDTH, GLA_QK_COLS, GLA_QK_COLS, GLA_WIDTH, GLA_WIDTH, GLA_GATE_RANK)
    parts = []
    off = 0
    for w in widths:
        parts.append(p[..., off:off + w])
        off += w
    dq, dk, dv, gq, gk, gv, gg, gr = parts

    dq = dq.reshape(b, s, DA_HEADS, 2, DA_QK_DIM).transpose(0, 2, 3, 1, 4)
    dk = dk.reshape(b, s, DA_HEADS, 2, DA_QK_DIM).transpose(0, 2, 3, 1, 4)
    dq = _rmsnorm(dq, da_qn)
    dk = _rmsnorm(dk, da_kn)
    dvh = _split_heads(dv, DA_HEADS)
    lam = (jnp.exp(jnp.sum(lq1.astype(f32) * lk1.astype(f32)))
           - jnp.exp(jnp.sum(lq2.astype(f32) * lk2.astype(f32))) + lam_init)
    da = _diff_attention(dq[:, :, 0], dq[:, :, 1], dk[:, :, 0], dk[:, :, 1], dvh, lam)
    da = _rmsnorm(da, da_on) * (1.0 - lam_init)
    da_out = _merge_heads(da)

    qg = _split_heads(gq, GLA_HEADS).astype(f32) * (GLA_K_DIM ** -0.5)
    kg = _split_heads(gk, GLA_HEADS).astype(f32)
    vg = _split_heads(gv, GLA_HEADS).astype(f32)
    z = gr.astype(f32) @ gate_w.astype(f32) + gate_b.astype(f32)
    log_a = _split_heads(jax.nn.log_sigmoid(z) / GLA_TAU, GLA_HEADS)
    og = _gla_chunked(qg, kg, vg, log_a)
    og = _rmsnorm(og, gla_on)
    gla_out = (_merge_heads(og) * jax.nn.silu(gg.astype(f32))).astype(h.dtype)

    return jnp.concatenate([da_out.astype(h.dtype), gla_out], axis=-1) @ w_o

def _cross_attention(h, mem, norm_g, norm_m, w_q, w_kv, qn, kn, w_out):
    b, s, d = h.shape
    m = mem.shape[1]
    u = _rmsnorm(h, norm_g)
    mn = _rmsnorm(mem, norm_m)
    q = _rmsnorm((u @ w_q).reshape(b, s, CROSS_HEADS, CROSS_DIM), qn)
    kv = mn @ w_kv
    k = _rmsnorm(kv[..., :d].reshape(b, m, CROSS_HEADS, CROSS_DIM), kn)
    v = kv[..., d:].reshape(b, m, CROSS_HEADS, CROSS_DIM)
    sc = jnp.einsum('bshd,bmhd->bhsm', q, k).astype(jnp.float32) * (CROSS_DIM ** -0.5)
    pr = jax.nn.softmax(sc, axis=-1).astype(v.dtype)
    o = jnp.einsum('bhsm,bmhd->bshd', pr, v).reshape(b, s, d)
    return o @ w_out

def _hier_moe(h, norm_g, w_group, b_group, w_expert, b_expert, w_gate, w_up, w_down):
    b, s, d = h.shape
    t = b * s
    f32 = jnp.float32
    xf = _rmsnorm(h, norm_g).reshape(t, d)
    xr = xf.astype(f32)
    p_group = jax.nn.softmax(xr @ w_group.astype(f32) + b_group.astype(f32), axis=-1)
    g_sel = jnp.argmax(p_group, axis=-1)
    p_g = jnp.take_along_axis(p_group, g_sel[:, None], axis=-1)
    e_logits = (xr @ w_expert.astype(f32) + b_expert.astype(f32)).reshape(t, N_GROUPS, EXPERTS_PER_GROUP)
    e_logits = jnp.take_along_axis(e_logits, g_sel[:, None, None], axis=1)[:, 0]
    top_p, top_i = lax.top_k(jax.nn.softmax(e_logits, axis=-1), TOP_K)
    gate = p_g * top_p / jnp.sum(top_p, axis=-1, keepdims=True)
    flat_id = (g_sel[:, None] * EXPERTS_PER_GROUP + top_i).reshape(-1).astype(jnp.int32)
    flat_gate = gate.reshape(-1)
    n_assign = t * TOP_K
    order = jnp.argsort(flat_id)
    sorted_id = flat_id[order]
    token_of = order // TOP_K
    sizes = jnp.bincount(flat_id, length=N_EXPERTS)
    padded = (sizes + EXPERT_BLOCK - 1) // EXPERT_BLOCK * EXPERT_BLOCK
    start = jnp.cumsum(sizes) - sizes
    padded_end = jnp.cumsum(padded)
    padded_start = padded_end - padded
    dest = padded_start[sorted_id] + jnp.arange(n_assign) - start[sorted_id]
    n_rows = n_assign + N_EXPERTS * EXPERT_BLOCK
    n_blocks = n_rows // EXPERT_BLOCK
    x_pad = jnp.zeros((n_rows, d), xf.dtype).at[dest].set(xf[token_of])
    block_expert = jnp.minimum(
        jnp.searchsorted(padded_end, jnp.arange(n_blocks) * EXPERT_BLOCK, side='right'), N_EXPERTS - 1)

    def expert_block(args):
        xb, e = args
        hid = jax.nn.silu(xb @ w_gate[e]) * (xb @ w_up[e])
        return hid @ w_down[e]

    out_pad = lax.map(expert_block, (x_pad.reshape(n_blocks, EXPERT_BLOCK, d), block_expert)).reshape(n_rows, d)
    out = out_pad[dest] * flat_gate[order][:, None].astype(out_pad.dtype)
    y = jnp.zeros((t, d), out.dtype).at[token_of].add(out)
    return y.reshape(b, s, d).astype(h.dtype)

def second_inputs(seed: int = 0) -> dict:
    key = jax.random.key(seed)
    ks = iter(jax.random.split(key, 40))
    f32 = jnp.float32
    D = D_MODEL

    def nrm(shape, scale):
        return scale * jax.random.normal(next(ks), shape, f32)

    def gain(n):
        return 1.0 + 0.02 * jax.random.normal(next(ks), (DEPTH, n), f32)

    return {
        'x': nrm((BATCH, SEQ, D), 1.0),
        'mem': nrm((BATCH, MEM_LEN, D), 1.0),
        'norm_mix': gain(D),
        'w_in': nrm((DEPTH, D, IN_WIDTH), D ** -0.5),
        'da_q_norm': gain(DA_QK_DIM),
        'da_k_norm': gain(DA_QK_DIM),
        'lambda_q1': nrm((DEPTH, DA_QK_DIM), 0.1),
        'lambda_k1': nrm((DEPTH, DA_QK_DIM), 0.1),
        'lambda_q2': nrm((DEPTH, DA_QK_DIM), 0.1),
        'lambda_k2': nrm((DEPTH, DA_QK_DIM), 0.1),
        'da_out_norm': gain(DA_V_DIM),
        'gla_gate_w': nrm((DEPTH, GLA_GATE_RANK, GLA_QK_COLS), GLA_GATE_RANK ** -0.5),
        'gla_gate_b': nrm((DEPTH, GLA_QK_COLS), 0.1),
        'gla_out_norm': gain(GLA_V_DIM),
        'w_o': nrm((DEPTH, MIX_WIDTH, D), MIX_WIDTH ** -0.5),
        'norm_cross': gain(D),
        'norm_mem': gain(D),
        'w_cq': nrm((DEPTH, D, D), D ** -0.5),
        'w_ckv': nrm((DEPTH, D, 2 * D), D ** -0.5),
        'cross_q_norm': gain(CROSS_DIM),
        'cross_k_norm': gain(CROSS_DIM),
        'w_co': nrm((DEPTH, D, D), D ** -0.5),
        'norm_ffn': gain(D),
        'w_group': nrm((DEPTH, D, N_GROUPS), D ** -0.5),
        'b_group': nrm((DEPTH, N_GROUPS), 0.01),
        'w_expert': nrm((DEPTH, D, N_EXPERTS), D ** -0.5),
        'b_expert': nrm((DEPTH, N_EXPERTS), 0.01),
        'w_e_gate': nrm((DEPTH, N_EXPERTS, D, D_EXPERT), D ** -0.5),
        'w_e_up': nrm((DEPTH, N_EXPERTS, D, D_EXPERT), D ** -0.5),
        'w_e_down': nrm((DEPTH, N_EXPERTS, D_EXPERT, D), D_EXPERT ** -0.5),
    }

def second_block(x, mem, norm_mix, w_in, da_q_norm, da_k_norm, lambda_q1, lambda_k1, lambda_q2, lambda_k2,
              da_out_norm, gla_gate_w, gla_gate_b, gla_out_norm, w_o, norm_cross, norm_mem, w_cq, w_ckv,
              cross_q_norm, cross_k_norm, w_co, norm_ffn, w_group, b_group, w_expert, b_expert,
              w_e_gate, w_e_up, w_e_down):
    h = x
    for l in range(DEPTH):
        lam_init = 0.8 - 0.6 * math.exp(-0.3 * l)
        h = h + _mixer(h, norm_mix[l], w_in[l], da_q_norm[l], da_k_norm[l], lambda_q1[l], lambda_k1[l],
                       lambda_q2[l], lambda_k2[l], da_out_norm[l], gla_gate_w[l], gla_gate_b[l],
                       gla_out_norm[l], w_o[l], lam_init)
        h = h + _cross_attention(h, mem, norm_cross[l], norm_mem[l], w_cq[l], w_ckv[l],
                                 cross_q_norm[l], cross_k_norm[l], w_co[l])
        h = h + _hier_moe(h, norm_ffn[l], w_group[l], b_group[l], w_expert[l], b_expert[l],
                          w_e_gate[l], w_e_up[l], w_e_down[l])
    return h


def setup_inputs(seed=0):
    out = dict(first_inputs(seed))
    for name, value in second_inputs(seed + 1).items():
        if name != "x":
            out[name + "_2"] = value
    return out


def reference(
    x, mem, positions, g_norm, w_in, g_qn_a, g_kn_a, g_cq, g_ckv, w_uq, w_ukv, g_qn_b, g_kn_b,
    g_mem, w_mem_kv, g_qn_m, g_kn_m, w_branch, w_out, mem_2, norm_mix_2, w_in_2, da_q_norm_2,
    da_k_norm_2, lambda_q1_2, lambda_k1_2, lambda_q2_2, lambda_k2_2, da_out_norm_2,
    gla_gate_w_2, gla_gate_b_2, gla_out_norm_2, w_o_2, norm_cross_2, norm_mem_2, w_cq_2,
    w_ckv_2, cross_q_norm_2, cross_k_norm_2, w_co_2, norm_ffn_2, w_group_2, b_group_2,
    w_expert_2, b_expert_2, w_e_gate_2, w_e_up_2, w_e_down_2,
):
    x = first_block(
        x, mem, positions, g_norm, w_in, g_qn_a, g_kn_a, g_cq, g_ckv, w_uq, w_ukv, g_qn_b,
        g_kn_b, g_mem, w_mem_kv, g_qn_m, g_kn_m, w_branch, w_out,
    )
    return second_block(
        x, mem_2, norm_mix_2, w_in_2, da_q_norm_2, da_k_norm_2, lambda_q1_2, lambda_k1_2,
        lambda_q2_2, lambda_k2_2, da_out_norm_2, gla_gate_w_2, gla_gate_b_2, gla_out_norm_2,
        w_o_2, norm_cross_2, norm_mem_2, w_cq_2, w_ckv_2, cross_q_norm_2, cross_k_norm_2,
        w_co_2, norm_ffn_2, w_group_2, b_group_2, w_expert_2, b_expert_2, w_e_gate_2, w_e_up_2,
        w_e_down_2,
    )


_drawn_inputs = setup_inputs


def setup_inputs(seed=0):
    import zlib

    import numpy as np

    out = dict(_drawn_inputs(seed))
    spreads = {}
    factors = {'g_qn_a': 4.446,
     'g_kn_a': 7.616,
     'g_cq': 5.809,
     'g_ckv': 5.054,
     'g_qn_b': 5.232,
     'g_kn_b': 5.168,
     'g_mem': 8.0,
     'g_qn_m': 6.777,
     'g_kn_m': 7.871,
     'da_out_norm_2': 2.77,
     'norm_cross_2': 8.0,
     'norm_mem_2': 4.029,
     'cross_q_norm_2': 8.0,
     'cross_k_norm_2': 5.317,
     'b_group_2': 28.64,
     'b_expert_2': 29.377,
     'gla_out_norm_2': 4.15,
     'norm_ffn_2': 8.0}
    for name, (base, spread) in spreads.items():
        noise = np.random.default_rng([zlib.crc32(name.encode()), seed]).standard_normal(out[name].shape)
        drawn = base * np.exp(spread * noise) if base else spread * noise
        out[name] = __import__('jax').numpy.asarray(drawn.astype(out[name].dtype))
    for name, factor in factors.items():
        out[name] = (out[name] * factor).astype(out[name].dtype)
    return out
```

```python
import math
from contextlib import ExitStack

import numpy as np

import concourse.bass as bass
from concourse import mybir

F32 = mybir.dt.float32
I32 = mybir.dt.int32
U32 = mybir.dt.uint32
ALU = mybir.AluOpType
ACT = mybir.ActivationFunctionType
AX_X = mybir.AxisListType.X

P = 128
D = 1024
S = 256
TT = S // P
KD = D // P
EPS = 1e-6
NEG = -1e30
TAKEN = -3e38
THETA = 500000.0
CHUNK = 64
TOPK = 64
N_EXPERTS = 32
N_GROUPS = 4
PER_GROUP = N_EXPERTS // N_GROUPS
D_EXPERT = 512
CAP = 64
PAIRS = N_EXPERTS // 2
LAM_INIT = 0.8 - 0.6 * math.exp(0.0)
RSQRT_SEED = float(0x5F3759DF)
SLOT = KD * 512
RING = 4

IN_QA, IN_KI, IN_ZA, IN_CQ, IN_CKV, IN_ZB, IN_QM, IN_ZM, IN_GATES = 0, 2048, 2120, 2632, 3016, 3304, 3816, 4328, 4840
PJ_QA, PJ_KA, PJ_VA, PJ_QI, PJ_KI, PJ_WI, PJ_CKV, PJ_KR, PJ_CQ, PJ_QM, PJ_W = 0, 512, 1024, 1536, 2048, 2112, 2120, 2376, 2408, 2792, 3304
GC_NORM, GC_MEM, GC_MIX, GC_CROSS, GC_MEM2, GC_FFN, GC_CQ, GC_CKV, GC_GATEB, GC_N = 0, 8, 16, 24, 32, 40, 48, 51, 53, 55
GB_A, GB_B, GB_M, GB_DA, GB_DAO, GB_GLAO, GB_X, GB_ROUTE, GB_LAM, GB_N = 0, 128, 320, 576, 704, 832, 960, 1472, 1508, 1764


def two_block_layer(nc, A, out):
    ctx = ExitStack()
    with ctx:
        def sb(name, cols, dt=F32, parts=P):
            return ctx.enter_context(nc.sbuf_tensor(name, [parts, cols], dt))

        def sem(name):
            return ctx.enter_context(nc.semaphore(name))

        ring = sb("ring", RING * SLOT)
        PJ = sb("PJ", 2 * SLOT)
        X = sb("X", TT * D)
        XT = sb("XT", KD * S)
        R1 = sb("R1", TT * D)
        R2 = sb("R2", KD * S)
        R3 = sb("R3", TT * D)
        R4 = sb("R4", 1536)
        R5 = sb("R5", 4096)
        ZT = sb("ZT", 3072)
        SQ = sb("SQ", 2048)
        SM = sb("SM", 1024)
        EX = sb("EX", 1024)
        PT = sb("PT", 1024)
        IX = sb("IX", 768)
        SEL = sb("SEL", TT * S)
        ident = sb("ident", P)
        causal = sb("causal", S)
        past = sb("past", P)
        future = sb("future", P)
        before = sb("before", P)
        ones = sb("ones", P)
        zeros = sb("zeros", P)
        iota = sb("iota", CAP)
        pref = sb("pref", 16)
        freq = sb("freq", 16)
        GC = sb("GC", GC_N)
        GB = sb("GB", GB_N)
        pos_i = sb("pos_i", TT, I32)
        trig = PJ[:, 7936:8128]
        iota_i = trig[:, 0:CAP].bitcast(I32)
        GW = PJ[0:16, 7680:7936]
        GRT = R4[0:16, 0:S]
        WR = R4[:, 0:KD * 36]
        RT = R4[:, 512:1056]
        GR = EX[0:GC_N, 512:640]
        ROT = PT[:, 0:512]
        MS = sb("MS", 32)
        NW = sb("NW", 4 * 32)
        NWI = sb("NWI", 32, I32)
        RS = sb("RS", 32)
        SMALL = sb("SMALL", 64)
        FLAG = sb("FLAG", 1, I32)

        slots = [ring[:, i * SLOT:(i + 1) * SLOT] for i in range(RING)] + [PJ[:, 0:SLOT], PJ[:, SLOT:2 * SLOT]]

        def v2(t, n=D):
            return t[:, 0:TT * n].rearrange("p (t n) -> p t n", t=TT)

        def kt(ap, k):
            return ap.rearrange("p (k s) -> p k s", k=k)

        X3, R1v, R3v = v2(X), v2(R1), v2(R3)
        ZTv = v2(ZT)
        XT3, R2T = kt(XT[:, :], KD), kt(R2[:, :], KD)
        PJ3 = PJ[:, 0:TT * PJ_W].rearrange("p (t n) -> p t n", t=TT)
        QB = R4[:, :].rearrange("p (t n) -> p t n", t=TT)
        KB = R2[:, 0:1536].rearrange("p (t h d) -> p t h d", t=TT, h=8)
        KNB = R3[:, 0:1024].rearrange("p (t h d) -> p t h d", t=TT, h=8)
        VB = R3[:, 1024:2048].rearrange("p (t h d) -> p t h d", t=TT, h=8)
        CQT, CKVT = kt(R2[:, 0:768], 3), kt(R2[:, 768:1280], 2)
        YT = kt(ZT[:, :], 12)
        QPAD = kt(R5[:, 0:2048], 8)
        KT4 = kt(R5[:, 2048:3072], 4)
        KIT = R5[:, 2048:2304]
        QBT, KBT = kt(R5[:, 0:2048], 8), kt(R5[:, 2048:4096], 8)
        QMT, KMT = kt(R5[:, 0:1024], 4), kt(R5[:, 1024:2048], 4)
        IX3, SEL3 = v2(IX, S), v2(SEL, S)
        R_sel = RT[:, 0:64].rearrange("p (t n) -> p t n", t=TT)
        DQ, DK, DV, GV, GG = (PJ[:, i * 1024:(i + 1) * 1024].rearrange("p (t n) -> p t n", t=TT) for i in range(5))
        KNZ, KPZ, QLZ = (kt(ZT[:, i * 1024:(i + 1) * 1024], 4) for i in range(3))
        QP, QN, KE = (kt(PJ[:, 5120 + i * 512:5632 + i * 512], 2) for i in range(3))
        KEN = PJ[:, 6656:7680].rearrange("p (c n d) -> p c n d", c=2, n=4)
        ATT = R5[:, 3072:4096].rearrange("p (t h q) -> p t h q", t=TT, h=4)
        ST = IX[:, 0:768].rearrange("p (c h v) -> p c h v", c=3, h=2)
        LZ, LA, LG_, LSUM = (T[:, i * 512:(i + 1) * 512] for T in (SM, EX) for i in range(2))
        LC, LE = (PT[:, i * 512:(i + 1) * 512] for i in range(2))
        EP, EN = IX[:, 0:512], SEL[:, :]
        EL, EE, GQ, GK = (R3[:, i * 512:(i + 1) * 512] for i in range(4))
        OG = SQ[:, 1024:2048].rearrange("p (t n) -> p t n", t=TT)
        CQ8, CK8 = kt(R5[:, 0:2048], 8), kt(R5[:, 2048:4096], 8)
        VM = R1v[:, :, 512:1024]
        TH = [R3[:, h * 1024:(h + 1) * 1024].rearrange("p (t n) -> p t n", t=TT) for h in range(2)]
        WI = SMALL[:, 32:48].rearrange("p (t n) -> p t n", t=TT)
        DEC = SMALL[:, 56:64]

        def stat(u, k):
            c = 8 * (u % 2) + 2 * k
            return SMALL[:, c:c + 2]

        def rt(c, *dims):
            n = int(np.prod(dims))
            ap = RT[:, c:c + n]
            if len(dims) == 2:
                return ap.rearrange("p (t n) -> p t n", t=dims[0])
            return ap.rearrange("p (t g j) -> p t g j", t=dims[0], g=dims[1]) if len(dims) == 3 else ap

        R_log, R_m, R_m1, R_m2 = rt(64, TT, 36), rt(136, TT), rt(138, TT), rt(140, TT)
        R_w4, R_gs, R_w8, R_el = rt(144, TT, 4), rt(152, TT, 4), rt(160, TT, 8), rt(176, TT, 8)
        R_s1, R_s2, R_big = rt(192, TT, 8), rt(208, TT, 8), rt(224, TT, 4, 8)
        R_dif, R_dif4, R_dif2 = RT[:, 288:298], rt(288, TT, 4), rt(296, TT)
        R_exp, R_exp4, R_exp2 = RT[:, 300:310], rt(300, TT, 4), rt(308, TT)
        R_gate, R_rank, R_over = rt(320, TT, 34), rt(400, TT, 34), rt(480, TT, 32)
        M_rows, M_xt = R1[:, 0:1024], kt(R1[:, 1024:2048], KD)
        M_o, M_hid, M_th = R2[:, 0:1024], R2[:, 1024:1536], R2[:, 1536:2048]
        M_hidt, M_place = kt(R3[:, 0:512], 4), R3[:, 512:768]
        M_pick, M_gpick = (R3[:, 768 + i * 256:1024 + i * 256].rearrange("p (t n) -> p t n", t=TT) for i in range(2))
        m_slot = [kt(slots[i], KD) for i in range(4)]
        m_down = [kt(slots[4 + e], 4) for e in range(2)]
        g_down = m_down[0]
        OUT = v2(R5)

        ACC = [ctx.enter_context(nc.psum_tensor(f"ACC{i}", [P, 1024], F32)) for i in range(2)]
        AUX = [ctx.enter_context(nc.psum_tensor(f"AUX{i}", [P, 512], F32)) for i in range(4)]
        SB0, TB, OB = 0, 2, 3

        slot_landed = [sem(f"slot_landed{i}") for i in range(RING)]
        small_landed = sem("small_landed")
        x_landed = sem("x_landed")
        mem_landed = sem("mem_landed")
        mem2_landed = sem("mem2_landed")
        consts_ready = sem("consts_ready")
        gains_ready = sem("gains_ready")
        acc_full = [sem(f"acc_full{i}") for i in range(2)]
        acc_free = [sem(f"acc_free{i}") for i in range(2)]
        aux_full = [sem(f"aux_full{i}") for i in range(4)]
        aux_free = [sem(f"aux_free{i}") for i in range(4)]
        squares_ready = sem("squares_ready")
        squares_used = sem("squares_used")
        rows_squared = sem("rows_squared")
        rows_normed = sem("rows_normed")
        heads_normed = sem("heads_normed")
        latents_normed = sem("latents_normed")
        trig_arg = sem("trig_arg")
        trig_ready = sem("trig_ready")
        roped = sem("roped")
        kb_joined = sem("kb_joined")
        pads_cleared = sem("pads_cleared")
        relu_used = sem("relu_used")
        masked = sem("masked")
        exped = sem("exped")
        normed = sem("normed")
        tanh_ready = sem("tanh_ready")
        merged_ready = sem("merged_ready")
        lambda_dots = sem("lambda_dots")
        lambda_exp = sem("lambda_exp")
        decay_a = sem("decay_a")
        decay_e = sem("decay_e")
        gla_products = sem("gla_products")
        gla_padded = sem("gla_padded")
        mix_ready = sem("mix_ready")
        route_work = sem("route_work")
        route_exp = sem("route_exp")
        route_ready = sem("route_ready")
        rank_ready = sem("rank_ready")
        flag_ready = sem("flag_ready")
        dve_steps = sem("dve_steps")
        act_steps = sem("act_steps")
        pool_steps = sem("pool_steps")
        moe_landed = [sem(f"moe_landed{i}") for i in range(6)]
        moe_picks = sem("moe_picks")
        moe_gathered = sem("moe_gathered")
        moe_rows = sem("moe_rows")
        moe_rows_turned = sem("moe_rows_turned")
        moe_input = sem("moe_input")
        moe_gate = sem("moe_gate")
        moe_up = sem("moe_up")
        moe_tanh = sem("moe_tanh")
        moe_gated = sem("moe_gated")
        moe_hidden = sem("moe_hidden")
        moe_turned = sem("moe_turned")
        moe_picks_turned = sem("moe_picks_turned")
        moe_hidden_t = sem("moe_hidden_t")
        moe_picks_t = sem("moe_picks_t")
        moe_down = sem("moe_down")
        moe_out = sem("moe_out")
        moe_summed = sem("moe_summed")
        all_landed = [sem(f"all_landed{i}") for i in range(3)]
        all_gate = sem("all_gate")
        all_tanh = sem("all_tanh")
        all_gated = sem("all_gated")
        all_hidden = sem("all_hidden")
        all_turned = sem("all_turned")
        all_hidden_t = sem("all_hidden_t")
        all_added = sem("all_added")
        y_done = sem("y_done")
        out_ready = sem("out_ready")
        out_ready2 = sem("out_ready2")
        router_landed = sem("router_landed")
        moe_weighting = sem("moe_weighting")
        stored = sem("stored")

        rows = lambda ap: ap[0].rearrange("(t p) n -> p t n", p=P)

        def cols(w, a, b, k=KD):
            return w.rearrange("(k p) n -> p k n", p=P)[:, 0:k, a:b]

        W1, W2 = A["w_in"][0], A["w_in_2"][0]
        chunks = [
            ("mk", 512, [(0, cols(A["w_mem_kv"][0], 0, 512))]),
            ("mv", 512, [(0, cols(A["w_mem_kv"][0], 512, 1024))]),
            ("cq", 384, [(0, cols(W1, IN_CQ, IN_CQ + 384))]),
            ("small", 360, [(0, cols(W1, IN_KI, IN_KI + 72)), (72, cols(W1, IN_CKV, IN_CKV + 288))]),
            ("qi", 512, [(0, cols(W1, 1536, 2048))]),
            ("uq", 768, [(0, cols(A["w_uq"][0], 0, 768, 3))]),
            ("ukv", 1024, [(0, cols(A["w_ukv"][0], 0, 1024, 2))]),
            ("qa", 512, [(0, cols(W1, 0, 512))]),
            ("ka", 512, [(0, cols(W1, 512, 1024))]),
            ("va", 512, [(0, cols(W1, 1024, 1536))]),
            ("za", 512, [(0, cols(W1, IN_ZA, IN_ZA + 512))]),
            ("zb", 512, [(0, cols(W1, IN_ZB, IN_ZB + 512))]),
            ("qm", 512, [(0, cols(W1, IN_QM, IN_QM + 512))]),
            ("zm", 512, [(0, cols(W1, IN_ZM, IN_ZM + 512))]),
        ]
        for n in range(3):
            for h in range(2):
                chunks.append((f"gate{n}{h}", 512, [(0, cols(W1, IN_GATES + n * D + h * 512, IN_GATES + n * D + h * 512 + 512))]))
            chunks.append((f"wb{n}", 1024, [(0, cols(A["w_branch"][0, n], 0, 1024, 4))]))
        for h in range(2):
            chunks.append((f"wout{h}", 512, [(0, cols(A["w_out"][0], h * 512, h * 512 + 512))]))
        W2c = {"gr": (3072, 3088), "gqk": (1536, 2048), "dq": (0, 512), "dk": (512, 1024), "gv": (2048, 2560),
               "dv": (1024, 1536), "gg": (2560, 3072)}

        def ckv_chunk(i):
            chunks.append((f"ckv{i}", 512, [(0, cols(A["w_ckv_2"][0], i * 512, i * 512 + 512))]))

        def w2_chunk(*names):
            for name in names:
                a, b = W2c[name]
                chunks.append((name, b - a, [(0, cols(W2, a, b))]))

        ckv_chunk(0)
        w2_chunk("gr", "gqk", "dq", "dk", "gv")
        ckv_chunk(1)
        w2_chunk("dv", "gg")
        ckv_chunk(2)
        for h in range(2):
            chunks.append((f"wo{h}", 512, [(0, cols(A["w_o_2"][0], h * 512, h * 512 + 512))]))
        ckv_chunk(3)
        for h in range(2):
            chunks.append((f"wcq{h}", 512, [(0, cols(A["w_cq_2"][0], h * 512, h * 512 + 512))]))
        for h in range(2):
            chunks.append((f"wco{h}", 512, [(0, cols(A["w_co_2"][0], h * 512, h * 512 + 512))]))
        chunk_at = {name: c for c, (name, _, _) in enumerate(chunks)}
        landed_value, seen = [], [0] * RING
        for c, (_, _, parts) in enumerate(chunks):
            seen[c % RING] += 16 * len(parts)
            landed_value.append(seen[c % RING])

        def slot_of(name):
            c = chunk_at[name]
            width = chunks[c][1]
            k = SLOT // width
            return slots[c % RING][:, 0:k * width].rearrange("p (k n) -> p k n", k=k)

        acc_no, aux_no, aux_uses, last_job = {}, {}, [0] * 4, {}

        def wait_full(eng, key):
            if key in acc_no:
                n = acc_no[key]
                eng.wait_ge(acc_full[n % 2], n // 2 + 1)
                return ACC[n % 2]
            b, n = aux_no[key]
            eng.wait_ge(aux_full[b], n + 1)
            return AUX[b]

        def wait_drained(eng, key):
            if key in acc_no:
                n = acc_no[key]
                eng.wait_ge(acc_free[n % 2], n // 2 + 1)
            else:
                b, n = aux_no[key]
                eng.wait_ge(aux_free[b], n + 1)

        def free_sem(key):
            return acc_free[acc_no[key] % 2] if key in acc_no else aux_free[aux_no[key][0]]

        units = {
            "A": [(t, h) for h in range(4) for t in range(TT)],
            "B": [(t, h) for h in range(4) for t in range(TT)],
            "M": [(None, h) for h in range(4)],
            "DA": [(t, h) for h in range(4) for t in range(TT)],
            "C": [(None, h) for h in range(4)],
        }
        scales = {"A": 64 ** -0.5, "B": 96 ** -0.5, "M": 128 ** -0.5, "DA": 64 ** -0.5, "C": 256 ** -0.5}
        first_unit, n_units = {}, 0
        for name in ("A", "B", "M", "DA", "C"):
            first_unit[name] = n_units
            n_units += len(units[name])

        def keys_of(t):
            return P if t == 0 else S

        def buf(T, u):
            return T[:, (u % 2) * 512:(u % 2) * 512 + 512]

        def blocks(T, u, nk):
            return buf(T, u)[:, 0:2 * nk].rearrange("p (i k) -> p i k", i=2)

        jobs = {}
        for t in range(TT):
            jobs["cq", t] = [PJ3[:, t, PJ_CQ + 128 * j:PJ_CQ + 128 * j + 128] for j in range(3)]
            jobs["ckv", t] = [PJ3[:, t, PJ_CKV + 128 * j:PJ_CKV + 128 * j + 128] for j in range(2)]
            jobs["qi", t] = [PJ3[:, t, PJ_QI + 128 * j:PJ_QI + 128 * j + 128] for j in range(4)]
            jobs["ki", t] = [EX[:, t * P:(t + 1) * P]]
            jobs["qa", t] = [PJ3[:, t, PJ_QA + 128 * j:PJ_QA + 128 * j + 128] for j in range(4)]
            jobs["ka", t] = [PJ3[:, t, PJ_KA + 128 * j:PJ_KA + 128 * j + 128] for j in range(4)]
            for g in range(2):
                jobs["qb", t, g] = [QB[:, t, 96 * h:96 * h + 96] for h in range(4 * g, 4 * g + 4)]
                jobs["kb", t, g] = [KB[:, t, h, :] for h in range(4 * g, 4 * g + 4)]
            jobs["qm", t] = [PJ3[:, t, PJ_QM + 128 * j:PJ_QM + 128 * j + 128] for j in range(4)]
            jobs["km", t] = [R1v[:, t, 128 * j:128 * j + 128] for j in range(4)]
            jobs["dq", t] = [DQ[:, t, 128 * j:128 * j + 128] for j in range(4)]
            jobs["dk", t] = [DK[:, t, 128 * j:128 * j + 128] for j in range(4)]
            for g in range(2):
                for name, view in (("mem", R3v), ("x0", ZTv), ("merged", R1v), ("mem2", R3v), ("x1", ZTv),
                                   ("x2", ZTv), ("x3", ZTv), ("xq", v2(R2)), ("xk", R1v)):
                    jobs[name, t, g] = [view[:, t, 512 * g + 128 * j:512 * g + 128 * j + 128] for j in range(4)]
        MIXA = R4[:, 0:1024].rearrange("p (t n) -> p t n", t=TT)
        MIXG = GG
        for t in range(TT):
            jobs["mix", t, 0] = [MIXA[:, t, 128 * j:128 * j + 128] for j in range(4)]
            jobs["mix", t, 1] = [MIXG[:, t, 128 * j:128 * j + 128] for j in range(4)]

        small = [(GR[r:r + n, :], A[name][0].rearrange("(k p) -> k p", p=P)) for name, r, n in (
            ("g_norm", GC_NORM, 8), ("g_mem", GC_MEM, 8), ("norm_mix_2", GC_MIX, 8), ("norm_cross_2", GC_CROSS, 8),
            ("norm_mem_2", GC_MEM2, 8), ("norm_ffn_2", GC_FFN, 8), ("g_cq", GC_CQ, 3), ("g_ckv", GC_CKV, 2),
            ("gla_gate_b_2", GC_GATEB, 2))]
        small += [(GB[:, c:c + n], A[name][0:1, :].broadcast_to([P, n])) for name, c, n in (
            ("g_qn_a", GB_A, 64), ("g_kn_a", GB_A + 64, 64), ("g_qn_b", GB_B, 96), ("g_kn_b", GB_B + 96, 96),
            ("g_qn_m", GB_M, 128), ("g_kn_m", GB_M + 128, 128), ("da_q_norm_2", GB_DA, 64), ("da_k_norm_2", GB_DA + 64, 64),
            ("da_out_norm_2", GB_DAO, 128), ("gla_out_norm_2", GB_GLAO, 128), ("cross_q_norm_2", GB_X, 256),
            ("cross_k_norm_2", GB_X + 256, 256), ("b_group_2", GB_ROUTE, 4), ("b_expert_2", GB_ROUTE + 4, 32),
            ("lambda_q1_2", GB_LAM, 64), ("lambda_k1_2", GB_LAM + 64, 64), ("lambda_q2_2", GB_LAM + 128, 64),
            ("lambda_k2_2", GB_LAM + 192, 64))]
        small += [(pos_i[:, :], A["positions"][0].rearrange("(t p) -> p t", p=P)), (GW[:, :], A["gla_gate_w_2"][0])]
        small_total = 16 * len(small)
        WG, WU, WD = (A[n][0] for n in ("w_e_gate_2", "w_e_up_2", "w_e_down_2"))

        block = ctx.enter_context(nc.Block())

        @block.tensor
        def _(pe):
            def acc(key):
                n = len(acc_no)
                acc_no[key] = n
                if n >= 2:
                    pe.wait_ge(acc_free[n % 2], n // 2)
                return ACC[n % 2], acc_full[n % 2]

            def aux(b, key):
                n = aux_uses[b]
                aux_uses[b] += 1
                aux_no[key] = (b, n)
                if n:
                    pe.wait_ge(aux_free[b], n)
                return AUX[b], aux_full[b]

            def wait_chunk(name):
                c = chunk_at[name]
                pe.wait_ge(slot_landed[c % RING], landed_value[c])

            def project(name, lhs, k=KD, a=0, width=512, key=None):
                wait_chunk(name)
                bank, full = acc(key or name)
                w = slot_of(name)
                for t in range(TT):
                    for i in range(k):
                        mm = nc.tensor.matmul(bank[:, t * 512:t * 512 + width], lhs[:, i, t * P:(t + 1) * P],
                                              w[:, i, a:a + width], start=(i == 0), stop=(i == k - 1))
                mm.then_inc(full, 1)
                last_job[name] = key or name

            def project_t(name, rhs, tiles=4, m=P):
                wait_chunk(name)
                bank, full = acc(name)
                w = slot_of(name)
                for j in range(tiles):
                    for i in range(KD):
                        mm = nc.tensor.matmul(bank[0:m, j * S:(j + 1) * S], w[:, i, j * P:j * P + m],
                                              rhs[:, i, :], start=(i == 0), stop=(i == KD - 1))
                mm.then_inc(full, 1)
                last_job[name] = name

            def turn(b, key):
                bank, full = aux(b, key)
                for j, src in enumerate(jobs[key]):
                    mm = nc.tensor.transpose(bank[0:src.shape[1], j * P:(j + 1) * P], src, ident[:, :])
                mm.then_inc(full, 1)

            def turn_rows(name, n):
                for t in range(TT):
                    pe.wait_ge(rows_normed, 2 * n + t + 1)
                    for g in range(2):
                        turn(2 * t + g, (name, t, g))

            def wait_turned(name):
                for t in range(TT):
                    for g in range(2):
                        wait_drained(pe, (name, t, g))

            def attend(name, score, value, dims):
                U = len(units[name])
                for s in range(U + 2):
                    if s < U:
                        u = first_unit[name] + s
                        t, h = units[name][s]
                        nk = keys_of(t)
                        bank, full = aux(SB0 + u % 2, ("S", u))
                        for i in range(2):
                            mm = score(bank[:, i * nk:(i + 1) * nk], t, h, i, nk)
                        mm.then_inc(full, 1)
                    if 1 <= s <= U:
                        u = first_unit[name] + s - 1
                        t, h = units[name][s - 1]
                        nk = keys_of(t)
                        pe.wait_ge(normed, u + 1)
                        bank, full = aux(TB, ("T", u))
                        e = blocks(EX, u, nk)
                        heads = 1 if name == "DA" else 2
                        for j in range(nk // P):
                            for i in range(heads):
                                mm = nc.tensor.transpose(bank[:, (j * heads + i) * P:(j * heads + i + 1) * P],
                                                         e[:, i, j * P:(j + 1) * P], ident[:, :])
                        mm.then_inc(full, 1)
                    if s >= 2:
                        u = first_unit[name] + s - 2
                        t, h = units[name][s - 2]
                        nk = keys_of(t)
                        wait_drained(pe, ("T", u))
                        bank, full = aux(OB, ("O", u))
                        p = buf(PT, u)
                        for d in range(dims):
                            for j in range(nk // P):
                                first, last = j == 0, j == nk // P - 1
                                if name == "DA":
                                    mm = nc.tensor.matmul(bank[:, 0:P], p[:, j * P:(j + 1) * P], value(j, h, d),
                                                          start=first, stop=last)
                                else:
                                    mm = nc.tensor.matmul(bank[:, d * 256:(d + 1) * 256], value(j, h, d),
                                                          p[:, j * 256:(j + 1) * 256], start=first, stop=last)
                        mm.then_inc(full, 1)

            pe.wait_ge(consts_ready, 1)
            pe.wait_ge(small_landed, small_total)
            bank, full = aux(3, "gains")
            nc.tensor.transpose(bank[:, 0:GC_N], GR[:, :], ident[0:GC_N, 0:GC_N]).then_inc(full, 1)
            turn_rows("mem", 0)
            turn_rows("x0", 1)
            wait_turned("mem")
            project("mk", R2T)
            project("mv", R2T)
            wait_turned("x0")
            project("cq", XT3, width=384)
            project("small", XT3, width=360)
            project("qi", XT3)
            for t in range(TT):
                pe.wait_ge(latents_normed, 1)
                turn(t, ("cq", t))
                turn(2 + t, ("ckv", t))
            for t in range(TT):
                wait_drained(pe, ("cq", t))
                wait_drained(pe, ("ckv", t))
            project("uq", CQT, k=3, a=0, width=512, key="uq0")
            project("uq", CQT, k=3, a=512, width=256, key="uq1")
            project("ukv", CKVT, k=2, a=0, width=512, key="ukv0")
            project("ukv", CKVT, k=2, a=512, width=512, key="ukv1")
            pe.wait_ge(roped, 1)
            for t in range(TT):
                turn(t, ("qi", t))
                turn(2 + t, ("ki", t))
            project("qa", XT3)
            for t in range(TT):
                wait_drained(pe, ("qi", t))
                wait_drained(pe, ("ki", t))
            for n in range(8):
                t, h = n // 4, n % 4
                nk = keys_of(t)
                bank, full = aux(n % 4, ("dots", n))
                for i in range(2):
                    mm = nc.tensor.matmul(bank[:, i * nk:(i + 1) * nk], QPAD[:, 2 * h + i, t * P:(t + 1) * P],
                                          KIT[:, 0:nk], start=True, stop=True)
                mm.then_inc(full, 1)
            project("ka", XT3)
            project("va", XT3)
            project_t("za", XT3)
            pe.wait_ge(roped, 3)
            for t in range(TT):
                turn(t, ("qa", t))
                turn(2 + t, ("ka", t))
            project_t("zb", XT3)
            for t in range(TT):
                wait_drained(pe, ("qa", t))
                wait_drained(pe, ("ka", t))
            wait_drained(pe, "va")
            attend("A", lambda o, t, h, i, nk: nc.tensor.matmul(
                o, QPAD[:, 2 * h + i, t * P:(t + 1) * P], KT4[:, h, 0:nk], start=True, stop=True),
                lambda j, h, d: PJ3[:, j, PJ_VA + P * h:PJ_VA + P * h + P], 1)
            project("qm", XT3)
            pe.wait_ge(roped, 2)
            for t in range(TT):
                for g in range(2):
                    turn(g, ("qb", t, g))
                    turn(2 + g, ("kb", t, g))
            project_t("zm", XT3)
            for t in range(TT):
                for g in range(2):
                    wait_drained(pe, ("qb", t, g))
                    wait_drained(pe, ("kb", t, g))
            attend("B", lambda o, t, h, i, nk: nc.tensor.matmul(
                o, QBT[0:96, 2 * h + i, t * P:(t + 1) * P], KBT[0:96, 2 * h + i, 0:nk], start=True, stop=True),
                lambda j, h, d: R3[:, 1024 + 512 * j + P * h:1024 + 512 * j + P * h + P], 1)
            pe.wait_ge(heads_normed, 5)
            for t in range(TT):
                turn(t, ("qm", t))
                turn(2 + t, ("km", t))
            project("gate00", XT3)
            for t in range(TT):
                wait_drained(pe, ("qm", t))
                wait_drained(pe, ("km", t))
            wait_drained(pe, "mv")
            attend("M", lambda o, t, h, i, nk: nc.tensor.matmul(
                o, QMT[:, h, i * P:(i + 1) * P], KMT[:, h, :], start=True, stop=True),
                lambda j, h, d: VM[:, j, P * h:P * h + P], 1)
            for n in range(3):
                if n:
                    project(f"gate{n}0", XT3)
                project(f"gate{n}1", XT3)
                last_unit = first_unit["ABM"[n]] + len(units["ABM"[n]]) - 1
                wait_drained(pe, ("O", last_unit))
                for h in range(2):
                    project(f"wb{n}", YT[:, 4 * n:4 * n + 4, :], k=4, a=512 * h, key=f"wb{n}{h}")
            for t in range(TT):
                for g in range(2):
                    pe.wait_ge(merged_ready, g + 1)
                    turn(2 * t + g, ("merged", t, g))
            wait_turned("merged")
            for h in range(2):
                project(f"wout{h}", XT3)
            turn_rows("mem2", 2)
            wait_turned("mem2")
            project("ckv0", R2T)
            turn_rows("x1", 3)
            wait_turned("x1")
            project_t("gr", XT3, tiles=1, m=16)
            project_t("gqk", XT3)
            wait_drained(pe, "gr")
            bank, full = acc("gate_z")
            for h in range(2):
                mm = nc.tensor.matmul(bank[:, h * S:(h + 1) * S], GW[:, h * P:(h + 1) * P], GRT[:, :],
                                      start=True, stop=True)
            mm.then_inc(full, 1)
            project("dq", XT3)
            project("dk", XT3)
            project("gv", XT3)
            project("ckv1", R2T)
            pe.wait_ge(heads_normed, 6)
            for t in range(TT):
                turn(t, ("dq", t))
                turn(2 + t, ("dk", t))
            project("dv", XT3)
            pe.wait_ge(gla_products, 1)
            pe.wait_ge(gla_padded, 1)
            for t in range(TT):
                bank, full = acc(("intra", t))
                for h in range(4):
                    nc.tensor.matmul(bank[:, h * P:(h + 1) * P], KNZ[:, h, t * P:(t + 1) * P],
                                     QP[:, h // 2, t * P:(t + 1) * P], start=True, stop=True)
                for h in range(4):
                    mm = nc.tensor.matmul(bank[:, 512 + h * P:512 + (h + 1) * P], KPZ[:, h, t * P:(t + 1) * P],
                                          QN[:, h // 2, t * P:(t + 1) * P], start=True, stop=True)
                mm.then_inc(full, 1)
            bank, full = aux(3, "kend")
            for t in range(TT):
                for h in range(2):
                    mm = nc.tensor.transpose(bank[:, (2 * t + h) * P:(2 * t + h + 1) * P], KE[:, h, t * P:(t + 1) * P],
                                             ident[:, :])
            mm.then_inc(full, 1)
            project("gg", XT3)
            wait_drained(pe, "kend")
            wait_drained(pe, "gv")
            for c in range(3):
                bank, full = aux(c, ("state", c))
                for h in range(2):
                    mm = nc.tensor.matmul(bank[:, h * 256:(h + 1) * 256], KEN[:, c % 2, 2 * (c // 2) + h, :],
                                          GV[:, c // 2, h * 256:(h + 1) * 256], start=True, stop=True)
                mm.then_inc(full, 1)
            project("ckv2", R2T)
            wait_drained(pe, ("intra", 1))
            wait_drained(pe, ("state", 2))
            for t in range(TT):
                bank, full = aux(3, ("gla", t))
                for h in range(4):
                    o = bank[:, h * P:(h + 1) * P]
                    nc.tensor.matmul(o, ATT[:, t, h, :], GV[:, t, h * P:(h + 1) * P], start=True, stop=False,
                                     skip_group_check=True)
                    for c in range(2):
                        if 2 * t + c:
                            mm = nc.tensor.matmul(bank[64 * c:64 * c + 64, h * P:(h + 1) * P],
                                                  QLZ[:, h, t * P + 64 * c:t * P + 64 * c + 64],
                                                  ST[:, 2 * t + c - 1, h // 2, :], start=False, stop=(c == 1),
                                                  skip_group_check=True)
                mm.then_inc(full, 1)
            for t in range(TT):
                wait_drained(pe, ("dq", t))
                wait_drained(pe, ("dk", t))
            wait_drained(pe, "dv")
            attend("DA", lambda o, t, h, i, nk: nc.tensor.matmul(
                o, QPAD[:, 2 * h + i, t * P:(t + 1) * P], KT4[:, h, 0:nk], start=True, stop=True),
                lambda j, h, d: DV[:, j, P * h:P * h + P], 1)
            project("ckv3", R2T)
            pe.wait_ge(mix_ready, 1)
            pe.wait_ge(heads_normed, 8)
            for t in range(TT):
                for g in range(2):
                    turn(2 * t + g, ("mix", t, g))
            wait_turned("mix")
            for h in range(2):
                project(f"wo{h}", XT3)
            pe.wait_ge(heads_normed, 9)
            for t in range(TT):
                for g in range(2):
                    turn(2 * t + g, ("xk", t, g))
            turn_rows("x2", 4)
            wait_turned("x2")
            for h in range(2):
                project(f"wcq{h}", XT3)
            pe.wait_ge(heads_normed, 10)
            for t in range(TT):
                for g in range(2):
                    turn(2 * t + g, ("xq", t, g))
            wait_turned("xq")
            wait_turned("xk")

            def cross_score(o, t, h, i, nk):
                nc.tensor.matmul(o, CQ8[:, 2 * h, i * P:(i + 1) * P], CK8[:, 2 * h, :], start=True, stop=False)
                return nc.tensor.matmul(o, CQ8[:, 2 * h + 1, i * P:(i + 1) * P], CK8[:, 2 * h + 1, :],
                                        start=False, stop=True)

            attend("C", cross_score, lambda j, h, d: R3v[:, j, 256 * h + P * d:256 * h + P * d + P], 2)
            wait_drained(pe, ("O", first_unit["C"] + 3))
            for h in range(2):
                project(f"wco{h}", XT3)
            turn_rows("x3", 5)
            wait_turned("x3")
            pe.wait_ge(router_landed, 32)
            bank, full = aux(0, "router")
            WR3 = WR[:, :].rearrange("p (k n) -> p k n", k=KD)
            for t in range(TT):
                for i in range(KD):
                    mm = nc.tensor.matmul(bank[:, 36 * t:36 * t + 36], XT3[:, i, t * P:(t + 1) * P], WR3[:, i, :],
                                          start=(i == 0), stop=(i == KD - 1))
            mm.then_inc(full, 1)
            pe.wait_ge(route_ready, 1)
            bank, full = aux(1, "ranks")
            nc.tensor.matmul(bank[:, 0:32], before[:, :], R_sel[:, 0, :], start=True, stop=True)
            nc.tensor.matmul(bank[:, 32:64], before[:, :], R_sel[:, 1, :], start=True, stop=False)
            nc.tensor.matmul(bank[:, 32:64], ones[:, :], R_sel[:, 0, :], start=False, stop=True)
            nc.tensor.matmul(bank[:, 64:96], ones[:, :], R_sel[:, 0, :], start=True, stop=False)
            nc.tensor.matmul(bank[:, 64:96], ones[:, :], R_sel[:, 1, :], start=False, stop=True).then_inc(full, 1)

            wait_drained(pe, "wco0")
            wait_drained(pe, "wco1")
            for t in range(TT):
                for h in range(2):
                    mm = nc.tensor.matmul(ACC[t][:, h * 512:(h + 1) * 512], ident[:, :], X3[:, t, h * 512:(h + 1) * 512],
                                          start=True, stop=False, skip_group_check=True)
            mm.then_inc(moe_picks_turned, 1)

            def gather():
                for h in range(2):
                    for t in range(TT):
                        mm = nc.tensor.matmul(AUX[h][:, :], M_pick[:, t, :], ZTv[:, t, h * 512:(h + 1) * 512],
                                              start=(t == 0), stop=(t == TT - 1))
                mm.then_inc(moe_gathered, 1)

            def turn_input():
                for j in range(KD):
                    mm = nc.tensor.transpose(AUX[j // 4][:, (j % 4) * P:(j % 4 + 1) * P], M_rows[:, j * P:(j + 1) * P],
                                             ident[:, :])
                mm.then_inc(moe_rows_turned, 1)

            pe.wait_ge(moe_picks, 1)
            wait_drained(pe, "router")
            wait_drained(pe, "ranks")
            gather()
            pe.wait_ge(moe_rows, 1)
            turn_input()
            with pe.Fori(0, PAIRS) as i:
                pe.wait_ge(moe_input, i + 1)
                for e in range(2):
                    pe.wait_ge(moe_landed[e], i * 16 + 16)
                for k in range(KD):
                    for e in range(2):
                        mm = nc.tensor.matmul(AUX[2][64 * e:64 * e + 64, :], M_xt[:, k, 64 * e:64 * e + 64],
                                              m_slot[e][:, k, :], start=(k == 0), stop=(k == KD - 1))
                mm.then_inc(moe_gate, 1)
                for e in range(2):
                    pe.wait_ge(moe_landed[2 + e], i * 16 + 16)
                for k in range(KD):
                    for e in range(2):
                        mm = nc.tensor.matmul(AUX[3][64 * e:64 * e + 64, :], M_xt[:, k, 64 * e:64 * e + 64],
                                              m_slot[2 + e][:, k, :], start=(k == 0), stop=(k == KD - 1))
                mm.then_inc(moe_up, 1)
                pe.wait_ge(moe_picks, i + 2)
                gather()
                pe.wait_ge(moe_hidden, i + 1)
                for j in range(4):
                    mm = nc.tensor.transpose(AUX[2][:, j * P:(j + 1) * P], M_hid[:, j * P:(j + 1) * P], ident[:, :])
                mm.then_inc(moe_turned, 1)
                for t in range(TT):
                    mm = nc.tensor.transpose(AUX[3][:, t * P:(t + 1) * P], M_gpick[:, t, :], ident[:, :])
                mm.then_inc(moe_picks_turned, 1)
                pe.wait_ge(moe_hidden_t, i + 1)
                pe.wait_ge(moe_picks_t, i + 1)
                for e in range(2):
                    pe.wait_ge(moe_landed[4 + e], i * 16 + 16)
                for k in range(4):
                    for h in range(2):
                        for e in range(2):
                            mm = nc.tensor.matmul(AUX[2 + h][64 * e:64 * e + 64, :], M_hidt[:, k, 64 * e:64 * e + 64],
                                                  m_down[e][:, k, h * 512:(h + 1) * 512], start=(k == 0), stop=(k == 3))
                mm.then_inc(moe_down, 1)
                pe.wait_ge(moe_rows, i + 2)
                turn_input()
                pe.wait_ge(moe_out, i + 1)
                for t in range(TT):
                    for h in range(2):
                        mm = nc.tensor.matmul(ACC[t][:, h * 512:(h + 1) * 512], M_place[:, t * P:(t + 1) * P],
                                              M_o[:, h * 512:(h + 1) * 512], start=False, stop=False,
                                              skip_group_check=True)
                mm.then_inc(moe_summed, 1)
            pe.wait_ge(flag_ready, 1)
            fullest = pe.value_load(FLAG[0:1, 0:1])
            with pe.If(fullest > CAP):
                pe.wait_ge(moe_input, PAIRS + 1)
                with pe.Fori(0, N_EXPERTS) as e:
                    for s in range(3):
                        pe.wait_ge(all_landed[s], e * 16 + 16)
                    for t in range(TT):
                        for k in range(KD):
                            nc.tensor.matmul(AUX[0][:, :], XT3[:, k, t * P:(t + 1) * P], m_slot[0][:, k, :],
                                             start=(k == 0), stop=(k == KD - 1))
                        for k in range(KD):
                            mm = nc.tensor.matmul(AUX[1][:, :], XT3[:, k, t * P:(t + 1) * P], m_slot[1][:, k, :],
                                                  start=(k == 0), stop=(k == KD - 1))
                        mm.then_inc(all_gate, 1)
                        pe.wait_ge(all_hidden, e * 2 + t + 1)
                        for j in range(4):
                            mm = nc.tensor.transpose(AUX[2][:, j * P:(j + 1) * P], M_hid[:, j * P:(j + 1) * P], ident[:, :])
                        mm.then_inc(all_turned, 1)
                        pe.wait_ge(all_hidden_t, e * 2 + t + 1)
                        for k in range(4):
                            for h in range(2):
                                mm = nc.tensor.matmul(ACC[t][:, h * 512:(h + 1) * 512], M_hidt[:, k, :],
                                                      g_down[:, k, h * 512:(h + 1) * 512], start=False, stop=False,
                                                      skip_group_check=True)
                        mm.then_inc(all_added, 1)
            for t in range(TT):
                for h in range(2):
                    mm = nc.tensor.matmul(ACC[t][:, h * 512:(h + 1) * 512], zeros[:, :], X3[:, t, h * 512:(h + 1) * 512],
                                          start=False, stop=True, skip_group_check=True)
            mm.then_inc(y_done, 1)

        @block.sync
        def _(sp):
            sp.dma_start(R1v, rows(A["mem"])).then_inc(mem_landed, 16)
            sp.dma_start(X3, rows(A["x"])).then_inc(x_landed, 16)
            for c, (name, width, parts) in enumerate(chunks):
                if c >= RING:
                    wait_full(sp, last_job[chunks[c - RING][0]])
                for first, src in parts:
                    k, n = src.shape[1], src.shape[2]
                    dst = slot_of(name)[:, 0:k, first:first + n]
                    sp.dma_start(dst, src).then_inc(slot_landed[c % RING], 16)
                if name == "wout0":
                    wait_full(sp, ("merged", 1, 1))
                    wait_full(sp, ("merged", 1, 0))
                    sp.dma_start(R1v, rows(A["mem_2"])).then_inc(mem2_landed, 16)

            def expert_parts(s, e):
                w = (WG, WG, WU, WU, WD, WD)[s]
                return w[bass.ds(e, 1), :, :].rearrange("e (k p) n -> p (e k) n", p=P)

            dsts = [m_slot[0], m_slot[1], m_slot[2], m_slot[3], m_down[0], m_down[1]]
            order = sorted(range(4), key=lambda s: max(c for c in range(len(chunks)) if c % RING == s))
            wait_full(sp, ("mix", 1, 1))
            wait_full(sp, ("mix", 1, 0))
            for name, a, b in (("w_group_2", 0, 4), ("w_expert_2", 4, 36)):
                sp.dma_start(kt(WR, KD)[:, :, a:b], A[name][0].rearrange("(k p) n -> p k n", p=P)).then_inc(router_landed, 16)
            for s in (4, 5):
                sp.dma_start(dsts[s], WD[s - 4].rearrange("(k p) n -> p k n", p=P)).then_inc(moe_landed[s], 16)
            for s in order:
                c = max(c for c in range(len(chunks)) if c % RING == s)
                wait_full(sp, last_job[chunks[c][0]])
                w = (WG, WG, WU, WU)[s]
                sp.dma_start(dsts[s], w[s % 2].rearrange("(k p) n -> p k n", p=P)).then_inc(moe_landed[s], 16)
            with sp.Fori(0, PAIRS - 1) as i:
                for group, used in enumerate((moe_gate, moe_up, moe_down)):
                    src = [expert_parts(2 * group + j, i * 2 + (2 + j)) for j in range(2)]
                    sp.wait_ge(used, i + 1)
                    for j in range(2):
                        sp.dma_start(dsts[2 * group + j], src[j]).then_inc(moe_landed[2 * group + j], 16)
            sp.wait_ge(flag_ready, 1)
            fullest = sp.value_load(FLAG[0:1, 0:1])
            with sp.If(fullest > CAP):
                sp.wait_ge(moe_down, PAIRS)
                for w, dst, landed in ((WG, m_slot[0], 0), (WU, m_slot[1], 1), (WD, g_down, 2)):
                    sp.dma_start(dst, w[0].rearrange("(k p) n -> p k n", p=P)).then_inc(all_landed[landed], 16)
                with sp.Fori(1, N_EXPERTS) as e:
                    srcs = [w[bass.ds(e, 1), :, :].rearrange("e (k p) n -> p (e k) n", p=P) for w in (WG, WU, WD)]
                    sp.wait_ge(all_gate, e * 2)
                    sp.dma_start(m_slot[0], srcs[0]).then_inc(all_landed[0], 16)
                    sp.dma_start(m_slot[1], srcs[1]).then_inc(all_landed[1], 16)
                    sp.wait_ge(all_added, e * 2)
                    sp.dma_start(g_down, srcs[2]).then_inc(all_landed[2], 16)
            for t in range(TT):
                sp.wait_ge((out_ready, out_ready2)[t], 1)
                sp.dma_start(out[0, t * P:(t + 1) * P, :], OUT[:, t, :]).then_inc(stored, 16)
            sp.wait_ge(stored, 16 * TT)

        @block.gpsimd
        def _(pool):
            steps = [0]

            def link(ins):
                steps[0] += 1
                ins.then_inc(pool_steps, 1)
                pool.wait_ge(pool_steps, steps[0])

            g = nc.gpsimd
            g.memset(ident[:, :], 0.0)
            g.memset(causal[:, :], 0.0)
            g.memset(past[:, :], 1.0)
            g.memset(future[:, :], 1.0)
            g.memset(before[:, :], 1.0)
            g.memset(ones[:, :], 1.0)
            g.memset(zeros[:, :], 0.0)
            for j in range(16):
                g.memset(freq[:, j:j + 1], float(np.float32(THETA) ** np.float32(-j / 16)))
            link(g.iota(iota_i[:, :], pattern=[[1, CAP]], base=0, channel_multiplier=0))
            g.tensor_copy(iota[:, :], iota_i[:, :])
            g.affine_select(out=ident[:, :], in_=ident[:, :], compare_op=ALU.not_equal, fill=1.0, base=0,
                            pattern=[[-1, P]], channel_multiplier=1)
            g.affine_select(out=causal[:, 128:256], in_=causal[:, 128:256], compare_op=ALU.is_ge, fill=NEG, base=0,
                            pattern=[[-1, P]], channel_multiplier=1)
            g.affine_select(out=past[:, :], in_=past[:, :], compare_op=ALU.is_ge, fill=0.0, base=0,
                            pattern=[[1, P]], channel_multiplier=-1)
            g.affine_select(out=future[:, :], in_=future[:, :], compare_op=ALU.is_gt, fill=0.0, base=0,
                            pattern=[[-1, P]], channel_multiplier=1)
            link(g.affine_select(out=before[:, :], in_=before[:, :], compare_op=ALU.is_gt, fill=0.0, base=0,
                                 pattern=[[1, P]], channel_multiplier=-1))
            link(g.memset(past[0:64, 64:128], 0.0))
            link(g.memset(future[64:128, 0:64], 0.0))
            g.tensor_scalar(pref[:, 0:8], iota[:, 0:8], -1.0, 8.0, ALU.mult, ALU.add)
            g.tensor_scalar(pref[:, 8:12], iota[:, 0:4], -1.0, 4.0, ALU.mult, ALU.add).then_inc(consts_ready, 1)
            g.memset(QPAD, 0.0).then_inc(pads_cleared, 1)

            def rope(view, t, off, half, step, groups):
                x = view[:, :, off:off + 2 * half].rearrange("p g (a d) -> p g a d", a=2)
                tab = [trig[:, c + 16 * t:c + 16 * t + 16].rearrange("p (d s) -> p d s", s=step)[:, :, 0]
                       .unsqueeze(1).unsqueeze(1).broadcast_to([P, groups, 2, half]) for c in (160, 128)]
                n = groups * 2 * half
                xc, xs = (ROT[:, i * 256:i * 256 + n].rearrange("p (g a d) -> p g a d", g=groups, a=2) for i in range(2))
                g.tensor_tensor(xc, x, tab[0], ALU.mult)
                link(g.tensor_tensor(xs, x, tab[1], ALU.mult))
                g.tensor_tensor(x[:, :, 0, :], xc[:, :, 0, :], xs[:, :, 1, :], ALU.subtract)
                link(g.tensor_tensor(x[:, :, 1, :], xc[:, :, 1, :], xs[:, :, 0, :], ALU.add))

            def heads(T3, t, a, n, w):
                return T3[:, t, a:a + n * w].rearrange("p (h d) -> p h d", h=n)

            pool.wait_ge(trig_ready, 1)
            wait_drained(pool, "small")
            wait_drained(pool, "qi")
            for t in range(TT):
                rope(heads(PJ3, t, PJ_QI, 9, 64), t, 0, 8, 2, 9)
            for t in range(TT):
                for i in range(2):
                    last = g.tensor_copy(EX[:, t * P + 64 * i:t * P + 64 * i + 64], PJ3[:, t, PJ_KI:PJ_KI + 64])
            last.then_inc(roped, 1)
            wait_drained(pool, "ukv0")
            wait_drained(pool, "ukv1")
            for t in range(TT):
                g.tensor_copy(KB[:, t, :, 0:64], KNB[:, t, :, :])
                last = g.tensor_copy(KB[:, t, :, 64:96],
                                     PJ3[:, t, PJ_KR:PJ_KR + 32].unsqueeze(1).broadcast_to([P, 8, 32]))
            last.then_inc(kb_joined, 1)
            pool.wait_ge(heads_normed, 3)
            for t in range(TT):
                rope(heads(QB, t, 0, 8, 96), t, 64, 16, 1, 8)
                rope(KB[:, t, :, :], t, 64, 16, 1, 8)
            g.memset(SMALL[:, 24:25], 0.0).then_inc(roped, 1)
            pool.wait_ge(heads_normed, 4)
            for t in range(TT):
                rope(heads(PJ3, t, PJ_QA, 16, 64), t, 0, 8, 2, 16)
            g.memset(SMALL[:, 25:26], 0.0).then_inc(roped, 1)
            for k in range(2):
                wait_full(pool, ("O", first_unit["M"] + 2 + k))
            g.memset(QPAD, 0.0).then_inc(pads_cleared, 1)
            g.memset(ATT, 0.0)
            link(g.memset(causal[:, 128:256], 0.0))
            g.memset(causal[0:64, 192:256], NEG).then_inc(pads_cleared, 1)
            wait_full(pool, ("x1", 1, 1))
            wait_full(pool, ("x1", 1, 0))
            g.memset(ZT[:, :], 0.0).then_inc(pads_cleared, 1)
            g.memset(KEN, 0.0).then_inc(pads_cleared, 1)
            pool.wait_ge(decay_e, 1)
            g.tensor_tensor(QP, kt(GQ, 2), kt(EP, 2), ALU.mult)
            g.tensor_tensor(QN, kt(GQ, 2), kt(EN, 2), ALU.mult)
            g.tensor_tensor(KE, kt(GK, 2), kt(EE, 2), ALU.mult).then_inc(gla_products, 1)

        @block.scalar
        def _(act):
            a_ = nc.scalar
            for dst, src in small:
                act.dma_start(dst, src, allow_slow_non_contiguous=dst.dtype == I32).then_inc(small_landed, 16)
            steps = [0]

            def link(ins):
                steps[0] += 1
                ins.then_inc(act_steps, 1)
                act.wait_ge(act_steps, steps[0])

            def square_rows(n, src, junk, ready):
                for r in ready:
                    wait_drained(act, r) if isinstance(r, str) else act.wait_ge(*r)
                for t in range(TT):
                    last = a_.activation(junk[:, t, :], src[:, t, :], ACT.Square, scale=D ** -0.5,
                                         accum_out=SMALL[:, 16 + t:17 + t])
                last.then_inc(rows_squared, 1)

            sq_calls = [0]

            def square_heads(src, dst, w):
                if sq_calls[0]:
                    act.wait_ge(squares_used, sq_calls[0])
                sq_calls[0] += 1
                a_.activation(dst, src, ACT.Square, scale=w ** -0.5).then_inc(squares_ready, 1)

            def drain(key, pairs):
                bank = wait_full(act, key)
                for dst, src in pairs:
                    last = a_.activation(dst, src(bank), ACT.Copy)
                last.then_inc(free_sem(key), 1)

            def by_token(T3, c, width=512):
                return [(T3[:, t, c:c + width], lambda b, t=t: b[:, t * 512:t * 512 + width]) for t in range(TT)]

            def drain_turned(key, dst, n, rows_=P):
                t = key[1]
                drain(key, [(dst[0:rows_, :, t * P:(t + 1) * P],
                             lambda b: b[0:rows_, 0:n * P].rearrange("p (k q) -> p k q", k=n))])

            def drain_padded(key, dst):
                t = key[1]
                view = dst.rearrange("p (h i) q -> p h i q", i=2)
                drain(key, [(view[64 * i:64 * i + 64, :, i, t * P:(t + 1) * P],
                             lambda b, i=i: b[64 * i:64 * i + 64, :].rearrange("p (k q) -> p k q", k=4)) for i in range(2)])

            def soften(name):
                U = len(units[name])
                for s in range(U + 1):
                    if s < U:
                        u = first_unit[name] + s
                        nk = keys_of(units[name][s][0])
                        act.wait_ge(masked, u + 1)
                        m, e = blocks(SM, u, nk), blocks(EX, u, nk)
                        if u >= 2:
                            wait_full(act, ("T", u - 2))
                        for i in range(2):
                            last = a_.activation(e[:, i, :], m[:, i, :], ACT.Exp, bias=stat(u, 0)[:, i:i + 1],
                                                 accum_out=stat(u, 1)[:, i:i + 1])
                        last.then_inc(exped, 1)
                    if s >= 1:
                        u = first_unit[name] + s - 1
                        nk = keys_of(units[name][s - 1][0])
                        n = nk if name == "DA" else 2 * nk
                        bank = wait_full(act, ("T", u))
                        if u >= 2:
                            wait_full(act, ("O", u - 2))
                        a_.activation(buf(PT, u)[:, 0:n], bank[:, 0:n], ACT.Copy).then_inc(free_sem(("T", u)), 1)

            act.wait_ge(consts_ready, 1)
            square_rows(0, R1v, R3v, [(mem_landed, 16)])
            act.wait_ge(rows_normed, 1)
            square_rows(1, X3, ZTv, [(x_landed, 16)])
            act.wait_ge(trig_arg, 2)
            a_.activation(trig[:, 128:192], trig[:, 64:128], ACT.Sin).then_inc(trig_ready, 1)
            drain("mk", by_token(R1v, 0))
            wait_drained(act, "mk")
            square_heads(R1v[:, :, 0:512], SQ[:, 0:1024].rearrange("p (t n) -> p t n", t=TT), 128)
            drain("mv", by_token(R1v, 512))
            drain("cq", by_token(PJ3, PJ_CQ, 384))
            drain("small", by_token(PJ3, PJ_KI, 360))
            wait_drained(act, "cq")
            wait_drained(act, "small")
            act.wait_ge(rows_normed, 4)
            for t in range(TT):
                for j, (c, w) in enumerate(((PJ_CQ, 384), (PJ_CKV, 256))):
                    junk = ((SM[:, 0:384], SM[:, 384:640]), (SM[:, 640:1024], EX[:, 768:1024]))[t][j]
                    last = a_.activation(junk, PJ3[:, t, c:c + w], ACT.Square, scale=w ** -0.5,
                                         accum_out=SMALL[:, 20 + 2 * t + j:21 + 2 * t + j])
            last.then_inc(rows_squared, 1)
            drain("qi", by_token(PJ3, PJ_QI))
            drain("uq0", by_token(QB, 0))
            drain("uq1", by_token(QB, 512, 256))
            wait_drained(act, "uq1")
            square_heads(QB, SQ[:, 0:1536].rearrange("p (t n) -> p t n", t=TT), 96)
            for g in range(2):
                drain(f"ukv{g}", [(T[:, t, 4 * g:4 * g + 4, :],
                                   lambda b, t=t, a=a: b[:, t * 512:(t + 1) * 512].rearrange("p (h a d) -> p h a d", h=4, a=2)[:, :, a, :])
                                  for t in range(TT) for a, T in enumerate((KNB, VB))])
            act.wait_ge(pads_cleared, 1)
            for t in range(TT):
                drain_padded(("qi", t), QPAD)
                drain(("ki", t), [(KIT[:, t * P:(t + 1) * P], lambda b: b[:, 0:P])])
            act.wait_ge(kb_joined, 1)
            square_heads(R2[:, 0:1536], SQ[:, 0:1536], 96)
            drain("qa", by_token(PJ3, PJ_QA))
            for n in range(8):
                nk = keys_of(n // 4)
                bank = wait_full(act, ("dots", n))
                if n >= 2:
                    act.wait_ge(relu_used, n - 1)
                a_.activation(buf(SM, n)[:, 0:2 * nk], bank[:, 0:2 * nk], ACT.Relu).then_inc(free_sem(("dots", n)), 1)
            drain("ka", by_token(PJ3, PJ_KA))
            wait_drained(act, "ka")
            wait_drained(act, "qa")
            square_heads(PJ3[:, :, 0:1024], SQ[:, :].rearrange("p (t n) -> p t n", t=TT), 64)
            drain("va", by_token(PJ3, PJ_VA))

            def tanh_of(key, dst, cols_=lambda b: b[:, :], done=None):
                bank = wait_full(act, key)
                a_.activation(dst, cols_(bank), ACT.Tanh, scale=0.5).then_inc(done or tanh_ready, 1)

            tanh_of("za", ZT[:, 0:1024])
            for t in range(TT):
                drain_padded(("qa", t), QPAD)
                drain_turned(("ka", t), KT4, 4)
            tanh_of("zb", ZT[:, 1024:2048])
            soften("A")
            drain("qm", by_token(PJ3, PJ_QM))
            wait_drained(act, "qm")
            square_heads(PJ3[:, :, PJ_QM:PJ_QM + 512], SQ[:, 0:1024].rearrange("p (t n) -> p t n", t=TT), 128)
            for t in range(TT):
                for h in range(2):
                    drain_turned(("qb", t, h), QBT[:, 4 * h:4 * h + 4, :], 4, 96)
                    drain_turned(("kb", t, h), KBT[:, 4 * h:4 * h + 4, :], 4, 96)
            tanh_of("zm", ZT[:, 2048:3072])
            soften("B")
            for t in range(TT):
                drain_turned(("qm", t), QMT, 4)
                drain_turned(("km", t), KMT, 4)
            by_half = lambda b: b[:, :].rearrange("p (t n) -> p t n", t=TT)
            tanh_of("gate00", TH[0], by_half, free_sem("gate00"))
            soften("M")
            for n in range(3):
                for h in range(2):
                    if n or h:
                        if n:
                            wait_drained(act, f"wb{n - 1}{h}")
                        tanh_of(f"gate{n}{h}", TH[h], by_half, free_sem(f"gate{n}{h}"))
            wait_drained(act, "wb21")
            act.wait_ge(rows_squared, 3)
            square_rows(2, R1v, R3v, [(mem2_landed, 16)])
            drain("ckv0", by_token(R1v, 0))
            act.wait_ge(rows_normed, 6)
            square_rows(3, X3, ZTv, ["wout0", "wout1"])
            drain("gr", [(GRT[:, :], lambda b: b[0:16, 0:S])])
            bank = wait_full(act, "gqk")
            a_.activation(GQ, bank[:, 0:512], ACT.Copy, scale=64 ** -0.5)
            a_.activation(GK, bank[:, 512:1024], ACT.Copy).then_inc(free_sem("gqk"), 1)
            bank = wait_full(act, "gate_z")
            for h in range(2):
                last = a_.activation(LZ[:, h * S:(h + 1) * S], bank[:, h * S:(h + 1) * S], ACT.Identity,
                                     bias=GC[:, GC_GATEB + h:GC_GATEB + h + 1])
            last.then_inc(free_sem("gate_z"), 1)
            wait_drained(act, "gate_z")
            link(a_.activation(LA, LZ, ACT.Abs))
            link(a_.activation(LA, LA, ACT.Exp, scale=-1.0))
            a_.activation(LA, LA, ACT.Ln, bias=1.0).then_inc(decay_a, 1)
            drain("dq", by_token(DQ, 0))
            drain("dk", by_token(DK, 0))
            wait_drained(act, "dk")
            wait_drained(act, "dq")
            act.wait_ge(decay_a, 2)
            a_.activation(EP, LC, ACT.Exp)
            a_.activation(EN, LC, ACT.Exp, scale=-1.0)
            a_.activation(EE, LE, ACT.Exp)
            a_.activation(EL, LSUM, ACT.Exp).then_inc(decay_e, 1)
            square_heads(PJ[:, 0:2048], SQ[:, :], 64)
            drain("gv", by_token(GV, 0))
            drain("ckv1", by_token(R1v, 512))
            act.wait_ge(pads_cleared, 5)
            for t in range(TT):
                drain_padded(("dq", t), QPAD)
                drain_turned(("dk", t), KT4, 4)
            drain("dv", by_token(DV, 0))
            act.wait_ge(lambda_dots, 1)
            a_.activation(SMALL[:, 50:52], SMALL[:, 48:50], ACT.Exp).then_inc(lambda_exp, 1)
            tanh_of("gg", GG, by_half)
            act.wait_ge(gla_products, 1)
            act.wait_ge(gla_padded, 1)
            drain("ckv2", by_token(R3v, 0))
            act.wait_ge(heads_normed, 6)
            for t in range(TT):
                drain(("gla", t), [(OG[:, t, :], lambda b: b[:, :])])
            wait_drained(act, ("gla", 1))
            square_heads(OG, SQ[:, 0:1024].rearrange("p (t n) -> p t n", t=TT), 128)
            soften("DA")
            act.wait_ge(normed, first_unit["C"])
            for k in range(2):
                wait_drained(act, ("O", first_unit["C"] - 1 - k))
            square_heads(MIXA, SQ[:, 0:1024].rearrange("p (t n) -> p t n", t=TT), 128)
            drain("ckv3", by_token(R3v, 512))
            square_heads(R1[:, :], SQ[:, :], 256)
            for t in range(TT):
                for h in range(2):
                    drain_turned(("mix", t, h), XT3[:, 4 * h:4 * h + 4, :], 4)
            for t in range(TT):
                for h in range(2):
                    drain_turned(("xk", t, h), CK8[:, 4 * h:4 * h + 4, :], 4)
            square_rows(4, X3, ZTv, ["wo0", "wo1"])
            CQN = v2(R2)
            drain("wcq0", by_token(CQN, 0))
            drain("wcq1", by_token(CQN, 512))
            wait_drained(act, "wcq0")
            wait_drained(act, "wcq1")
            square_heads(R2[:, :], SQ[:, :], 256)
            for t in range(TT):
                for h in range(2):
                    drain_turned(("xq", t, h), CQ8[:, 4 * h:4 * h + 4, :], 4)
            soften("C")
            square_rows(5, X3, ZTv, ["wco0", "wco1"])
            act.wait_ge(route_exp, 1)
            a_.activation(R_exp, R_dif, ACT.Exp).then_inc(route_exp, 1)

            act.wait_ge(moe_gathered, 1)
            for h in range(2):
                last = a_.activation(M_rows[:, h * 512:(h + 1) * 512], AUX[h][:, :], ACT.Copy)
            last.then_inc(moe_rows, 1)
            with act.Fori(0, PAIRS) as i:
                act.wait_ge(moe_gate, i + 1)
                a_.activation(M_th, AUX[2][:, :], ACT.Tanh, scale=0.5).then_inc(moe_tanh, 1)
                act.wait_ge(moe_gathered, i + 2)
                for h in range(2):
                    last = a_.activation(M_rows[:, h * 512:(h + 1) * 512], AUX[h][:, :], ACT.Copy)
                last.then_inc(moe_rows, 1)
                act.wait_ge(moe_picks_turned, i + 2)
                a_.activation(M_place, AUX[3][:, 0:256], ACT.Copy).then_inc(moe_picks_t, 1)
                act.wait_ge(moe_down, i + 1)
                for h in range(2):
                    last = a_.activation(M_o[:, h * 512:(h + 1) * 512], AUX[2 + h][:, :], ACT.Copy)
                last.then_inc(moe_out, 1)
            act.wait_ge(flag_ready, 1)
            fullest = act.value_load(FLAG[0:1, 0:1])
            with act.If(fullest > CAP):
                with act.Fori(0, N_EXPERTS * TT) as u:
                    act.wait_ge(all_gate, u + 1)
                    a_.activation(M_th, AUX[0][:, :], ACT.Tanh, scale=0.5).then_inc(all_tanh, 1)
            act.wait_ge(y_done, 1)
            a_.activation(OUT[:, 1, :], ACC[1][:, :], ACT.Copy).then_inc(out_ready2, 1)

        @block.vector
        def _(dve):
            v = nc.vector
            steps = [0]

            def link(ins):
                steps[0] += 1
                ins.then_inc(dve_steps, 1)
                dve.wait_ge(dve_steps, steps[0])

            def rsqrt(n, src):
                x, y, a, b = (NW[:, i * 32:i * 32 + n] for i in range(4))
                link(v.tensor_scalar(x, src, EPS, None, ALU.add))
                link(v.tensor_scalar(NWI[:, 0:n], x.bitcast(I32), 1, None, ALU.logical_shift_right))
                link(v.tensor_scalar(y.bitcast(I32), NWI[:, 0:n], -1.0, RSQRT_SEED, ALU.mult, ALU.add))
                for k in range(3):
                    link(v.tensor_tensor(a, y, y, ALU.mult))
                    link(v.scalar_tensor_tensor(out=b, in0=a, scalar=-0.5, in1=x, op0=ALU.mult, op1=ALU.mult))
                    dst = RS[:, 0:n] if k == 2 else y
                    link(v.scalar_tensor_tensor(out=dst, in0=b, scalar=1.5, in1=y, op0=ALU.add, op1=ALU.mult))

            def norm_rows(n, src, dst, squared):
                dve.wait_ge(rows_squared, squared)
                rsqrt(2, SMALL[:, 16:18])
                for t in range(TT):
                    v.tensor_scalar(dst[:, t, :], src[:, t, :], RS[:, t:t + 1], None, ALU.mult).then_inc(rows_normed, 1)

            def drain_rows(name, dst, gain):
                for t in range(TT):
                    for h in range(2):
                        key = (name, t, h)
                        bank = wait_full(dve, key)
                        v.tensor_tensor(dst[:, 4 * h:4 * h + 4, t * P:(t + 1) * P],
                                        bank[:, :].rearrange("p (k q) -> p k q", k=4),
                                        GC[:, gain + 4 * h:gain + 4 * h + 4].unsqueeze(2).broadcast_to([P, 4, P]),
                                        ALU.mult).then_inc(free_sem(key), 1)

            sq_calls = [0]

            def norm_heads(squares, groups, w, apply, n_gains):
                sq_calls[0] += 1
                dve.wait_ge(squares_ready, sq_calls[0])
                v.tensor_reduce(MS[:, 0:groups], squares.rearrange("p (g w) -> p g w", g=groups), AX_X,
                                ALU.add).then_inc(squares_used, 1)
                dve.wait_ge(squares_used, sq_calls[0])
                rsqrt(groups, MS[:, 0:groups])
                apply()

            def scale_heads(view, c0, h):
                w = view.shape[2]
                return v.tensor_tensor(view, view, RS[:, c0:c0 + h].unsqueeze(2).broadcast_to([P, h, w]), ALU.mult)

            def gain_heads(view, c, factor=None):
                h, w = view.shape[1], view.shape[2]
                gb = GB[:, c:c + w].unsqueeze(1).broadcast_to([P, h, w])
                if factor is None:
                    return v.tensor_tensor(view, view, gb, ALU.mult)
                return v.scalar_tensor_tensor(out=view, in0=view, scalar=factor, in1=gb, op0=ALU.mult, op1=ALU.mult)

            def hv(ap, h):
                return ap.rearrange("p (h w) -> p h w", h=h)

            def mask_scores(name, u, t, h):
                nk = keys_of(t)
                bank = wait_full(dve, ("S", u))
                m = blocks(SM, u, nk)
                b = bank[:, 0:2 * nk].rearrange("p (i k) -> p i k", i=2)
                mask = {"A": None if t is None else SEL3[:, t or 0, 0:nk], "B": causal[:, S - nk:S],
                        "DA": causal[:, S - nk:S]}.get(name)
                if mask is None:
                    ins = v.tensor_scalar(m, b, scales[name], None, ALU.mult)
                else:
                    ins = v.scalar_tensor_tensor(out=m, in0=b, scalar=scales[name],
                                                 in1=mask.unsqueeze(1).broadcast_to([P, 2, nk]), op0=ALU.mult, op1=ALU.add)
                ins.then_inc(free_sem(("S", u)), 1)
                wait_drained(dve, ("S", u))
                link(v.tensor_reduce(stat(u, 2), m, AX_X, ALU.max))
                v.tensor_scalar(stat(u, 0), stat(u, 2), -1.0, None, ALU.mult).then_inc(masked, 1)

            def normalize(name, u, t, h):
                nk = keys_of(t)
                dve.wait_ge(exped, u + 1)
                e = blocks(EX, u, nk)
                link(v.reciprocal(stat(u, 2), stat(u, 1)))
                if name == "DA":
                    link(v.tensor_scalar(e[:, 0, :], e[:, 0, :], stat(u, 2)[:, 0:1], None, ALU.mult))
                    link(v.tensor_scalar(stat(u, 2)[:, 1:2], stat(u, 2)[:, 1:2], SMALL[:, 54:55], None, ALU.mult))
                    v.scalar_tensor_tensor(out=e[:, 0, :], in0=e[:, 1, :], scalar=stat(u, 2)[:, 1:2], in1=e[:, 0, :],
                                           op0=ALU.mult, op1=ALU.add).then_inc(normed, 1)
                else:
                    v.tensor_tensor(e, e, stat(u, 2).unsqueeze(2).broadcast_to([P, 2, nk]), ALU.mult).then_inc(normed, 1)

            def take_output(name, u, t, h):
                bank = wait_full(dve, ("O", u))
                free = free_sem(("O", u))
                if name in ("A", "B"):
                    y = YT[:, 4 * (name == "B") + h, t * P:(t + 1) * P]
                    for i in range(2):
                        r = slice(64 * i, 64 * i + 64)
                        ins = v.tensor_tensor(y[r], bank[r, i * P:(i + 1) * P], y[r], ALU.mult)
                elif name == "M":
                    ins = v.tensor_tensor(YT[:, 8 + h, :], bank[:, 0:S], YT[:, 8 + h, :], ALU.mult)
                elif name == "DA":
                    ins = v.tensor_copy(MIXA[:, t, h * P:(h + 1) * P], bank[:, 0:P])
                else:
                    ins = v.tensor_copy(XT3[:, 2 * h:2 * h + 2, :], bank[:, :].rearrange("p (d q) -> p d q", d=2))
                ins.then_inc(free, 1)

            def attention(name):
                U = len(units[name])
                for s in range(U + 2):
                    for lag, step in enumerate((mask_scores, normalize, take_output)):
                        if 0 <= s - lag < U:
                            step(name, first_unit[name] + s - lag, *units[name][s - lag])

            tanhs = [0]

            def silu_t(key, dst):
                tanhs[0] += 1
                dve.wait_ge(tanh_ready, tanhs[0])
                bank = wait_full(dve, key)
                v.scalar_tensor_tensor(out=dst, in0=dst, scalar=1.0, in1=bank[:, :], op0=ALU.add,
                                       op1=ALU.mult).then_inc(free_sem(key), 1)

            dve.wait_ge(consts_ready, 1)
            bank = wait_full(dve, "gains")
            v.tensor_copy(GC[:, :], bank[:, 0:GC_N]).then_inc(free_sem("gains"), 1)
            wait_drained(dve, "gains")
            dve.wait_ge(small_landed, small_total)
            norm_rows(0, R1v, R3v, 1)
            norm_rows(1, X3, ZTv, 2)
            drain_rows("mem", R2T, GC_MEM)
            drain_rows("x0", XT3, GC_NORM)
            posf = NW[:, 0:2]
            ang, turns, sin_a, cos_a = (trig[:, 32 * i:32 * i + 32] for i in range(4))
            link(v.tensor_copy(posf, pos_i[:, :]))
            for t in range(TT):
                ins = v.tensor_scalar(ang[:, 16 * t:16 * t + 16], freq[:, :], posf[:, t:t + 1], None, ALU.mult)
            link(ins)
            for arg, shift in ((sin_a, 0.0), (cos_a, 0.25)):
                link(v.tensor_scalar(turns, ang, 1.0 / (2 * math.pi), shift, ALU.mult, ALU.add))
                link(v.tensor_scalar(turns, turns, 12582912.0, 12582912.0, ALU.add, ALU.subtract))
                link(v.scalar_tensor_tensor(out=arg, in0=turns, scalar=-6.28125, in1=ang, op0=ALU.mult, op1=ALU.add))
                for part in (2029 / 2 ** 20, 2 * math.pi - 6.28125 - 2029 / 2 ** 20):
                    link(v.scalar_tensor_tensor(out=arg, in0=turns, scalar=-part, in1=arg, op0=ALU.mult, op1=ALU.add))
                if shift:
                    link(v.tensor_scalar(arg, arg, math.pi / 2, None, ALU.add))
                v.tensor_scalar(arg, arg, 3.1415925, -3.1415925, ALU.min, ALU.max).then_inc(trig_arg, 1)
                dve.wait_ge(trig_arg, 2 if shift else 1)

            def apply_km():
                for t in range(TT):
                    ins = scale_heads(hv(R1v[:, t, 0:512], 4), 4 * t, 4)
                link(ins)
                for t in range(TT):
                    ins = gain_heads(hv(R1v[:, t, 0:512], 4), GB_M + 128)
                ins.then_inc(heads_normed, 1)

            norm_heads(SQ[:, 0:1024], 8, 128, apply_km, 1)
            dve.wait_ge(rows_squared, 3)
            rsqrt(4, SMALL[:, 20:24])
            for t in range(TT):
                v.tensor_scalar(PJ3[:, t, PJ_CQ:PJ_CQ + 384], PJ3[:, t, PJ_CQ:PJ_CQ + 384], RS[:, 2 * t:2 * t + 1], None, ALU.mult)
                ins = v.tensor_scalar(PJ3[:, t, PJ_CKV:PJ_CKV + 256], PJ3[:, t, PJ_CKV:PJ_CKV + 256],
                                      RS[:, 2 * t + 1:2 * t + 2], None, ALU.mult)
            ins.then_inc(latents_normed, 1)
            for t in range(TT):
                for name, n, dst, gain in (("cq", 3, CQT, GC_CQ), ("ckv", 2, CKVT, GC_CKV)):
                    bank = wait_full(dve, (name, t))
                    v.tensor_tensor(dst[:, :, t * P:(t + 1) * P], bank[:, 0:n * P].rearrange("p (k q) -> p k q", k=n),
                                    GC[:, gain:gain + n].unsqueeze(2).broadcast_to([P, n, P]),
                                    ALU.mult).then_inc(free_sem((name, t)), 1)
            link(v.tensor_scalar(WI, PJ3[:, :, PJ_WI:PJ_WI + 8], 64 ** -0.5 * 8 ** -0.5, None, ALU.mult))

            def apply_heads(per_tile, gain, count=True):
                for t in range(TT):
                    view, c = per_tile(t)
                    ins = scale_heads(view, c, view.shape[1])
                link(ins)
                for t in range(TT):
                    view, c = per_tile(t)
                    ins = gain_heads(view, gain)
                ins.then_inc(heads_normed, 1)

            norm_heads(SQ[:, 0:1536], 16, 96, lambda: apply_heads(lambda t: (hv(QB[:, t, :], 8), 8 * t), GB_B), 1)
            norm_heads(SQ[:, 0:1536], 16, 96, lambda: apply_heads(lambda t: (KB[:, t, :, :], 8 * t), GB_B + 96), 1)
            for n in range(8):
                t = n // 4
                nk = keys_of(t)
                wait_drained(dve, ("dots", n))
                for i in range(2):
                    h = 2 * (n % 4) + i
                    r = buf(SM, n)[:, i * nk:(i + 1) * nk]
                    acc_ = IX3[:, t, 0:nk]
                    if h == 0:
                        ins = v.tensor_scalar(acc_, r, WI[:, t, h:h + 1], None, ALU.mult)
                    else:
                        ins = v.scalar_tensor_tensor(out=acc_, in0=r, scalar=WI[:, t, h:h + 1], in1=acc_,
                                                     op0=ALU.mult, op1=ALU.add)
                    if i == 0:
                        link(ins)
                ins.then_inc(relu_used, 1)
                dve.wait_ge(relu_used, n + 1)
            for t in range(TT):
                nk = keys_of(t)
                ins = v.tensor_tensor(IX3[:, t, 0:nk], IX3[:, t, 0:nk], causal[:, S - nk:S], ALU.add)
            link(ins)
            best = NW[:, 0:16].rearrange("p (t n) -> p t n", t=TT)
            for k in range(TOPK // 8):
                for t in range(TT):
                    ins = v.max(best[:, t, :], IX3[:, t, 0:keys_of(t)])
                link(ins)
                for t in range(TT):
                    ins = v.match_replace(IX3[:, t, 0:keys_of(t)], best[:, t, :], IX3[:, t, 0:keys_of(t)], TAKEN)
                link(ins)
            for t in range(TT):
                nk = keys_of(t)
                ins = v.tensor_scalar(IX3[:, t, 0:nk], IX3[:, t, 0:nk], -2e38, NEG, ALU.is_gt, ALU.mult)
            link(ins)
            for t in range(TT):
                nk = keys_of(t)
                ins = v.tensor_tensor(SEL3[:, t, 0:nk], IX3[:, t, 0:nk], causal[:, S - nk:S], ALU.add)
            link(ins)

            def apply_a(q, k, g0):
                def go():
                    for t in range(TT):
                        ins = scale_heads(q(t), 16 * t, 16) if k is None else None
                        if k is not None:
                            scale_heads(q(t), 8 * t, 8)
                            ins = scale_heads(k(t), 16 + 8 * t, 8)
                    link(ins)
                    for t in range(TT):
                        if k is None:
                            gain_heads(q(t)[:, 0:8, :], g0)
                            ins = gain_heads(q(t)[:, 8:16, :], g0 + 64)
                        else:
                            gain_heads(q(t), g0)
                            ins = gain_heads(k(t), g0 + 64)
                    ins.then_inc(heads_normed, 1)
                return go

            norm_heads(SQ[:, :], 32, 64, apply_a(lambda t: hv(PJ3[:, t, 0:1024], 16), None, GB_A), 2)
            silu_t("za", ZT[:, 0:1024])
            silu_t("zb", ZT[:, 1024:2048])
            attention("A")
            norm_heads(SQ[:, 0:1024], 8, 128,
                       lambda: apply_heads(lambda t: (hv(PJ3[:, t, PJ_QM:PJ_QM + 512], 4), 4 * t), GB_M), 1)
            silu_t("zm", ZT[:, 2048:3072])
            attention("B")
            attention("M")
            for n in range(3):
                for h in range(2):
                    dst = R1v[:, :, h * 512:(h + 1) * 512]
                    tmp = R4[:, 0:1024].rearrange("p (t n) -> p t n", t=TT)
                    key = f"wb{n}{h}"
                    wait_drained(dve, f"gate{n}{h}")
                    bank = wait_full(dve, key)
                    ins = v.scalar_tensor_tensor(out=dst if n == 0 else tmp, in0=TH[h], scalar=1.0,
                                                 in1=bank[:, :].rearrange("p (t n) -> p t n", t=TT), op0=ALU.add, op1=ALU.mult)
                    ins.then_inc(free_sem(key), 1)
                    if n:
                        wait_drained(dve, key)
                        ins = v.tensor_tensor(dst, dst, tmp, ALU.add)
                        if n == 2:
                            ins.then_inc(merged_ready, 1)
                            dve.wait_ge(merged_ready, h + 1)
                        else:
                            link(ins)
            for t in range(TT):
                for h in range(2):
                    key = ("merged", t, h)
                    bank = wait_full(dve, key)
                    v.tensor_copy(XT3[:, 4 * h:4 * h + 4, t * P:(t + 1) * P],
                                  bank[:, :].rearrange("p (k q) -> p k q", k=4)).then_inc(free_sem(key), 1)

            def add_to_x(key, h, factor):
                bank = wait_full(dve, key)
                x = X3[:, :, h * 512:(h + 1) * 512]
                v.scalar_tensor_tensor(out=x, in0=bank[:, :].rearrange("p (t n) -> p t n", t=TT), scalar=factor, in1=x,
                                       op0=ALU.mult, op1=ALU.add).then_inc(free_sem(key), 1)
                wait_drained(dve, key)

            add_to_x("wout0", 0, 0.25)
            add_to_x("wout1", 1, 0.25)
            norm_rows(2, R1v, R3v, 4)
            drain_rows("mem2", R2T, GC_MEM2)
            norm_rows(3, X3, ZTv, 5)
            drain_rows("x1", XT3, GC_MIX)
            lam = GB[:, GB_LAM:GB_LAM + 256].rearrange("p (a b d) -> p a b d", a=2, b=2)
            link(v.tensor_tensor(lam[:, :, 0, :], lam[:, :, 0, :], lam[:, :, 1, :], ALU.mult))
            v.tensor_reduce(SMALL[:, 48:50], lam[:, :, 0, :], AX_X, ALU.add).then_inc(lambda_dots, 1)
            dve.wait_ge(decay_a, 1)
            link(v.tensor_scalar(LZ, LZ, 0.0, 1 / 16, ALU.min, ALU.mult))
            link(v.scalar_tensor_tensor(out=LG_, in0=LA, scalar=-1 / 16, in1=LZ, op0=ALU.mult, op1=ALU.add))
            for c in range(8):
                one = slice(64 * c, 64 * c + 64)
                ins = v.tensor_tensor_scan(LSUM[:, one], ones[:, 0:64], LG_[:, one], 0.0, ALU.mult, ALU.add)
            link(ins)
            chunked_ = lambda ap: ap.rearrange("p (c i) -> p c i", i=CHUNK)
            ls = chunked_(LSUM)
            v.tensor_tensor(chunked_(LC), ls, ls[:, :, 31:32].broadcast_to([P, 8, CHUNK]), ALU.subtract)
            v.tensor_tensor(chunked_(LE), ls[:, :, 63:64].broadcast_to([P, 8, CHUNK]), ls, ALU.subtract).then_inc(decay_a, 1)
            dve.wait_ge(decay_e, 1)
            dve.wait_ge(pads_cleared, 4)
            link(v.tensor_copy(DEC, chunked_(EL)[:, :, 63]))
            for dst, a, b in ((KNZ, GK, EN), (KPZ, GK, EP), (QLZ, GQ, EL)):
                for i in range(2):
                    r = slice(64 * i, 64 * i + 64)
                    ins = v.tensor_tensor(dst.rearrange("p (h i) q -> p h i q", i=2)[r, :, i, :], kt(a, 2)[r], kt(b, 2)[r],
                                          ALU.mult)
            ins.then_inc(gla_padded, 1)
            norm_heads(SQ[:, :], 32, 64, apply_a(lambda t: hv(DQ[:, t, :], 8), lambda t: hv(DK[:, t, :], 8), GB_DA), 2)
            for t in range(TT):
                bank = wait_full(dve, ("intra", t))
                pb = bank[:, :].rearrange("p (a h q) -> p a h q", a=2, h=4)
                link(v.copy_predicated(ATT[:, t, :, :], past[:, :].bitcast(U32).unsqueeze(1).broadcast_to([P, 4, P]), pb[:, 0]))
                v.copy_predicated(ATT[:, t, :, :], future[:, :].bitcast(U32).unsqueeze(1).broadcast_to([P, 4, P]),
                                  pb[:, 1]).then_inc(free_sem(("intra", t)), 1)
            bank = wait_full(dve, "kend")
            kb_ = bank[:, :].rearrange("p (n d) -> p n d", n=4)
            v.tensor_copy(KEN[0:64, 0, :, :], kb_[0:64])
            v.tensor_copy(KEN[64:128, 1, :, :], kb_[64:128]).then_inc(free_sem("kend"), 1)
            dve.wait_ge(tanh_ready, 4)
            bank = wait_full(dve, "gg")
            v.scalar_tensor_tensor(out=GG, in0=GG, scalar=1.0, in1=bank[:, :].rearrange("p (t n) -> p t n", t=TT),
                                   op0=ALU.add, op1=ALU.mult).then_inc(free_sem("gg"), 1)
            for c in range(3):
                bank = wait_full(dve, ("state", c))
                for h in range(2):
                    for i in range(2):
                        r = slice(64 * i, 64 * i + 64)
                        u_ = bank[r, h * 256 + i * P:h * 256 + (i + 1) * P]
                        if c == 0:
                            ins = v.tensor_copy(ST[r, c, h, :], u_)
                        else:
                            ins = v.scalar_tensor_tensor(out=ST[r, c, h, :], in0=ST[r, c - 1, h, :],
                                                         scalar=DEC[r, 4 * h + c:4 * h + c + 1], in1=u_, op0=ALU.mult, op1=ALU.add)
                ins.then_inc(free_sem(("state", c)), 1)
                wait_drained(dve, ("state", c))
            dve.wait_ge(lambda_exp, 1)
            link(v.tensor_tensor(SMALL[:, 53:54], SMALL[:, 51:52], SMALL[:, 50:51], ALU.subtract))
            link(v.tensor_scalar(SMALL[:, 54:55], SMALL[:, 53:54], -LAM_INIT, None, ALU.add))

            def apply_out(view, gain, factor):
                def go():
                    for t in range(TT):
                        ins = scale_heads(hv(view[:, t, :], 4), 4 * t, 4)
                    link(ins)
                    for t in range(TT):
                        ins = gain_heads(hv(view[:, t, :], 4), gain, factor)
                    ins.then_inc(heads_normed, 1)
                return go

            norm_heads(SQ[:, 0:1024], 8, 128, apply_out(OG, GB_GLAO, 0.5), 1)
            dve.wait_ge(heads_normed, 7)
            v.tensor_tensor(GG, GG, OG, ALU.mult).then_inc(mix_ready, 1)
            attention("DA")
            norm_heads(SQ[:, 0:1024], 8, 128, apply_out(MIXA, GB_DAO, 1.0 - LAM_INIT), 1)

            def apply_cross(T, gain):
                def go():
                    link(scale_heads(hv(T[:, :], 8), 0, 8))
                    gain_heads(hv(T[:, :], 8), gain).then_inc(heads_normed, 1)
                return go

            norm_heads(SQ[:, :], 8, 256, apply_cross(R1, GB_X + 256), 1)
            add_to_x("wo0", 0, 1.0)
            add_to_x("wo1", 1, 1.0)
            norm_rows(4, X3, ZTv, 6)
            drain_rows("x2", XT3, GC_CROSS)
            norm_heads(SQ[:, :], 8, 256, apply_cross(R2, GB_X), 1)
            attention("C")
            add_to_x("wco0", 0, 1.0)
            add_to_x("wco1", 1, 1.0)
            norm_rows(5, X3, ZTv, 7)
            drain_rows("x3", XT3, GC_FFN)

            b4 = lambda ap, n: ap.unsqueeze(2).broadcast_to([P, TT, n])
            bank = wait_full(dve, "router")
            v.tensor_tensor(R_log, bank[:, 0:72].rearrange("p (t n) -> p t n", t=TT),
                            GB[:, GB_ROUTE:GB_ROUTE + 36].unsqueeze(1).broadcast_to([P, TT, 36]),
                            ALU.add).then_inc(free_sem("router"), 1)
            wait_drained(dve, "router")
            lg, le = R_log[:, :, 0:4], R_log[:, :, 4:36].rearrange("p t (g j) -> p t g j", g=4)

            def first_best(x, n, m, w, one, pr):
                link(v.tensor_reduce(m, x, AX_X, ALU.max))
                link(v.tensor_tensor(w, x, b4(m, n), ALU.is_equal))
                link(v.tensor_tensor(w, w, pr.unsqueeze(1).broadcast_to([P, TT, n]), ALU.mult))
                link(v.tensor_reduce(R_m, w, AX_X, ALU.max))
                link(v.tensor_tensor(one, w, b4(R_m, n), ALU.is_equal))

            first_best(lg, 4, R_m1, R_w4, R_gs, pref[:, 8:12])
            link(v.tensor_tensor(R_dif4, lg, b4(R_m1, 4), ALU.subtract))
            link(v.tensor_tensor(R_big, le, R_gs.unsqueeze(3).broadcast_to([P, TT, 4, 8]), ALU.mult))
            link(v.tensor_reduce(R_el, R_big.rearrange("p t g j -> p t j g"), AX_X, ALU.add))
            first_best(R_el, 8, R_m1, R_w8, R_s1, pref[:, 0:8])
            link(v.scalar_tensor_tensor(out=R_el, in0=R_s1, scalar=NEG, in1=R_el, op0=ALU.mult, op1=ALU.add))
            first_best(R_el, 8, R_m2, R_w8, R_s2, pref[:, 0:8])
            v.tensor_tensor(R_dif2, R_m2, R_m1, ALU.subtract).then_inc(route_exp, 1)
            dve.wait_ge(route_exp, 2)
            link(v.tensor_reduce(R_m1, R_exp4, AX_X, ALU.add))
            link(v.scalar_tensor_tensor(out=R_m2, in0=R_exp2, scalar=1.0, in1=R_m1, op0=ALU.add, op1=ALU.mult))
            link(v.reciprocal(R_m1, R_m2))
            link(v.tensor_tensor(R_m2, R_m1, R_exp2, ALU.mult))
            link(v.tensor_tensor(R_w8, R_s1, b4(R_m1, 8), ALU.mult))
            link(v.tensor_tensor(R_el, R_s2, b4(R_m2, 8), ALU.mult))
            link(v.tensor_tensor(R_w8, R_w8, R_el, ALU.add))
            link(v.tensor_tensor(R_s1, R_s1, R_s2, ALU.add))
            for t in range(TT):
                for dst, src in ((R_gate[:, t, 0:32], R_w8), (R_sel[:, t, :], R_s1)):
                    ins = v.tensor_tensor(hv(dst, 4), R_gs[:, t, :].unsqueeze(2).broadcast_to([P, 4, 8]),
                                          src[:, t, :].unsqueeze(1).broadcast_to([P, 4, 8]), ALU.mult)
            v.memset(R_gate[:, :, 32:34], 0.0)
            v.memset(R_rank[:, :, 32:34], -1.0)
            ins.then_inc(route_ready, 1)
            bank = wait_full(dve, "ranks")
            link(v.tensor_reduce(R_m[:, 0:1], bank[:, 64:96], AX_X, ALU.max))
            v.tensor_copy(FLAG[:, :], R_m[:, 0:1]).then_inc(flag_ready, 1)
            rk = R_rank[:, :, 0:32]
            link(v.scalar_tensor_tensor(out=rk, in0=bank[:, 0:64].rearrange("p (t n) -> p t n", t=TT), scalar=1.0,
                                        in1=R_sel, op0=ALU.add, op1=ALU.mult))
            link(v.tensor_scalar(rk, rk, -1.0, None, ALU.add))
            link(v.tensor_scalar(R_over, rk, CAP - 0.5, 0.5, ALU.is_gt, ALU.mult))
            v.tensor_tensor(R_over, R_over, R_gate[:, :, 0:32], ALU.mult).then_inc(free_sem("ranks"), 1)
            wait_drained(dve, "ranks")

            pl = iota[:, :].unsqueeze(1).broadcast_to([P, 2, CAP])

            def picks(dst, t, first):
                return v.tensor_tensor(dst[:, t, :].rearrange("p (e c) -> p e c", e=2), pl,
                                       R_rank[:, t, first].unsqueeze(2).broadcast_to([P, 2, CAP]), ALU.is_equal)

            def take_input():
                for h in range(2):
                    ins = v.tensor_tensor(M_xt[:, 4 * h:4 * h + 4, :], AUX[h][:, :].rearrange("p (k c) -> p k c", k=4),
                                          GC[:, GC_FFN + 4 * h:GC_FFN + 4 * h + 4].unsqueeze(2).broadcast_to([P, 4, P]), ALU.mult)
                ins.then_inc(moe_input, 1)

            picks(M_pick, 0, slice(0, 2))
            picks(M_pick, 1, slice(0, 2)).then_inc(moe_picks, 1)
            dve.wait_ge(moe_rows_turned, 1)
            take_input()
            with dve.Fori(0, PAIRS) as i:
                dve.wait_ge(moe_picks_turned, i + 1)
                picks(M_gpick, 0, bass.ds(i * 2, 2))
                picks(M_gpick, 1, bass.ds(i * 2, 2)).then_inc(moe_weighting, 1)
                dve.wait_ge(moe_weighting, i * 2 + 1)
                for t in range(TT):
                    ins = v.tensor_tensor(M_gpick[:, t, :].rearrange("p (e c) -> p e c", e=2),
                                          M_gpick[:, t, :].rearrange("p (e c) -> p e c", e=2),
                                          R_gate[:, t, bass.ds(i * 2, 2)].unsqueeze(2).broadcast_to([P, 2, CAP]), ALU.mult)
                ins.then_inc(moe_weighting, 1)
                dve.wait_ge(moe_gathered, i + 1)
                picks(M_pick, 0, bass.ds(i * 2 + 2, 2))
                picks(M_pick, 1, bass.ds(i * 2 + 2, 2)).then_inc(moe_picks, 1)
                dve.wait_ge(moe_tanh, i + 1)
                v.scalar_tensor_tensor(out=M_hid, in0=M_th, scalar=1.0, in1=AUX[2][:, :], op0=ALU.add,
                                       op1=ALU.mult).then_inc(moe_gated, 1)
                dve.wait_ge(moe_gated, i + 1)
                dve.wait_ge(moe_up, i + 1)
                v.scalar_tensor_tensor(out=M_hid, in0=M_hid, scalar=0.5, in1=AUX[3][:, :], op0=ALU.mult,
                                       op1=ALU.mult).then_inc(moe_hidden, 1)
                dve.wait_ge(moe_turned, i + 1)
                v.tensor_copy(M_hidt, AUX[2][:, :].rearrange("p (k c) -> p k c", k=4)).then_inc(moe_hidden_t, 1)
                dve.wait_ge(moe_rows_turned, i + 2)
                take_input()
            dve.wait_ge(flag_ready, 1)
            fullest = dve.value_load(FLAG[0:1, 0:1])
            with dve.If(fullest > CAP):
                with dve.Fori(0, N_EXPERTS) as e:
                    for t in range(TT):
                        dve.wait_ge(all_tanh, e * 2 + t + 1)
                        v.scalar_tensor_tensor(out=M_hid, in0=M_th, scalar=1.0, in1=AUX[0][:, :], op0=ALU.add,
                                               op1=ALU.mult).then_inc(all_gated, 1)
                        dve.wait_ge(all_gated, e * 2 + t + 1)
                        v.scalar_tensor_tensor(out=M_hid, in0=M_hid, scalar=R_over[:, t, bass.ds(e, 1)], in1=AUX[1][:, :],
                                               op0=ALU.mult, op1=ALU.mult).then_inc(all_hidden, 1)
                        dve.wait_ge(all_turned, e * 2 + t + 1)
                        v.tensor_copy(M_hidt, AUX[2][:, :].rearrange("p (k c) -> p k c", k=4)).then_inc(all_hidden_t, 1)
            dve.wait_ge(y_done, 1)
            v.tensor_copy(OUT[:, 0, :], ACC[0][:, :]).then_inc(out_ready, 1)


_INS = ["x", "mem", "positions", "g_norm", "w_in", "g_qn_a", "g_kn_a", "g_cq", "g_ckv", "w_uq", "w_ukv", "g_qn_b",
        "g_kn_b", "g_mem", "w_mem_kv", "g_qn_m", "g_kn_m", "w_branch", "w_out", "mem_2", "norm_mix_2", "w_in_2",
        "da_q_norm_2", "da_k_norm_2", "lambda_q1_2", "lambda_k1_2", "lambda_q2_2", "lambda_k2_2", "da_out_norm_2",
        "gla_gate_w_2", "gla_gate_b_2", "gla_out_norm_2", "w_o_2", "norm_cross_2", "norm_mem_2", "w_cq_2", "w_ckv_2",
        "cross_q_norm_2", "cross_k_norm_2", "w_co_2", "norm_ffn_2", "w_group_2", "b_group_2", "w_expert_2", "b_expert_2",
        "w_e_gate_2", "w_e_up_2", "w_e_down_2"]


def kernel(**inputs):
    import numpy as _np
    import concourse.bacc as _bacc
    from concourse import mybir as _mybir
    from concourse.bass_utils import run_bass_kernel_spmd as _run

    nc = _bacc.Bacc("TRN2", target_bir_lowering=False, num_devices=1)
    arrays, args = {}, {}
    for name in _INS:
        a = _np.ascontiguousarray(inputs[name])
        arrays[f"in_{name}_dram"] = a
        args[name] = nc.dram_tensor(f"in_{name}_dram", a.shape, _mybir.dt.from_np(a.dtype), kind="ExternalInput").ap()
    out = nc.dram_tensor("out_0_dram", (1, S, D), F32, kind="ExternalOutput").ap()
    two_block_layer(nc, args, out)
    r = _run(nc, [arrays], core_ids=[0])
    return r.results[0]["out_0_dram"]
```

```python
import math
from contextlib import ExitStack

import numpy as np

import concourse.bass as bass
from concourse import mybir

F32 = mybir.dt.float32
I32 = mybir.dt.int32
BF16 = mybir.dt.bfloat16
U32 = mybir.dt.uint32
ALU = mybir.AluOpType
ACT = mybir.ActivationFunctionType
AX_X = mybir.AxisListType.X

P = 128
D = 1024
S = 256
TT = S // P
KD = D // P
EPS = 1e-6
NEG = -1e30
TAKEN = -3e38
THETA = 500000.0
CHUNK = 64
TOPK = 64
N_EXPERTS = 32
N_GROUPS = 4
PER_GROUP = N_EXPERTS // N_GROUPS
D_EXPERT = 512
CAP = 64
PAIRS = N_EXPERTS // 2
LAM_INIT = 0.8 - 0.6 * math.exp(0.0)
RSQRT_SEED = float(0x5F3759DF)
SLOT = KD * 512
RING = 4

IN_QA, IN_KI, IN_ZA, IN_CQ, IN_CKV, IN_ZB, IN_QM, IN_ZM, IN_GATES = 0, 2048, 2120, 2632, 3016, 3304, 3816, 4328, 4840
PJ_QA, PJ_KA, PJ_VA, PJ_QI, PJ_KI, PJ_WI, PJ_CKV, PJ_KR, PJ_CQ, PJ_QM, PJ_W = 0, 512, 1024, 1536, 2048, 2112, 2120, 2376, 2408, 2792, 3304
GC_NORM, GC_MEM, GC_MIX, GC_CROSS, GC_MEM2, GC_FFN, GC_CQ, GC_CKV, GC_GATEB, GC_N = 0, 8, 16, 24, 32, 40, 48, 51, 53, 55
GB_A, GB_B, GB_M, GB_DA, GB_DAO, GB_GLAO, GB_X, GB_ROUTE, GB_LAM, GB_N = 0, 128, 320, 576, 704, 832, 960, 1472, 1508, 1764


def two_block_layer(nc, A, out):
    ctx = ExitStack()
    with ctx:
        def sb(name, cols, dt=F32, parts=P):
            return ctx.enter_context(nc.sbuf_tensor(name, [parts, cols], dt))

        def sem(name):
            return ctx.enter_context(nc.semaphore(name))

        ring = sb("ring", RING * SLOT)
        PJ = sb("PJ", 2 * SLOT)
        BIG1 = sb("BIG1", 3072 + 1024 + TT * D)
        ZT = BIG1[:, 0:3072]
        PT = BIG1[:, 3072:4096]
        X = BIG1[:, 4096:6144]
        BIG2 = sb("BIG2", TT * D + 768 + TT * S + KD * S)
        R3 = BIG2[:, 0:2048]
        IX = BIG2[:, 2048:2816]
        SEL = BIG2[:, 2816:3328]
        XT = BIG2[:, 3328:5376]
        R1 = sb("R1", TT * D)
        R2 = sb("R2", KD * S)
        R4 = sb("R4", 1536)
        R5 = sb("R5", 4096)
        SQE = sb("SQE", SLOT)
        ident = sb("ident", P)
        causal = sb("causal", S)
        past = sb("past", P)
        future = sb("future", P)
        before = sb("before", P)
        ones = sb("ones", P)
        zeros = sb("zeros", P)
        iota = sb("iota", CAP)
        pref = sb("pref", 16)
        freq = sb("freq", 16)
        GC = sb("GC", GC_N)
        GB = sb("GB", GB_N)
        pos_i = sb("pos_i", TT, I32)
        trig = PJ[:, 7936:8128]
        iota_i = trig[:, 0:CAP].bitcast(I32)
        GW = PJ[0:16, 7680:7936]
        GRT = R4[0:16, 0:S]
        WR = R4[:, 0:KD * 36]
        RT = R4[:, 512:1056]
        SQ = SQE[:, 0:2048]
        SME = SQE[:, 2048:4096]
        SM, EX = SME[:, 0:1024], SME[:, 1024:2048]
        GR = EX[0:GC_N, 512:640]
        ROT = PT[:, 0:512]
        MS = sb("MS", 32)
        NW = sb("NW", 4 * 32)
        NWI = sb("NWI", 32, I32)
        RS = sb("RS", 32)
        SMALL = sb("SMALL", 80)
        FLAG = sb("FLAG", 1, I32)

        slots = [ring[:, i * SLOT:(i + 1) * SLOT] for i in range(RING)] + [PJ[:, 0:SLOT], PJ[:, SLOT:2 * SLOT]]

        def v2(t, n=D):
            return t[:, 0:TT * n].rearrange("p (t n) -> p t n", t=TT)

        def kt(ap, k):
            return ap.rearrange("p (k s) -> p k s", k=k)

        X3, R1v, R3v = v2(X), v2(R1), v2(R3)
        ZTv = v2(ZT)
        XT3, R2T = kt(XT[:, :], KD), kt(R2[:, :], KD)
        PJ3 = PJ[:, 0:TT * PJ_W].rearrange("p (t n) -> p t n", t=TT)
        QB = R4[:, :].rearrange("p (t n) -> p t n", t=TT)
        KB = R2[:, 0:1536].rearrange("p (t h d) -> p t h d", t=TT, h=8)
        KNB = R3[:, 0:1024].rearrange("p (t h d) -> p t h d", t=TT, h=8)
        VB = R3[:, 1024:2048].rearrange("p (t h d) -> p t h d", t=TT, h=8)
        CQT, CKVT = kt(R2[:, 0:768], 3), kt(R2[:, 768:1280], 2)
        YT = kt(ZT[:, :], 12)
        QPAD = kt(R5[:, 0:2048], 8)
        KT4 = kt(R5[:, 2048:3072], 4)
        KIT = R5[:, 2048:2304]
        QBT, KBT = kt(R5[:, 0:2048], 8), kt(R5[:, 2048:4096], 8)
        QMT, KMT = kt(R5[:, 0:1024], 4), kt(R5[:, 1024:2048], 4)
        IX3, SEL3 = v2(IX, S), v2(SEL, S)
        R_sel = RT[:, 0:64].rearrange("p (t n) -> p t n", t=TT)
        DQ, DK, DV, GV, GG = (PJ[:, i * 1024:(i + 1) * 1024].rearrange("p (t n) -> p t n", t=TT) for i in range(5))
        KNZ, KPZ, QLZ = (kt(ZT[:, i * 1024:(i + 1) * 1024], 4) for i in range(3))
        QP, QN, KE = (kt(PJ[:, 5120 + i * 512:5632 + i * 512], 2) for i in range(3))
        KEN = PJ[:, 6656:7680].rearrange("p (c n d) -> p c n d", c=2, n=4)
        ATT = R5[:, 3072:4096].rearrange("p (t h q) -> p t h q", t=TT, h=4)
        ST = IX[:, 0:768].rearrange("p (c h v) -> p c h v", c=3, h=2)
        LZ, LA, LG_, LSUM = (T[:, i * 512:(i + 1) * 512] for T in (SM, EX) for i in range(2))
        LC, LE = (PT[:, i * 512:(i + 1) * 512] for i in range(2))
        EP, EN = IX[:, 0:512], SEL[:, :]
        EL, EE, GQ, GK = (R3[:, i * 512:(i + 1) * 512] for i in range(4))
        OG = SQ[:, 1024:2048].rearrange("p (t n) -> p t n", t=TT)
        CQ8, CK8 = kt(R5[:, 0:2048], 8), kt(R5[:, 2048:4096], 8)
        VM = R1v[:, :, 512:1024]
        TH = [R3[:, h * 1024:(h + 1) * 1024].rearrange("p (t n) -> p t n", t=TT) for h in range(2)]
        WI = SMALL[:, 32:48].rearrange("p (t n) -> p t n", t=TT)
        DEC = SMALL[:, 56:64]

        def stat(u, k):
            c = 6 * (u % 4) + 2 * k
            return SMALL[:, c:c + 2]

        def rt(c, *dims):
            n = int(np.prod(dims))
            ap = RT[:, c:c + n]
            if len(dims) == 2:
                return ap.rearrange("p (t n) -> p t n", t=dims[0])
            return ap.rearrange("p (t g j) -> p t g j", t=dims[0], g=dims[1]) if len(dims) == 3 else ap

        R_log, R_m, R_m1, R_m2 = rt(64, TT, 36), rt(136, TT), rt(138, TT), rt(140, TT)
        R_w4, R_gs, R_w8, R_el = rt(144, TT, 4), rt(152, TT, 4), rt(160, TT, 8), rt(176, TT, 8)
        R_s1, R_s2, R_big = rt(192, TT, 8), rt(208, TT, 8), rt(224, TT, 4, 8)
        R_dif, R_dif4, R_dif2 = RT[:, 288:298], rt(288, TT, 4), rt(296, TT)
        R_exp, R_exp4, R_exp2 = RT[:, 300:310], rt(300, TT, 4), rt(308, TT)
        R_gate, R_rank, R_over = rt(320, TT, 34), rt(400, TT, 34), rt(480, TT, 32)
        M_rows, M_xt = R1[:, 0:1024], kt(R1[:, 1024:2048], KD)
        M_o, M_hid, M_th = R2[:, 0:1024], R2[:, 1024:1536], R2[:, 1536:2048]
        M_hidt, M_place = kt(R3[:, 0:512], 4), R3[:, 512:768]
        M_pick, M_gpick = (R3[:, 768 + i * 256:1024 + i * 256].rearrange("p (t n) -> p t n", t=TT) for i in range(2))
        m_slot = [kt(slots[i], KD) for i in range(4)]
        gate_sets = [(m_slot[0:2], 0), ([kt(R5[:, :], KD), kt(SQE[:, :], KD)], 6),
                     ([kt(BIG1[:, 2048:6144], KD), kt(BIG2[:, 1280:5376], KD)], 8)]
        m_down = [kt(slots[4 + e], 4) for e in range(2)]
        g_down = m_down[0]
        OUT = v2(R5)

        ACC = [ctx.enter_context(nc.psum_tensor(f"ACC{i}", [P, 1024], F32)) for i in range(2)]
        AUX = [ctx.enter_context(nc.psum_tensor(f"AUX{i}", [P, 512], F32)) for i in range(4)]
        SB0, TB, OB = 0, 2, 3

        slot_landed = [sem(f"slot_landed{i}") for i in range(RING)]
        gains_landed = sem("gains_landed")
        small_landed = sem("small_landed")
        x_landed = sem("x_landed")
        mem_landed = sem("mem_landed")
        mem2_landed = sem("mem2_landed")
        consts_ready = sem("consts_ready")
        gains_ready = sem("gains_ready")
        acc_full = [sem(f"acc_full{i}") for i in range(2)]
        acc_free = [sem(f"acc_free{i}") for i in range(2)]
        aux_full = [sem(f"aux_full{i}") for i in range(4)]
        aux_free = [sem(f"aux_free{i}") for i in range(4)]
        squares_ready = sem("squares_ready")
        squares_used = sem("squares_used")
        rows_squared = sem("rows_squared")
        mem_scaled = sem("mem_scaled")
        rows_normed = sem("rows_normed")
        heads_normed = sem("heads_normed")
        latents_normed = sem("latents_normed")
        trig_arg = sem("trig_arg")
        trig_ready = sem("trig_ready")
        roped = sem("roped")
        kb_joined = sem("kb_joined")
        pads_cleared = sem("pads_cleared")
        relu_used = sem("relu_used")
        masked = sem("masked")
        exped = sem("exped")
        normed = sem("normed")
        tanh_ready = sem("tanh_ready")
        merged_ready = sem("merged_ready")
        lambda_dots = sem("lambda_dots")
        lambda_exp = sem("lambda_exp")
        decay_a = sem("decay_a")
        decay_e = sem("decay_e")
        gla_products = sem("gla_products")
        gla_padded = sem("gla_padded")
        mix_ready = sem("mix_ready")
        route_work = sem("route_work")
        route_exp = sem("route_exp")
        route_ready = sem("route_ready")
        rank_ready = sem("rank_ready")
        flag_ready = sem("flag_ready")
        dve_steps = sem("dve_steps")
        act_steps = sem("act_steps")
        pool_steps = sem("pool_steps")
        moe_landed = [sem(f"moe_landed{i}") for i in range(10)]
        moe_picks = sem("moe_picks")
        moe_gathered = sem("moe_gathered")
        moe_rows = sem("moe_rows")
        moe_rows_turned = sem("moe_rows_turned")
        moe_input = sem("moe_input")
        moe_gate = sem("moe_gate")
        moe_up = sem("moe_up")
        moe_tanh = sem("moe_tanh")
        moe_gated = sem("moe_gated")
        moe_hidden = sem("moe_hidden")
        moe_turned = sem("moe_turned")
        moe_picks_turned = sem("moe_picks_turned")
        moe_hidden_t = sem("moe_hidden_t")
        moe_picks_t = sem("moe_picks_t")
        moe_down = sem("moe_down")
        moe_out = [sem(f"moe_out{h}") for h in range(2)]
        moe_summed = sem("moe_summed")
        all_landed = [sem(f"all_landed{i}") for i in range(3)]
        all_rows_turned = sem("all_rows_turned")
        all_input = sem("all_input")
        all_gate = sem("all_gate")
        all_tanh = sem("all_tanh")
        all_gated = sem("all_gated")
        all_hidden = sem("all_hidden")
        all_turned = sem("all_turned")
        all_hidden_t = sem("all_hidden_t")
        all_added = sem("all_added")
        y_done = sem("y_done")
        out_ready = sem("out_ready")
        out_ready2 = sem("out_ready2")
        router_landed = sem("router_landed")
        moe_weighting = sem("moe_weighting")
        stored = sem("stored")

        rows = lambda ap: ap[0].rearrange("(t p) n -> p t n", p=P)

        def cols(w, a, b, k=KD):
            return w.rearrange("(k p) n -> p k n", p=P)[:, 0:k, a:b]

        W1, W2 = A["w_in"][0], A["w_in_2"][0]
        chunks = [
            ("mk", 512, [(0, cols(A["w_mem_kv"][0], 0, 512))]),
            ("mv", 512, [(0, cols(A["w_mem_kv"][0], 512, 1024))]),
            ("cq", 384, [(0, cols(W1, IN_CQ, IN_CQ + 384))]),
            ("small", 360, [(0, cols(W1, IN_KI, IN_KI + 72)), (72, cols(W1, IN_CKV, IN_CKV + 288))]),
            ("qi", 512, [(0, cols(W1, 1536, 2048))]),
            ("uq", 768, [(0, cols(A["w_uq"][0], 0, 768, 3))]),
            ("ukv", 1024, [(0, cols(A["w_ukv"][0], 0, 1024, 2))]),
            ("qa", 512, [(0, cols(W1, 0, 512))]),
            ("ka", 512, [(0, cols(W1, 512, 1024))]),
            ("va", 512, [(0, cols(W1, 1024, 1536))]),
            ("za", 512, [(0, cols(W1, IN_ZA, IN_ZA + 512))]),
            ("zb", 512, [(0, cols(W1, IN_ZB, IN_ZB + 512))]),
            ("qm", 512, [(0, cols(W1, IN_QM, IN_QM + 512))]),
            ("zm", 512, [(0, cols(W1, IN_ZM, IN_ZM + 512))]),
        ]
        for n in range(3):
            for h in range(2):
                chunks.append((f"gate{n}{h}", 512, [(0, cols(W1, IN_GATES + n * D + h * 512, IN_GATES + n * D + h * 512 + 512))]))
            chunks.append((f"wb{n}", 1024, [(0, cols(A["w_branch"][0, n], 0, 1024, 4))]))
        for h in range(2):
            chunks.append((f"wout{h}", 512, [(0, cols(A["w_out"][0], h * 512, h * 512 + 512))]))
        W2c = {"gr": (3072, 3088), "gqk": (1536, 2048), "dq": (0, 512), "dk": (512, 1024), "gv": (2048, 2560),
               "dv": (1024, 1536), "gg": (2560, 3072)}

        def ckv_chunk(i):
            chunks.append((f"ckv{i}", 512, [(0, cols(A["w_ckv_2"][0], i * 512, i * 512 + 512))]))

        def w2_chunk(*names):
            for name in names:
                a, b = W2c[name]
                chunks.append((name, b - a, [(0, cols(W2, a, b))]))

        ckv_chunk(0)
        w2_chunk("gr", "gqk", "dq", "dk", "gv")
        ckv_chunk(1)
        w2_chunk("gg", "dv")
        ckv_chunk(2)
        for h in range(2):
            chunks.append((f"wo{h}", 512, [(0, cols(A["w_o_2"][0], h * 512, h * 512 + 512))]))
        ckv_chunk(3)
        for h in range(2):
            chunks.append((f"wcq{h}", 512, [(0, cols(A["w_cq_2"][0], h * 512, h * 512 + 512))]))
        for h in range(2):
            chunks.append((f"wco{h}", 512, [(0, cols(A["w_co_2"][0], h * 512, h * 512 + 512))]))
        chunk_at = {name: c for c, (name, _, _) in enumerate(chunks)}
        landed_value, seen = [], [0] * RING
        for c, (_, _, parts) in enumerate(chunks):
            seen[c % RING] += 16 * len(parts)
            landed_value.append(seen[c % RING])

        def slot_of(name):
            c = chunk_at[name]
            width = chunks[c][1]
            k = SLOT // width
            return slots[c % RING][:, 0:k * width].rearrange("p (k n) -> p k n", k=k)

        acc_no, aux_no, aux_uses, last_job = {}, {}, [0] * 4, {}

        def wait_full(eng, key):
            if key in acc_no:
                n = acc_no[key]
                eng.wait_ge(acc_full[n % 2], n // 2 + 1)
                return ACC[n % 2]
            b, n = aux_no[key]
            eng.wait_ge(aux_full[b], n + 1)
            return AUX[b]

        def wait_drained(eng, key):
            if key in acc_no:
                n = acc_no[key]
                eng.wait_ge(acc_free[n % 2], n // 2 + 1)
            else:
                b, n = aux_no[key]
                eng.wait_ge(aux_free[b], n + 1)

        def free_sem(key):
            return acc_free[acc_no[key] % 2] if key in acc_no else aux_free[aux_no[key][0]]

        units = {
            "A": [(t, h) for h in range(4) for t in range(TT)],
            "B": [(t, h) for h in range(4) for t in range(TT)],
            "M": [(None, h) for h in range(4)],
            "DA": [(t, h) for h in range(4) for t in range(TT)],
            "C": [(None, h) for h in range(4)],
        }
        scales = {"A": 64 ** -0.5, "B": 96 ** -0.5, "M": 128 ** -0.5, "DA": 64 ** -0.5, "C": 256 ** -0.5}
        first_unit, n_units = {}, 0
        for name in ("A", "B", "M", "DA", "C"):
            first_unit[name] = n_units
            n_units += len(units[name])

        def keys_of(t):
            return P if t == 0 else S

        def buf(T, u):
            return T[:, (u % 2) * 512:(u % 2) * 512 + 512]

        def blocks(u, nk):
            return SME[:, (u % 4) * 512:(u % 4) * 512 + 2 * nk].rearrange("p (i k) -> p i k", i=2)

        jobs = {}
        for t in range(TT):
            jobs["cq", t] = [PJ3[:, t, PJ_CQ + 128 * j:PJ_CQ + 128 * j + 128] for j in range(3)]
            jobs["ckv", t] = [PJ3[:, t, PJ_CKV + 128 * j:PJ_CKV + 128 * j + 128] for j in range(2)]
            jobs["qi", t] = [PJ3[:, t, PJ_QI + 128 * j:PJ_QI + 128 * j + 128] for j in range(4)]
            jobs["ki", t] = [EX[:, t * P:(t + 1) * P]]
            jobs["qa", t] = [PJ3[:, t, PJ_QA + 128 * j:PJ_QA + 128 * j + 128] for j in range(4)]
            jobs["ka", t] = [PJ3[:, t, PJ_KA + 128 * j:PJ_KA + 128 * j + 128] for j in range(4)]
            for g in range(2):
                jobs["qb", t, g] = [QB[:, t, 96 * h:96 * h + 96] for h in range(4 * g, 4 * g + 4)]
                jobs["kb", t, g] = [KB[:, t, h, :] for h in range(4 * g, 4 * g + 4)]
            jobs["qm", t] = [PJ3[:, t, PJ_QM + 128 * j:PJ_QM + 128 * j + 128] for j in range(4)]
            jobs["km", t] = [R1v[:, t, 128 * j:128 * j + 128] for j in range(4)]
            jobs["dq", t] = [DQ[:, t, 128 * j:128 * j + 128] for j in range(4)]
            jobs["dk", t] = [DK[:, t, 128 * j:128 * j + 128] for j in range(4)]
            for g in range(2):
                for name, view in (("mem", R1v), ("x0", ZTv), ("merged", R1v), ("mem2", R3v), ("x1", ZTv),
                                   ("x2", ZTv), ("x3", ZTv), ("xq", v2(R2)), ("xk", R1v)):
                    jobs[name, t, g] = [view[:, t, 512 * g + 128 * j:512 * g + 128 * j + 128] for j in range(4)]
        MIXA = R4[:, 0:1024].rearrange("p (t n) -> p t n", t=TT)
        MIXG = GG
        for t in range(TT):
            jobs["mix", t, 0] = [MIXA[:, t, 128 * j:128 * j + 128] for j in range(4)]
            jobs["mix", t, 1] = [MIXG[:, t, 128 * j:128 * j + 128] for j in range(4)]

        gains = [(GR[r:r + n, :], A[name][0].rearrange("(k p) -> k p", p=P)) for name, r, n in (
            ("g_norm", GC_NORM, 8), ("g_mem", GC_MEM, 8), ("norm_mix_2", GC_MIX, 8), ("norm_cross_2", GC_CROSS, 8),
            ("norm_mem_2", GC_MEM2, 8), ("norm_ffn_2", GC_FFN, 8), ("g_cq", GC_CQ, 3), ("g_ckv", GC_CKV, 2),
            ("gla_gate_b_2", GC_GATEB, 2))]
        small = [(GB[:, c:c + n], A[name][0:1, :].broadcast_to([P, n])) for name, c, n in (
            ("g_qn_a", GB_A, 64), ("g_kn_a", GB_A + 64, 64), ("g_qn_b", GB_B, 96), ("g_kn_b", GB_B + 96, 96),
            ("g_qn_m", GB_M, 128), ("g_kn_m", GB_M + 128, 128), ("da_q_norm_2", GB_DA, 64), ("da_k_norm_2", GB_DA + 64, 64),
            ("da_out_norm_2", GB_DAO, 128), ("gla_out_norm_2", GB_GLAO, 128), ("cross_q_norm_2", GB_X, 256),
            ("cross_k_norm_2", GB_X + 256, 256), ("b_group_2", GB_ROUTE, 4), ("b_expert_2", GB_ROUTE + 4, 32),
            ("lambda_q1_2", GB_LAM, 64), ("lambda_k1_2", GB_LAM + 64, 64), ("lambda_q2_2", GB_LAM + 128, 64),
            ("lambda_k2_2", GB_LAM + 192, 64))]
        small += [(pos_i[:, :], A["positions"][0].rearrange("(t p) -> p t", p=P)), (GW[:, :], A["gla_gate_w_2"][0])]
        small_total = 16 * len(small)
        WG, WU, WD = (A[n][0] for n in ("w_e_gate_2", "w_e_up_2", "w_e_down_2"))

        block = ctx.enter_context(nc.Block())

        @block.tensor
        def _(pe):
            def acc(key):
                n = len(acc_no)
                acc_no[key] = n
                if n >= 2:
                    pe.wait_ge(acc_free[n % 2], n // 2)
                return ACC[n % 2], acc_full[n % 2]

            def aux(b, key):
                n = aux_uses[b]
                aux_uses[b] += 1
                aux_no[key] = (b, n)
                if n:
                    pe.wait_ge(aux_free[b], n)
                return AUX[b], aux_full[b]

            def wait_chunk(name):
                c = chunk_at[name]
                pe.wait_ge(slot_landed[c % RING], landed_value[c])

            def project(name, lhs, k=KD, a=0, width=512, key=None, between=None):
                wait_chunk(name)
                bank, full = acc(key or name)
                w = slot_of(name)
                for t in range(TT):
                    if t and between:
                        between()
                    for i in range(k):
                        mm = nc.tensor.matmul(bank[:, t * 512:t * 512 + width], lhs[:, i, t * P:(t + 1) * P],
                                              w[:, i, a:a + width], start=(i == 0), stop=(i == k - 1))
                mm.then_inc(full, 1)
                last_job[name] = key or name

            def project_t(name, rhs, tiles=4, m=P, between=None):
                wait_chunk(name)
                bank, full = acc(name)
                w = slot_of(name)
                for j in range(tiles):
                    if j == 2 and between:
                        between()
                    for i in range(KD):
                        mm = nc.tensor.matmul(bank[0:m, j * S:(j + 1) * S], w[:, i, j * P:j * P + m],
                                              rhs[:, i, :], start=(i == 0), stop=(i == KD - 1))
                mm.then_inc(full, 1)
                last_job[name] = name

            def project_rows(names, lhs, key, before=lambda t, h: None, by_half=False):
                for t in range(TT):
                    for h in range(2):
                        before(t, h)
                        if by_half:
                            bank, full = acc((key, t, h))
                        elif h == 0:
                            bank, full = acc((key, t))
                        wait_chunk(names[h])
                        w = slot_of(names[h])
                        c = 0 if by_half else h * 512
                        for i in range(KD):
                            mm = nc.tensor.matmul(bank[:, c:c + 512], lhs[:, i, t * P:(t + 1) * P],
                                                  w[:, i, :], start=(i == 0), stop=(i == KD - 1))
                        if by_half or h:
                            mm.then_inc(full, 1)
                for h in range(2):
                    last_job[names[h]] = (key, TT - 1, h) if by_half else (key, TT - 1)

            def turn(b, key):
                bank, full = aux(b, key)
                for j, src in enumerate(jobs[key]):
                    mm = nc.tensor.transpose(bank[0:src.shape[1], j * P:(j + 1) * P], src, ident[:, :])
                mm.then_inc(full, 1)

            def turn_rows(name, n, tiles=range(TT), spread=2):
                for t in tiles:
                    pe.wait_ge(rows_normed, 2 * n + t + 1)
                    for g in range(2):
                        turn(spread * t + g, (name, t, g))

            def wait_turned(name, tiles=range(TT)):
                for t in tiles:
                    for g in range(2):
                        wait_drained(pe, (name, t, g))

            def attend(name, a=0, b=None):
                score, value, dims = branches[name]
                U = len(units[name])
                for s in range(a, U + 3 if b is None else b):
                    if s < U:
                        u = first_unit[name] + s
                        t, h = units[name][s]
                        nk = keys_of(t)
                        bank, full = aux(SB0 + u % 2, ("S", u))
                        for i in range(2):
                            mm = score(bank[:, i * nk:(i + 1) * nk], t, h, i, nk)
                        mm.then_inc(full, 1)
                    if 2 <= s < U + 2:
                        u = first_unit[name] + s - 2
                        t, h = units[name][s - 2]
                        nk = keys_of(t)
                        pe.wait_ge(normed, u + 1)
                        bank, full = aux(TB, ("T", u))
                        e = blocks(u, nk)
                        heads = 1 if name == "DA" else 2
                        for j in range(nk // P):
                            for i in range(heads):
                                mm = nc.tensor.transpose(bank[:, (j * heads + i) * P:(j * heads + i + 1) * P],
                                                         e[:, i, j * P:(j + 1) * P], ident[:, :])
                        mm.then_inc(full, 1)
                    if s >= 3:
                        u = first_unit[name] + s - 3
                        t, h = units[name][s - 3]
                        nk = keys_of(t)
                        wait_drained(pe, ("T", u))
                        bank, full = aux(OB, ("O", u))
                        p = buf(PT, u)
                        for d in range(dims):
                            for j in range(nk // P):
                                first, last = j == 0, j == nk // P - 1
                                if name == "DA":
                                    mm = nc.tensor.matmul(bank[:, 0:P], p[:, j * P:(j + 1) * P], value(j, h, d),
                                                          start=first, stop=last)
                                elif name in ("A", "B"):
                                    for i in range(2):
                                        mm = nc.tensor.matmul(bank[64 * i:64 * i + 64, i * P:(i + 1) * P],
                                                              value(j, h, d)[:, 64 * i:64 * i + 64],
                                                              p[:, j * 256 + i * P:j * 256 + (i + 1) * P],
                                                              start=first, stop=last)
                                else:
                                    mm = nc.tensor.matmul(bank[:, d * 256:(d + 1) * 256], value(j, h, d),
                                                          p[:, j * 256:(j + 1) * 256], start=first, stop=last)
                        mm.then_inc(full, 1)

            def plain_score(queries, keys):
                return lambda o, t, h, i, nk: nc.tensor.matmul(o, queries(t, h, i), keys(h, i, nk), start=True, stop=True)

            def cross_score(o, t, h, i, nk):
                nc.tensor.matmul(o, CQ8[:, 2 * h, i * P:(i + 1) * P], CK8[:, 2 * h, :], start=True, stop=False)
                return nc.tensor.matmul(o, CQ8[:, 2 * h + 1, i * P:(i + 1) * P], CK8[:, 2 * h + 1, :],
                                        start=False, stop=True)

            padded_score = plain_score(lambda t, h, i: QPAD[:, 2 * h + i, t * P:(t + 1) * P],
                                       lambda h, i, nk: KT4[:, h, 0:nk])
            branches = {
                "A": (padded_score, lambda j, h, d: PJ3[:, j, PJ_VA + P * h:PJ_VA + P * h + P], 1),
                "B": (plain_score(lambda t, h, i: QBT[0:96, 2 * h + i, t * P:(t + 1) * P],
                                  lambda h, i, nk: KBT[0:96, 2 * h + i, 0:nk]),
                      lambda j, h, d: R3[:, 1024 + 512 * j + P * h:1024 + 512 * j + P * h + P], 1),
                "M": (plain_score(lambda t, h, i: QMT[:, h, i * P:(i + 1) * P], lambda h, i, nk: KMT[:, h, :]),
                      lambda j, h, d: VM[:, j, P * h:P * h + P], 1),
                "DA": (padded_score, lambda j, h, d: DV[:, j, P * h:P * h + P], 1),
                "C": (cross_score, lambda j, h, d: R3v[:, j, 256 * h + P * d:256 * h + P * d + P], 2),
            }

            pe.wait_ge(consts_ready, 1)
            pe.wait_ge(mem_landed, 16)
            for t, g in ((0, 0), (0, 1), (1, 0)):
                turn(2 * t + g, ("mem", t, g))
            pe.wait_ge(gains_landed, 16 * len(gains))
            bank, full = aux(3, "gains")
            nc.tensor.transpose(bank[:, 0:GC_N], GR[:, :], ident[0:GC_N, 0:GC_N]).then_inc(full, 1)
            turn(3, ("mem", 1, 1))
            wait_turned("mem")
            project("mk", R2T)
            turn_rows("x0", 0)
            project("mv", R2T)
            wait_turned("x0")
            project("cq", XT3, width=384)
            project("small", XT3, width=360)
            project("qi", XT3)
            for t in range(TT):
                pe.wait_ge(latents_normed, 1)
                turn(t, ("cq", t))
                turn(2 + t, ("ckv", t))
            for t in range(TT):
                wait_drained(pe, ("cq", t))
                wait_drained(pe, ("ckv", t))
            project("uq", CQT, k=3, a=0, width=512, key="uq0")
            project("uq", CQT, k=3, a=512, width=256, key="uq1")
            project("ukv", CKVT, k=2, a=0, width=512, key="ukv0")
            project("ukv", CKVT, k=2, a=512, width=512, key="ukv1")
            pe.wait_ge(roped, 1)
            for t in range(TT):
                turn(t, ("qi", t))
                turn(2 + t, ("ki", t))
            project("qa", XT3)
            for t in range(TT):
                wait_drained(pe, ("qi", t))
                wait_drained(pe, ("ki", t))
            for n in range(8):
                t, h = n // 4, n % 4
                nk = keys_of(t)
                bank, full = aux(n % 4, ("dots", n))
                for i in range(2):
                    mm = nc.tensor.matmul(bank[:, i * nk:(i + 1) * nk], QPAD[:, 2 * h + i, t * P:(t + 1) * P],
                                          KIT[:, 0:nk], start=True, stop=True)
                mm.then_inc(full, 1)
            project("ka", XT3)
            project("va", XT3)
            project_t("za", XT3)
            pe.wait_ge(roped, 3)
            for t in range(TT):
                turn(t, ("qa", t))
                turn(2 + t, ("ka", t))
            def start_a():
                for t in range(TT):
                    wait_drained(pe, ("qa", t))
                    wait_drained(pe, ("ka", t))
                attend("A", 0, 2)

            project_t("zb", XT3, between=start_a)
            wait_drained(pe, "va")
            attend("A", 2, 8)
            project("qm", XT3)
            attend("A", 8)
            pe.wait_ge(roped, 2)
            for t in range(TT):
                for g in range(2):
                    turn(g, ("qb", t, g))
                    turn(2 + g, ("kb", t, g))

            def start_b():
                for t in range(TT):
                    for g in range(2):
                        wait_drained(pe, ("qb", t, g))
                        wait_drained(pe, ("kb", t, g))
                attend("B", 0, 2)

            project_t("zm", XT3, between=start_b)
            attend("B", 2, 8)

            def end_b():
                attend("B", 8)
                pe.wait_ge(heads_normed, 5)
                for t in range(TT):
                    turn(t, ("qm", t))
                    turn(2 + t, ("km", t))

            project("gate00", XT3, between=end_b)
            for t in range(TT):
                wait_drained(pe, ("qm", t))
                wait_drained(pe, ("km", t))
            wait_drained(pe, "mv")
            attend("M", 0, 2)
            project("gate01", XT3)
            attend("M", 2, 4)
            wait_drained(pe, ("O", first_unit["A"] + 7))
            for h in range(2):
                project("wb0", YT[:, 0:4, :], k=4, a=512 * h, key=f"wb0{h}")
                if h == 0:
                    attend("M", 4)
            for n in (1, 2):
                project(f"gate{n}0", XT3)
                project(f"gate{n}1", XT3)
                wait_drained(pe, ("O", first_unit["ABM"[n]] + len(units["ABM"[n]]) - 1))
                for h in range(2):
                    project(f"wb{n}", YT[:, 4 * n:4 * n + 4, :], k=4, a=512 * h, key=f"wb{n}{h}")
            for t in range(TT):
                for g in range(2):
                    pe.wait_ge(merged_ready, g + 1)
                    turn(2 * t + g, ("merged", t, g))
            wait_turned("merged")
            project("wout0", XT3)
            turn_rows("mem2", 1)
            project("wout1", XT3)
            wait_turned("mem2")
            project("ckv0", R2T)
            turn_rows("x1", 2)
            wait_turned("x1")
            project_t("gr", XT3, tiles=1, m=16)
            project_t("gqk", XT3)
            wait_drained(pe, "gr")
            bank, full = acc("gate_z")
            for h in range(2):
                mm = nc.tensor.matmul(bank[:, h * S:(h + 1) * S], GW[:, h * P:(h + 1) * P], GRT[:, :],
                                      start=True, stop=True)
            mm.then_inc(full, 1)
            project("dq", XT3)
            project("dk", XT3)
            project("gv", XT3)
            project("ckv1", R2T)
            pe.wait_ge(heads_normed, 6)
            for t in range(TT):
                turn(t, ("dq", t))
                turn(2 + t, ("dk", t))
            pe.wait_ge(gla_products, 1)
            pe.wait_ge(gla_padded, 1)
            for t in range(TT):
                bank, full = acc(("intra", t))
                for h in range(4):
                    nc.tensor.matmul(bank[:, h * P:(h + 1) * P], KNZ[:, h, t * P:(t + 1) * P],
                                     QP[:, h // 2, t * P:(t + 1) * P], start=True, stop=True)
                for h in range(4):
                    mm = nc.tensor.matmul(bank[:, 512 + h * P:512 + (h + 1) * P], KPZ[:, h, t * P:(t + 1) * P],
                                          QN[:, h // 2, t * P:(t + 1) * P], start=True, stop=True)
                mm.then_inc(full, 1)
            bank, full = aux(3, "kend")
            for t in range(TT):
                for h in range(2):
                    mm = nc.tensor.transpose(bank[:, (2 * t + h) * P:(2 * t + h + 1) * P], KE[:, h, t * P:(t + 1) * P],
                                             ident[:, :])
            mm.then_inc(full, 1)
            project("gg", XT3)
            wait_drained(pe, "kend")
            wait_drained(pe, "gv")
            for c in range(3):
                bank, full = aux(c, ("state", c))
                for h in range(2):
                    mm = nc.tensor.matmul(bank[:, h * 256:(h + 1) * 256], KEN[:, c % 2, 2 * (c // 2) + h, :],
                                          GV[:, c // 2, h * 256:(h + 1) * 256], start=True, stop=True)
                mm.then_inc(full, 1)
            project("dv", XT3)
            wait_drained(pe, ("intra", 1))
            wait_drained(pe, ("state", 2))
            for t in range(TT):
                bank, full = aux(3, ("gla", t))
                for h in range(4):
                    o = bank[:, h * P:(h + 1) * P]
                    nc.tensor.matmul(o, ATT[:, t, h, :], GV[:, t, h * P:(h + 1) * P], start=True, stop=False,
                                     skip_group_check=True)
                    for c in range(2):
                        if 2 * t + c:
                            mm = nc.tensor.matmul(bank[64 * c:64 * c + 64, h * P:(h + 1) * P],
                                                  QLZ[:, h, t * P + 64 * c:t * P + 64 * c + 64],
                                                  ST[:, 2 * t + c - 1, h // 2, :], start=False, stop=(c == 1),
                                                  skip_group_check=True)
                mm.then_inc(full, 1)
            for t in range(TT):
                wait_drained(pe, ("dq", t))
                wait_drained(pe, ("dk", t))
            wait_drained(pe, "dv")
            attend("DA", 0, 2)
            project("ckv2", R2T)
            attend("DA", 2, 8)

            def end_da():
                attend("DA", 8)
                pe.wait_ge(mix_ready, 1)
                for t in range(TT):
                    turn(2 * t + 1, ("mix", t, 1))

            project("ckv3", R2T, between=end_da)
            pe.wait_ge(heads_normed, 8)
            for t in range(TT):
                turn(2 * t, ("mix", t, 0))
            wait_turned("mix")
            def during_wo(t, h):
                if (t, h) == (1, 1):
                    turn_rows("x2", 3, [0])

            project_rows(("wo0", "wo1"), XT3, "wo", during_wo)
            wait_turned("x2", [0])

            def during_wcq(t, h):
                if (t, h) == (0, 1):
                    turn_rows("x2", 3, [1])
                elif (t, h) == (1, 0):
                    wait_turned("x2", [1])
                elif (t, h) == (1, 1):
                    turn_queries(0)

            def turn_queries(t):
                for g in range(2):
                    pe.wait_ge(heads_normed, 10 + 2 * t + g)
                    turn(2 * t + g, ("xq", t, g))

            project_rows(("wcq0", "wcq1"), XT3, "wcq", during_wcq, by_half=True)
            pe.wait_ge(heads_normed, 9)
            for t in range(TT):
                for g in range(2):
                    turn(2 * t + g, ("xk", t, g))
            turn_queries(1)
            wait_turned("xq")
            wait_turned("xk")
            attend("C", 0, 4)
            for t in range(TT):
                bank, full = acc(("wco", t))
                for head in range(4):
                    if t == 0:
                        if head < 3:
                            attend("C", 4 + head, 5 + head)
                        wait_drained(pe, ("O", first_unit["C"] + head))
                    elif head == 2:
                        turn_rows("x3", 4, [0])
                    for h in range(2):
                        wait_chunk(f"wco{h}")
                        for i in (2 * head, 2 * head + 1):
                            mm = nc.tensor.matmul(bank[:, h * 512:(h + 1) * 512], XT3[:, i, t * P:(t + 1) * P],
                                                  slot_of(f"wco{h}")[:, i, :], start=(i == 0), stop=(i == KD - 1),
                                                  skip_group_check=True)
                mm.then_inc(full, 1)
            for h in range(2):
                last_job[f"wco{h}"] = ("wco", 1)
            pe.wait_ge(router_landed, 32)
            bank, full = aux(2, "router")
            WR3 = WR[:, :].rearrange("p (k n) -> p k n", k=KD)
            def start_sum(t):
                wait_drained(pe, ("wco", t))
                for h in range(2):
                    mm = nc.tensor.matmul(ACC[t][:, h * 512:(h + 1) * 512], ident[:, :], X3[:, t, h * 512:(h + 1) * 512],
                                          start=True, stop=False, skip_group_check=True)
                return mm

            for t in range(TT):
                if t:
                    start_sum(0)
                    turn_rows("x3", 4, [1], spread=0)
                wait_turned("x3", [t])
                for i in range(KD):
                    mm = nc.tensor.matmul(bank[:, 36 * t:36 * t + 36], XT3[:, i, t * P:(t + 1) * P], WR3[:, i, :],
                                          start=(i == 0), stop=(i == KD - 1))
            mm.then_inc(full, 1)
            start_sum(1).then_inc(moe_picks_turned, 1)
            pe.wait_ge(route_ready, 1)
            bank, full = aux(1, "ranks")
            nc.tensor.matmul(bank[:, 0:32], before[:, :], R_sel[:, 0, :], start=True, stop=True)
            nc.tensor.matmul(bank[:, 32:64], before[:, :], R_sel[:, 1, :], start=True, stop=False)
            nc.tensor.matmul(bank[:, 32:64], ones[:, :], R_sel[:, 0, :], start=False, stop=True)
            nc.tensor.matmul(bank[:, 64:96], ones[:, :], R_sel[:, 0, :], start=True, stop=False)
            nc.tensor.matmul(bank[:, 64:96], ones[:, :], R_sel[:, 1, :], start=False, stop=True).then_inc(full, 1)

            def gather():
                for h in range(2):
                    for t in range(TT):
                        mm = nc.tensor.matmul(AUX[h][:, :], M_pick[:, t, :], ZTv[:, t, h * 512:(h + 1) * 512],
                                              start=(t == 0), stop=(t == TT - 1))
                mm.then_inc(moe_gathered, 1)

            def turn_input(tiles):
                for j in tiles:
                    mm = nc.tensor.transpose(AUX[j // 4][:, (j % 4) * P:(j % 4 + 1) * P], M_rows[:, j * P:(j + 1) * P],
                                             ident[:, :])
                if KD - 1 in tiles:
                    mm.then_inc(moe_rows_turned, 1)

            pe.wait_ge(moe_picks, 1)
            wait_drained(pe, "router")
            wait_drained(pe, "ranks")
            gather()
            pe.wait_ge(moe_rows, 1)
            turn_input(range(KD))
            def expert_pair(turn_, after, loads, last=False):
                gate_slot, gate_landed = gate_sets[turn_]
                pe.wait_ge(moe_input, after(1))
                for e in range(2):
                    pe.wait_ge(moe_landed[gate_landed + e], loads)
                for k in range(KD):
                    for e in range(2):
                        mm = nc.tensor.matmul(AUX[2][64 * e:64 * e + 64, :], M_xt[:, k, 64 * e:64 * e + 64],
                                              gate_slot[e][:, k, :], start=(k == 0), stop=(k == KD - 1))
                mm.then_inc(moe_gate, 1)
                for e in range(2):
                    pe.wait_ge(moe_landed[2 + e], after(0) * 16 + 16)
                for k in range(KD):
                    for e in range(2):
                        mm = nc.tensor.matmul(AUX[3][64 * e:64 * e + 64, :], M_xt[:, k, 64 * e:64 * e + 64],
                                              m_slot[2 + e][:, k, :], start=(k == 0), stop=(k == KD - 1))
                mm.then_inc(moe_up, 1)
                if not last:
                    pe.wait_ge(moe_picks, after(2))
                    gather()
                pe.wait_ge(moe_hidden, after(1))
                for j in range(4):
                    mm = nc.tensor.transpose(AUX[2][:, j * P:(j + 1) * P], M_hid[:, j * P:(j + 1) * P], ident[:, :])
                mm.then_inc(moe_turned, 1)
                for t in range(TT):
                    mm = nc.tensor.transpose(AUX[3][:, t * P:(t + 1) * P], M_gpick[:, t, :], ident[:, :])
                mm.then_inc(moe_picks_turned, 1)
                if not last:
                    pe.wait_ge(moe_rows, after(2))
                    turn_input(range(4))
                pe.wait_ge(moe_hidden_t, after(1))
                pe.wait_ge(moe_picks_t, after(1))
                for e in range(2):
                    pe.wait_ge(moe_landed[4 + e], after(0) * 16 + 16)
                for k in range(4):
                    for h in range(2):
                        for e in range(2):
                            mm = nc.tensor.matmul(AUX[2 + h][64 * e:64 * e + 64, :], M_hidt[:, k, 64 * e:64 * e + 64],
                                                  m_down[e][:, k, h * 512:(h + 1) * 512], start=(k == 0), stop=(k == 3))
                mm.then_inc(moe_down, 1)
                if not last:
                    turn_input(range(4, KD))
                for h in range(2):
                    pe.wait_ge(moe_out[h], after(1))
                    for t in range(TT):
                        mm = nc.tensor.matmul(ACC[t][:, h * 512:(h + 1) * 512], M_place[:, t * P:(t + 1) * P],
                                              M_o[:, h * 512:(h + 1) * 512], start=False, stop=False,
                                              skip_group_check=True)
                mm.then_inc(moe_summed, 1)

            with pe.Fori(0, (PAIRS - 1) // 3) as i:
                for third in range(3):
                    expert_pair(third, lambda k: i * 3 + (third + k), i * 16 + 16)
            expert_pair(0, lambda k: PAIRS - 1 + k, 16 * ((PAIRS - 1) // 3 + 1), last=True)
            pe.wait_ge(flag_ready, 1)
            fullest = pe.value_load(FLAG[0:1, 0:1])
            with pe.If(fullest > CAP):
                pe.wait_ge(moe_input, PAIRS)
                for h in range(2):
                    pe.wait_ge(moe_out[h], PAIRS)
                for t in range(TT):
                    for g in range(2):
                        for j, src in enumerate(jobs["x3", t, g]):
                            mm = nc.tensor.transpose(AUX[2 * t + g][:, j * P:(j + 1) * P], src, ident[:, :])
                mm.then_inc(all_rows_turned, 1)
                pe.wait_ge(all_input, 1)
                with pe.Fori(0, N_EXPERTS) as e:
                    for s in range(3):
                        pe.wait_ge(all_landed[s], e * 16 + 16)
                    for t in range(TT):
                        for k in range(KD):
                            nc.tensor.matmul(AUX[0][:, :], XT3[:, k, t * P:(t + 1) * P], m_slot[0][:, k, :],
                                             start=(k == 0), stop=(k == KD - 1))
                        for k in range(KD):
                            mm = nc.tensor.matmul(AUX[1][:, :], XT3[:, k, t * P:(t + 1) * P], m_slot[1][:, k, :],
                                                  start=(k == 0), stop=(k == KD - 1))
                        mm.then_inc(all_gate, 1)
                        pe.wait_ge(all_hidden, e * 2 + t + 1)
                        for j in range(4):
                            mm = nc.tensor.transpose(AUX[2][:, j * P:(j + 1) * P], M_hid[:, j * P:(j + 1) * P], ident[:, :])
                        mm.then_inc(all_turned, 1)
                        pe.wait_ge(all_hidden_t, e * 2 + t + 1)
                        for k in range(4):
                            for h in range(2):
                                mm = nc.tensor.matmul(ACC[t][:, h * 512:(h + 1) * 512], M_hidt[:, k, :],
                                                      g_down[:, k, h * 512:(h + 1) * 512], start=False, stop=False,
                                                      skip_group_check=True)
                        mm.then_inc(all_added, 1)
            for t in range(TT):
                for h in range(2):
                    mm = nc.tensor.matmul(ACC[t][:, h * 512:(h + 1) * 512], zeros[:, 0:64].bitcast(BF16),
                                          causal[:, :].bitcast(BF16), start=False, stop=True, skip_group_check=True)
            mm.then_inc(y_done, 1)

        @block.sync
        def _(sp):
            sp.dma_start(R1v, rows(A["mem"])).then_inc(mem_landed, 16)
            for dst, src in gains:
                sp.dma_start(dst, src).then_inc(gains_landed, 16)
            for c, (name, width, parts) in enumerate(chunks):
                if c >= RING:
                    wait_full(sp, last_job[chunks[c - RING][0]])
                for first, src in parts:
                    k, n = src.shape[1], src.shape[2]
                    dst = slot_of(name)[:, 0:k, first:first + n]
                    sp.dma_start(dst, src).then_inc(slot_landed[c % RING], 16)
                if c == 0:
                    sp.dma_start(X3, rows(A["x"])).then_inc(x_landed, 16)
                if c == RING - 1:
                    for dst, src in small:
                        sp.dma_start(dst, src, allow_slow_non_contiguous=dst.dtype == I32).then_inc(small_landed, 16)
                if name == "wout0":
                    wait_full(sp, ("merged", 1, 1))
                    wait_full(sp, ("merged", 1, 0))
                    sp.dma_start(R1v, rows(A["mem_2"])).then_inc(mem2_landed, 16)

            def expert_parts(s, e):
                w = (WG, WG, WU, WU, WD, WD)[s]
                return w[bass.ds(e, 1), :, :].rearrange("e (k p) n -> p (e k) n", p=P)

            dsts = [m_slot[0], m_slot[1], m_slot[2], m_slot[3], m_down[0], m_down[1]]
            order = sorted(range(4), key=lambda s: max(c for c in range(len(chunks)) if c % RING == s))
            wait_full(sp, ("mix", 1, 1))
            wait_full(sp, ("mix", 1, 0))
            for name, a, b in (("w_group_2", 0, 4), ("w_expert_2", 4, 36)):
                sp.dma_start(kt(WR, KD)[:, :, a:b], A[name][0].rearrange("(k p) n -> p k n", p=P)).then_inc(router_landed, 16)
            for s in (4, 5):
                sp.dma_start(dsts[s], WD[s - 4].rearrange("(k p) n -> p k n", p=P)).then_inc(moe_landed[s], 16)

            def first_gates(pair):
                for j in range(2):
                    dst, landed = gate_sets[pair]
                    sp.dma_start(dst[j], WG[2 * pair + j].rearrange("(k p) n -> p k n", p=P)).then_inc(
                        moe_landed[landed + j], 16)

            for n, s in enumerate(order):
                if n == 2:
                    wait_full(sp, ("S", first_unit["C"] + 3))
                    wait_full(sp, ("T", first_unit["C"] + 3))
                    first_gates(1)
                c = max(c for c in range(len(chunks)) if c % RING == s)
                wait_full(sp, last_job[chunks[c][0]])
                w = (WG, WG, WU, WU)[s]
                sp.dma_start(dsts[s], w[s % 2].rearrange("(k p) n -> p k n", p=P)).then_inc(moe_landed[s], 16)

            def next_weights(group, e, used, value, dst, landed):
                src = [expert_parts(2 * group + j, e + j) for j in range(2)]
                sp.wait_ge(used, value)
                for j in range(2):
                    sp.dma_start(dst[j], src[j]).then_inc(moe_landed[landed + j], 16)

            sp.wait_ge(moe_picks_turned, 1)
            first_gates(2)

            def refill(done, e):
                next_weights(1, e, moe_up, done, m_slot[2:4], 2)
                next_weights(2, e, moe_down, done, m_down, 4)

            looped = 3
            with sp.Fori(0, looped) as i:
                for third in range(3):
                    done = i * 3 + (third + 1)
                    refill(done, i * 6 + (2 * third + 2))
                    next_weights(0, i * 6 + (2 * third + 6), moe_gate, done, *gate_sets[third])
            for done in range(3 * looped + 1, PAIRS):
                refill(done, 2 * done)
                pair = done + 1
                if 3 * looped + 3 <= pair < PAIRS:
                    next_weights(0, 2 * pair, moe_gate, pair - 2, *gate_sets[pair % 3])
            sp.wait_ge(flag_ready, 1)
            fullest = sp.value_load(FLAG[0:1, 0:1])
            with sp.If(fullest > CAP):
                sp.wait_ge(moe_down, PAIRS)
                for w, dst, landed in ((WG, m_slot[0], 0), (WU, m_slot[1], 1), (WD, g_down, 2)):
                    sp.dma_start(dst, w[0].rearrange("(k p) n -> p k n", p=P)).then_inc(all_landed[landed], 16)
                with sp.Fori(1, N_EXPERTS) as e:
                    srcs = [w[bass.ds(e, 1), :, :].rearrange("e (k p) n -> p (e k) n", p=P) for w in (WG, WU, WD)]
                    sp.wait_ge(all_gate, e * 2)
                    sp.dma_start(m_slot[0], srcs[0]).then_inc(all_landed[0], 16)
                    sp.dma_start(m_slot[1], srcs[1]).then_inc(all_landed[1], 16)
                    sp.wait_ge(all_added, e * 2)
                    sp.dma_start(g_down, srcs[2]).then_inc(all_landed[2], 16)
            for t in range(TT):
                sp.wait_ge((out_ready, out_ready2)[t], 1)
                sp.dma_start(out[0, t * P:(t + 1) * P, :], OUT[:, t, :]).then_inc(stored, 16)
            sp.wait_ge(stored, 16 * TT)

        @block.gpsimd
        def _(pool):
            steps = [0]

            def link(ins):
                steps[0] += 1
                ins.then_inc(pool_steps, 1)
                pool.wait_ge(pool_steps, steps[0])

            g = nc.gpsimd
            g.memset(ident[:, :], 0.0)
            g.memset(causal[:, :], 0.0)
            g.memset(past[:, :], 1.0)
            g.memset(future[:, :], 1.0)
            g.memset(before[:, :], 1.0)
            g.memset(ones[:, :], 1.0)
            g.memset(zeros[:, :], 0.0)
            for j in range(16):
                g.memset(freq[:, j:j + 1], float(np.float32(THETA) ** np.float32(-j / 16)))
            link(g.iota(iota_i[:, :], pattern=[[1, CAP]], base=0, channel_multiplier=0))
            g.tensor_copy(iota[:, :], iota_i[:, :])
            g.affine_select(out=ident[:, :], in_=ident[:, :], compare_op=ALU.not_equal, fill=1.0, base=0,
                            pattern=[[-1, P]], channel_multiplier=1)
            g.affine_select(out=causal[:, 128:256], in_=causal[:, 128:256], compare_op=ALU.is_ge, fill=NEG, base=0,
                            pattern=[[-1, P]], channel_multiplier=1)
            g.affine_select(out=past[:, :], in_=past[:, :], compare_op=ALU.is_ge, fill=0.0, base=0,
                            pattern=[[1, P]], channel_multiplier=-1)
            g.affine_select(out=future[:, :], in_=future[:, :], compare_op=ALU.is_gt, fill=0.0, base=0,
                            pattern=[[-1, P]], channel_multiplier=1)
            link(g.affine_select(out=before[:, :], in_=before[:, :], compare_op=ALU.is_gt, fill=0.0, base=0,
                                 pattern=[[1, P]], channel_multiplier=-1))
            link(g.memset(past[0:64, 64:128], 0.0))
            link(g.memset(future[64:128, 0:64], 0.0))
            g.tensor_scalar(pref[:, 0:8], iota[:, 0:8], -1.0, 8.0, ALU.mult, ALU.add)
            g.tensor_scalar(pref[:, 8:12], iota[:, 0:4], -1.0, 4.0, ALU.mult, ALU.add).then_inc(consts_ready, 1)
            g.memset(QPAD, 0.0).then_inc(pads_cleared, 1)

            def rope(view, t, off, half, step, groups):
                x = view[:, :, off:off + 2 * half].rearrange("p g (a d) -> p g a d", a=2)
                tab = [trig[:, c + 16 * t:c + 16 * t + 16].rearrange("p (d s) -> p d s", s=step)[:, :, 0]
                       .unsqueeze(1).unsqueeze(1).broadcast_to([P, groups, 2, half]) for c in (160, 128)]
                n = groups * 2 * half
                xc, xs = (ROT[:, i * 256:i * 256 + n].rearrange("p (g a d) -> p g a d", g=groups, a=2) for i in range(2))
                g.tensor_tensor(xc, x, tab[0], ALU.mult)
                link(g.tensor_tensor(xs, x, tab[1], ALU.mult))
                g.tensor_tensor(x[:, :, 0, :], xc[:, :, 0, :], xs[:, :, 1, :], ALU.subtract)
                link(g.tensor_tensor(x[:, :, 1, :], xc[:, :, 1, :], xs[:, :, 0, :], ALU.add))

            def heads(T3, t, a, n, w):
                return T3[:, t, a:a + n * w].rearrange("p (h d) -> p h d", h=n)

            pool.wait_ge(trig_ready, 1)
            wait_drained(pool, "small")
            wait_drained(pool, "qi")
            for t in range(TT):
                rope(heads(PJ3, t, PJ_QI, 9, 64), t, 0, 8, 2, 9)
            for t in range(TT):
                for i in range(2):
                    last = g.tensor_copy(EX[:, t * P + 64 * i:t * P + 64 * i + 64], PJ3[:, t, PJ_KI:PJ_KI + 64])
            last.then_inc(roped, 1)
            wait_drained(pool, "ukv0")
            wait_drained(pool, "ukv1")
            for t in range(TT):
                g.tensor_copy(KB[:, t, :, 0:64], KNB[:, t, :, :])
                last = g.tensor_copy(KB[:, t, :, 64:96],
                                     PJ3[:, t, PJ_KR:PJ_KR + 32].unsqueeze(1).broadcast_to([P, 8, 32]))
            last.then_inc(kb_joined, 1)
            pool.wait_ge(heads_normed, 3)
            for t in range(TT):
                rope(heads(QB, t, 0, 8, 96), t, 64, 16, 1, 8)
                rope(KB[:, t, :, :], t, 64, 16, 1, 8)
            g.memset(SMALL[:, 72:73], 0.0).then_inc(roped, 1)
            pool.wait_ge(heads_normed, 4)
            for t in range(TT):
                rope(heads(PJ3, t, PJ_QA, 16, 64), t, 0, 8, 2, 16)
            g.memset(SMALL[:, 73:74], 0.0).then_inc(roped, 1)
            for k in range(2):
                wait_full(pool, ("O", first_unit["M"] + 2 + k))
            g.memset(QPAD, 0.0).then_inc(pads_cleared, 1)
            g.memset(ATT, 0.0)
            link(g.memset(causal[:, 128:256], 0.0))
            g.memset(causal[0:64, 192:256], NEG).then_inc(pads_cleared, 1)
            wait_full(pool, ("x1", 1, 1))
            wait_full(pool, ("x1", 1, 0))
            g.memset(ZT[:, :], 0.0).then_inc(pads_cleared, 1)
            g.memset(KEN, 0.0).then_inc(pads_cleared, 1)
            pool.wait_ge(decay_e, 1)
            g.tensor_tensor(QP, kt(GQ, 2), kt(EP, 2), ALU.mult)
            g.tensor_tensor(QN, kt(GQ, 2), kt(EN, 2), ALU.mult)
            g.tensor_tensor(KE, kt(GK, 2), kt(EE, 2), ALU.mult).then_inc(gla_products, 1)

        @block.scalar
        def _(act):
            a_ = nc.scalar
            steps = [0]

            def link(ins):
                steps[0] += 1
                ins.then_inc(act_steps, 1)
                act.wait_ge(act_steps, steps[0])

            def square_rows(n, src, junk, ready, tiles=range(TT)):
                for r in ready:
                    wait_drained(act, r) if r in acc_no else act.wait_ge(*r)
                for t in tiles:
                    last = a_.activation(junk[:, t, :], src[:, t, :], ACT.Square, scale=D ** -0.5,
                                         accum_out=SMALL[:, 64 + t:65 + t])
                last.then_inc(rows_squared, 1)

            sq_calls = [0]

            def square_heads(src, dst, w):
                if sq_calls[0]:
                    act.wait_ge(squares_used, sq_calls[0])
                sq_calls[0] += 1
                a_.activation(dst, src, ACT.Square, scale=w ** -0.5).then_inc(squares_ready, 1)

            def drain(key, pairs):
                bank = wait_full(act, key)
                for dst, src in pairs:
                    last = a_.activation(dst, src(bank), ACT.Copy)
                last.then_inc(free_sem(key), 1)

            def by_token(T3, c, width=512):
                return [(T3[:, t, c:c + width], lambda b, t=t: b[:, t * 512:t * 512 + width]) for t in range(TT)]

            def drain_turned(key, dst, n, rows_=P):
                t = key[1]
                drain(key, [(dst[0:rows_, :, t * P:(t + 1) * P],
                             lambda b: b[0:rows_, 0:n * P].rearrange("p (k q) -> p k q", k=n))])

            def drain_padded(key, dst):
                t = key[1]
                view = dst.rearrange("p (h i) q -> p h i q", i=2)
                drain(key, [(view[64 * i:64 * i + 64, :, i, t * P:(t + 1) * P],
                             lambda b, i=i: b[64 * i:64 * i + 64, :].rearrange("p (k q) -> p k q", k=4)) for i in range(2)])

            def soften(name, a=0, b=None):
                U = len(units[name])
                for s in range(a, U + 2 if b is None else b):
                    if s < U:
                        u = first_unit[name] + s
                        nk = keys_of(units[name][s][0])
                        act.wait_ge(masked, u + 1)
                        e = blocks(u, nk)
                        for i in range(2):
                            last = a_.activation(e[:, i, :], e[:, i, :], ACT.Exp, bias=stat(u, 0)[:, i:i + 1],
                                                 accum_out=stat(u, 1)[:, i:i + 1])
                        last.then_inc(exped, 1)
                    if s >= 2:
                        u = first_unit[name] + s - 2
                        nk = keys_of(units[name][s - 2][0])
                        n = nk if name == "DA" else 2 * nk
                        bank = wait_full(act, ("T", u))
                        if u >= 2:
                            wait_full(act, ("O", u - 2))
                        a_.activation(buf(PT, u)[:, 0:n], bank[:, 0:n], ACT.Copy).then_inc(free_sem(("T", u)), 1)

            act.wait_ge(consts_ready, 1)
            square_rows(0, R1v, R3v, [(mem_landed, 16)])
            act.wait_ge(mem_scaled, 1)
            square_rows(1, X3, ZTv, [(x_landed, 16)])
            act.wait_ge(trig_arg, 2)
            a_.activation(trig[:, 128:192], trig[:, 64:128], ACT.Sin).then_inc(trig_ready, 1)
            def drain_mem(key, c):
                bank = wait_full(act, key)
                for t in range(TT):
                    last = a_.activation(R1v[:, t, c:c + 512], bank[:, t * 512:(t + 1) * 512], ACT.Copy,
                                         scale=SMALL[:, 74 + t:75 + t])
                last.then_inc(free_sem(key), 1)

            drain_mem("mk", 0)
            wait_drained(act, "mk")
            square_heads(R1v[:, :, 0:512], SQ[:, 0:1024].rearrange("p (t n) -> p t n", t=TT), 128)
            drain_mem("mv", 512)
            drain("cq", by_token(PJ3, PJ_CQ, 384))
            drain("small", by_token(PJ3, PJ_KI, 360))
            wait_drained(act, "cq")
            wait_drained(act, "small")
            act.wait_ge(rows_normed, 2)
            for t in range(TT):
                for j, (c, w) in enumerate(((PJ_CQ, 384), (PJ_CKV, 256))):
                    junk = ((SM[:, 0:384], SM[:, 384:640]), (SM[:, 640:1024], EX[:, 768:1024]))[t][j]
                    last = a_.activation(junk, PJ3[:, t, c:c + w], ACT.Square, scale=w ** -0.5,
                                         accum_out=SMALL[:, 68 + 2 * t + j:69 + 2 * t + j])
            last.then_inc(rows_squared, 1)
            drain("qi", by_token(PJ3, PJ_QI))
            drain("uq0", by_token(QB, 0))
            drain("uq1", by_token(QB, 512, 256))
            wait_drained(act, "uq1")
            square_heads(QB, SQ[:, 0:1536].rearrange("p (t n) -> p t n", t=TT), 96)
            for g in range(2):
                drain(f"ukv{g}", [(T[:, t, 4 * g:4 * g + 4, :],
                                   lambda b, t=t, a=a: b[:, t * 512:(t + 1) * 512].rearrange("p (h a d) -> p h a d", h=4, a=2)[:, :, a, :])
                                  for t in range(TT) for a, T in enumerate((KNB, VB))])
            act.wait_ge(pads_cleared, 1)
            for t in range(TT):
                drain_padded(("qi", t), QPAD)
                drain(("ki", t), [(KIT[:, t * P:(t + 1) * P], lambda b: b[:, 0:P])])
            act.wait_ge(kb_joined, 1)
            square_heads(R2[:, 0:1536], SQ[:, 0:1536], 96)
            drain("qa", by_token(PJ3, PJ_QA))
            for n in range(8):
                nk = keys_of(n // 4)
                bank = wait_full(act, ("dots", n))
                if n >= 2:
                    act.wait_ge(relu_used, n - 1)
                a_.activation(buf(SM, n)[:, 0:2 * nk], bank[:, 0:2 * nk], ACT.Relu).then_inc(free_sem(("dots", n)), 1)
            drain("ka", by_token(PJ3, PJ_KA))
            wait_drained(act, "ka")
            wait_drained(act, "qa")
            square_heads(PJ3[:, :, 0:1024], SQ[:, :].rearrange("p (t n) -> p t n", t=TT), 64)
            drain("va", by_token(PJ3, PJ_VA))

            def tanh_of(key, dst, cols_=lambda b: b[:, :], done=None):
                bank = wait_full(act, key)
                a_.activation(dst, cols_(bank), ACT.Tanh, scale=0.5).then_inc(done or tanh_ready, 1)

            tanh_of("za", ZT[:, 0:1024])
            for t in range(TT):
                drain_padded(("qa", t), QPAD)
                drain_turned(("ka", t), KT4, 4)
            soften("A", 0, 8)
            tanh_of("zb", ZT[:, 1024:2048])
            soften("A", 8)
            drain("qm", by_token(PJ3, PJ_QM))
            wait_drained(act, "qm")
            square_heads(PJ3[:, :, PJ_QM:PJ_QM + 512], SQ[:, 0:1024].rearrange("p (t n) -> p t n", t=TT), 128)
            for t in range(TT):
                for h in range(2):
                    drain_turned(("qb", t, h), QBT[:, 4 * h:4 * h + 4, :], 4, 96)
                    drain_turned(("kb", t, h), KBT[:, 4 * h:4 * h + 4, :], 4, 96)
            soften("B", 0, 8)
            tanh_of("zm", ZT[:, 2048:3072])
            soften("B", 8)
            for t in range(TT):
                drain_turned(("qm", t), QMT, 4)
                drain_turned(("km", t), KMT, 4)
            by_half = lambda b: b[:, :].rearrange("p (t n) -> p t n", t=TT)
            tanh_of("gate00", TH[0], by_half, free_sem("gate00"))
            soften("M", 0, 2)
            wait_drained(act, ("O", first_unit["M"] - 1))
            tanh_of("gate01", TH[1], by_half, free_sem("gate01"))
            soften("M", 2)
            for n in (1, 2):
                for h in range(2):
                    wait_drained(act, f"wb{n - 1}{h}")
                    tanh_of(f"gate{n}{h}", TH[h], by_half, free_sem(f"gate{n}{h}"))
            wait_drained(act, "wb21")
            act.wait_ge(rows_squared, 3)
            square_rows(2, R1v, R3v, [(mem2_landed, 16)])
            act.wait_ge(rows_normed, 4)
            square_rows(3, X3, ZTv, ["wout0", "wout1"])
            drain("ckv0", by_token(R1v, 0))
            drain("gr", [(GRT[:, :], lambda b: b[0:16, 0:S])])
            bank = wait_full(act, "gqk")
            a_.activation(GQ, bank[:, 0:512], ACT.Copy, scale=64 ** -0.5)
            a_.activation(GK, bank[:, 512:1024], ACT.Copy).then_inc(free_sem("gqk"), 1)
            bank = wait_full(act, "gate_z")
            for h in range(2):
                last = a_.activation(LZ[:, h * S:(h + 1) * S], bank[:, h * S:(h + 1) * S], ACT.Identity,
                                     bias=GC[:, GC_GATEB + h:GC_GATEB + h + 1])
            last.then_inc(free_sem("gate_z"), 1)
            wait_drained(act, "gate_z")
            link(a_.activation(LA, LZ, ACT.Abs))
            link(a_.activation(LA, LA, ACT.Exp, scale=-1.0))
            a_.activation(LA, LA, ACT.Ln, bias=1.0).then_inc(decay_a, 1)
            drain("dq", by_token(DQ, 0))
            drain("dk", by_token(DK, 0))
            wait_drained(act, "dk")
            wait_drained(act, "dq")
            act.wait_ge(decay_a, 2)
            a_.activation(EP, LC, ACT.Exp)
            a_.activation(EN, LC, ACT.Exp, scale=-1.0)
            a_.activation(EE, LE, ACT.Exp)
            a_.activation(EL, LSUM, ACT.Exp).then_inc(decay_e, 1)
            square_heads(PJ[:, 0:2048], SQ[:, :], 64)
            drain("gv", by_token(GV, 0))
            drain("ckv1", by_token(R1v, 512))
            act.wait_ge(pads_cleared, 5)
            for t in range(TT):
                drain_padded(("dq", t), QPAD)
                drain_turned(("dk", t), KT4, 4)
            act.wait_ge(lambda_dots, 1)
            a_.activation(SMALL[:, 50:52], SMALL[:, 48:50], ACT.Exp).then_inc(lambda_exp, 1)
            tanh_of("gg", GG, by_half)
            drain("dv", by_token(DV, 0))
            act.wait_ge(heads_normed, 6)
            for t in range(TT):
                drain(("gla", t), [(OG[:, t, :], lambda b: b[:, :])])
            wait_drained(act, ("gla", 1))
            square_heads(OG, SQ[:, 0:1024].rearrange("p (t n) -> p t n", t=TT), 128)
            soften("DA", 0, 2)
            act.wait_ge(gla_products, 1)
            act.wait_ge(gla_padded, 1)
            drain("ckv2", by_token(R3v, 0))
            soften("DA", 2)
            for k in range(2):
                wait_drained(act, ("O", first_unit["C"] - 1 - k))
            square_heads(MIXA, SQ[:, 0:1024].rearrange("p (t n) -> p t n", t=TT), 128)
            for h in (1, 0):
                for t in range(TT):
                    drain_turned(("mix", t, h), XT3[:, 4 * h:4 * h + 4, :], 4)
            drain("ckv3", by_token(R3v, 512))
            square_heads(R1[:, :], SQ[:, :], 256)
            for t in range(TT):
                square_rows(4, X3, ZTv, [("wo", t)], [t])
            CQN = v2(R2)
            for t in range(TT):
                for h in range(2):
                    key = ("wcq", t, h)
                    bank = wait_full(act, key)
                    square_heads(bank[:, 0:512], SQ[:, t * D + h * 512:t * D + h * 512 + 512], 256)
                    drain(key, [(CQN[:, t, h * 512:(h + 1) * 512], lambda b: b[:, 0:512])])
                if t:
                    for k in range(TT):
                        for h in range(2):
                            drain_turned(("xk", k, h), CK8[:, 4 * h:4 * h + 4, :], 4)
                for h in range(2):
                    drain_turned(("xq", t, h), CQ8[:, 4 * h:4 * h + 4, :], 4)
            soften("C")
            for t in range(TT):
                square_rows(5, X3, ZTv, [("wco", t)], [t])
            act.wait_ge(route_exp, 1)
            a_.activation(R_exp, R_dif, ACT.Exp).then_inc(route_exp, 1)

            act.wait_ge(moe_gathered, 1)
            for h in range(2):
                last = a_.activation(M_rows[:, h * 512:(h + 1) * 512], AUX[h][:, :], ACT.Copy)
            last.then_inc(moe_rows, 1)

            def serve_pair(after, last=False):
                act.wait_ge(moe_gate, after(1))
                a_.activation(M_th, AUX[2][:, :], ACT.Tanh, scale=0.5).then_inc(moe_tanh, 1)
                if not last:
                    act.wait_ge(moe_gathered, after(2))
                    for h in range(2):
                        ins = a_.activation(M_rows[:, h * 512:(h + 1) * 512], AUX[h][:, :], ACT.Copy)
                    ins.then_inc(moe_rows, 1)
                act.wait_ge(moe_picks_turned, after(2))
                a_.activation(M_place, AUX[3][:, 0:256], ACT.Copy).then_inc(moe_picks_t, 1)
                act.wait_ge(moe_down, after(1))
                for h in range(2):
                    a_.activation(M_o[:, h * 512:(h + 1) * 512], AUX[2 + h][:, :], ACT.Copy).then_inc(moe_out[h], 1)

            with act.Fori(0, PAIRS - 1) as i:
                serve_pair(lambda k: i + k)
            serve_pair(lambda k: PAIRS - 1 + k, last=True)
            act.wait_ge(flag_ready, 1)
            fullest = act.value_load(FLAG[0:1, 0:1])
            with act.If(fullest > CAP):
                with act.Fori(0, N_EXPERTS * TT) as u:
                    act.wait_ge(all_gate, u + 1)
                    a_.activation(M_th, AUX[0][:, :], ACT.Tanh, scale=0.5).then_inc(all_tanh, 1)
            act.wait_ge(y_done, 1)
            a_.activation(OUT[:, 1, :], ACC[1][:, :], ACT.Copy).then_inc(out_ready2, 1)

        @block.vector
        def _(dve):
            v = nc.vector
            steps = [0]

            def link(ins):
                steps[0] += 1
                ins.then_inc(dve_steps, 1)
                dve.wait_ge(dve_steps, steps[0])

            def rsqrt(n, src):
                x, y, a, b = (NW[:, i * 32:i * 32 + n] for i in range(4))
                link(v.tensor_scalar(x, src, EPS, None, ALU.add))
                link(v.tensor_scalar(NWI[:, 0:n], x.bitcast(I32), 1, None, ALU.logical_shift_right))
                seed = v.tensor_scalar(y.bitcast(I32), NWI[:, 0:n], -1.0, RSQRT_SEED, ALU.mult, ALU.add)
                if n > 1:
                    link(seed)
                if n == 1:
                    link(v.tensor_scalar(a, x, -0.5, None, ALU.mult))
                for k in range(3):
                    if n == 1:
                        link(v.scalar_tensor_tensor(out=b, in0=y, scalar=y, in1=a, op0=ALU.mult, op1=ALU.mult))
                    else:
                        link(v.tensor_tensor(a, y, y, ALU.mult))
                        link(v.scalar_tensor_tensor(out=b, in0=a, scalar=-0.5, in1=x, op0=ALU.mult, op1=ALU.mult))
                    dst = RS[:, 0:n] if k == 2 else y
                    link(v.scalar_tensor_tensor(out=dst, in0=b, scalar=1.5, in1=y, op0=ALU.add, op1=ALU.mult))

            def norm_rows(n, src, dst, squared):
                dve.wait_ge(rows_squared, squared)
                rsqrt(2, SMALL[:, 64:66])
                for t in range(TT):
                    v.tensor_scalar(dst[:, t, :], src[:, t, :], RS[:, t:t + 1], None, ALU.mult).then_inc(rows_normed, 1)

            def norm_tile(t, src, dst, squared):
                dve.wait_ge(rows_squared, squared)
                rsqrt(1, SMALL[:, 64 + t:65 + t])
                v.tensor_scalar(dst[:, t, :], src[:, t, :], RS[:, 0:1], None, ALU.mult).then_inc(rows_normed, 1)

            def drain_rows(name, dst, gain, tiles=range(TT)):
                for t in tiles:
                    for h in range(2):
                        key = (name, t, h)
                        bank = wait_full(dve, key)
                        v.tensor_tensor(dst[:, 4 * h:4 * h + 4, t * P:(t + 1) * P],
                                        bank[:, :].rearrange("p (k q) -> p k q", k=4),
                                        GC[:, gain + 4 * h:gain + 4 * h + 4].unsqueeze(2).broadcast_to([P, 4, P]),
                                        ALU.mult).then_inc(free_sem(key), 1)

            sq_calls = [0]

            def norm_heads(squares, groups, w, apply, n_gains):
                sq_calls[0] += 1
                dve.wait_ge(squares_ready, sq_calls[0])
                v.tensor_reduce(MS[:, 0:groups], squares.rearrange("p (g w) -> p g w", g=groups), AX_X,
                                ALU.add).then_inc(squares_used, 1)
                dve.wait_ge(squares_used, sq_calls[0])
                rsqrt(groups, MS[:, 0:groups])
                apply()

            def scale_heads(view, c0, h):
                w = view.shape[2]
                return v.tensor_tensor(view, view, RS[:, c0:c0 + h].unsqueeze(2).broadcast_to([P, h, w]), ALU.mult)

            def gain_heads(view, c, factor=None):
                h, w = view.shape[1], view.shape[2]
                gb = GB[:, c:c + w].unsqueeze(1).broadcast_to([P, h, w])
                if factor is None:
                    return v.tensor_tensor(view, view, gb, ALU.mult)
                return v.scalar_tensor_tensor(out=view, in0=view, scalar=factor, in1=gb, op0=ALU.mult, op1=ALU.mult)

            def hv(ap, h):
                return ap.rearrange("p (h w) -> p h w", h=h)

            def mask_scores(name, u, t, h):
                nk = keys_of(t)
                bank = wait_full(dve, ("S", u))
                if u >= 4:
                    wait_full(dve, ("T", u - 4))
                m = blocks(u, nk)
                b = bank[:, 0:2 * nk].rearrange("p (i k) -> p i k", i=2)
                mask = {"A": None if t is None else SEL3[:, t or 0, 0:nk], "B": causal[:, S - nk:S],
                        "DA": causal[:, S - nk:S]}.get(name)
                if mask is None:
                    ins = v.tensor_scalar(m, b, scales[name], None, ALU.mult)
                else:
                    ins = v.scalar_tensor_tensor(out=m, in0=b, scalar=scales[name],
                                                 in1=mask.unsqueeze(1).broadcast_to([P, 2, nk]), op0=ALU.mult, op1=ALU.add)
                ins.then_inc(free_sem(("S", u)), 1)
                wait_drained(dve, ("S", u))
                v.tensor_reduce(stat(u, 0), m, AX_X, ALU.max, negate=True).then_inc(masked, 1)

            def normalize(name, u, t, h):
                nk = keys_of(t)
                dve.wait_ge(exped, u + 1)
                e = blocks(u, nk)
                link(v.reciprocal(stat(u, 2), stat(u, 1)))
                if name == "DA":
                    link(v.tensor_scalar(e[:, 0, :], e[:, 0, :], stat(u, 2)[:, 0:1], None, ALU.mult))
                    link(v.tensor_scalar(stat(u, 2)[:, 1:2], stat(u, 2)[:, 1:2], SMALL[:, 54:55], None, ALU.mult))
                    v.scalar_tensor_tensor(out=e[:, 0, :], in0=e[:, 1, :], scalar=stat(u, 2)[:, 1:2], in1=e[:, 0, :],
                                           op0=ALU.mult, op1=ALU.add).then_inc(normed, 1)
                else:
                    v.tensor_tensor(e, e, stat(u, 2).unsqueeze(2).broadcast_to([P, 2, nk]), ALU.mult).then_inc(normed, 1)

            def take_output(name, u, t, h):
                bank = wait_full(dve, ("O", u))
                free = free_sem(("O", u))
                if name in ("A", "B"):
                    y = YT[:, 4 * (name == "B") + h, t * P:(t + 1) * P]
                    for i in range(2):
                        r = slice(64 * i, 64 * i + 64)
                        ins = v.tensor_tensor(y[r], bank[r, i * P:(i + 1) * P], y[r], ALU.mult)
                elif name == "M":
                    ins = v.tensor_tensor(YT[:, 8 + h, :], bank[:, 0:S], YT[:, 8 + h, :], ALU.mult)
                elif name == "DA":
                    ins = v.tensor_copy(MIXA[:, t, h * P:(h + 1) * P], bank[:, 0:P])
                else:
                    ins = v.tensor_copy(XT3[:, 2 * h:2 * h + 2, :], bank[:, :].rearrange("p (d q) -> p d q", d=2))
                ins.then_inc(free, 1)

            def attention(name, a=0, b=None):
                U = len(units[name])
                for s in range(a, U + 3 if b is None else b):
                    for lag, step in ((0, mask_scores), (1, normalize), (3, take_output)):
                        if 0 <= s - lag < U:
                            step(name, first_unit[name] + s - lag, *units[name][s - lag])

            tanhs = [0]

            def silu_t(key, dst):
                tanhs[0] += 1
                dve.wait_ge(tanh_ready, tanhs[0])
                bank = wait_full(dve, key)
                v.scalar_tensor_tensor(out=dst, in0=dst, scalar=1.0, in1=bank[:, :], op0=ALU.add,
                                       op1=ALU.mult).then_inc(free_sem(key), 1)

            dve.wait_ge(consts_ready, 1)
            bank = wait_full(dve, "gains")
            v.tensor_copy(GC[:, :], bank[:, 0:GC_N]).then_inc(free_sem("gains"), 1)
            wait_drained(dve, "gains")
            drain_rows("mem", R2T, GC_MEM)
            dve.wait_ge(rows_squared, 1)
            rsqrt(2, SMALL[:, 64:66])
            v.tensor_copy(SMALL[:, 74:76], RS[:, 0:2]).then_inc(mem_scaled, 1)
            norm_rows(1, X3, ZTv, 2)
            drain_rows("x0", XT3, GC_NORM)
            posf = NW[:, 0:2]
            ang, turns, sin_a, cos_a = (trig[:, 32 * i:32 * i + 32] for i in range(4))
            dve.wait_ge(small_landed, small_total)
            link(v.tensor_copy(posf, pos_i[:, :]))
            for t in range(TT):
                ins = v.tensor_scalar(ang[:, 16 * t:16 * t + 16], freq[:, :], posf[:, t:t + 1], None, ALU.mult)
            link(ins)
            for arg, shift in ((sin_a, 0.0), (cos_a, 0.25)):
                link(v.tensor_scalar(turns, ang, 1.0 / (2 * math.pi), shift, ALU.mult, ALU.add))
                link(v.tensor_scalar(turns, turns, 12582912.0, 12582912.0, ALU.add, ALU.subtract))
                link(v.scalar_tensor_tensor(out=arg, in0=turns, scalar=-6.28125, in1=ang, op0=ALU.mult, op1=ALU.add))
                for part in (2029 / 2 ** 20, 2 * math.pi - 6.28125 - 2029 / 2 ** 20):
                    link(v.scalar_tensor_tensor(out=arg, in0=turns, scalar=-part, in1=arg, op0=ALU.mult, op1=ALU.add))
                if shift:
                    link(v.tensor_scalar(arg, arg, math.pi / 2, None, ALU.add))
                v.tensor_scalar(arg, arg, 3.1415925, -3.1415925, ALU.min, ALU.max).then_inc(trig_arg, 1)
                dve.wait_ge(trig_arg, 2 if shift else 1)

            def apply_km():
                for t in range(TT):
                    ins = scale_heads(hv(R1v[:, t, 0:512], 4), 4 * t, 4)
                link(ins)
                for t in range(TT):
                    ins = gain_heads(hv(R1v[:, t, 0:512], 4), GB_M + 128)
                ins.then_inc(heads_normed, 1)

            norm_heads(SQ[:, 0:1024], 8, 128, apply_km, 1)
            dve.wait_ge(rows_squared, 3)
            rsqrt(4, SMALL[:, 68:72])
            for t in range(TT):
                v.tensor_scalar(PJ3[:, t, PJ_CQ:PJ_CQ + 384], PJ3[:, t, PJ_CQ:PJ_CQ + 384], RS[:, 2 * t:2 * t + 1], None, ALU.mult)
                ins = v.tensor_scalar(PJ3[:, t, PJ_CKV:PJ_CKV + 256], PJ3[:, t, PJ_CKV:PJ_CKV + 256],
                                      RS[:, 2 * t + 1:2 * t + 2], None, ALU.mult)
            ins.then_inc(latents_normed, 1)
            for t in range(TT):
                for name, n, dst, gain in (("cq", 3, CQT, GC_CQ), ("ckv", 2, CKVT, GC_CKV)):
                    bank = wait_full(dve, (name, t))
                    v.tensor_tensor(dst[:, :, t * P:(t + 1) * P], bank[:, 0:n * P].rearrange("p (k q) -> p k q", k=n),
                                    GC[:, gain:gain + n].unsqueeze(2).broadcast_to([P, n, P]),
                                    ALU.mult).then_inc(free_sem((name, t)), 1)
            link(v.tensor_scalar(WI, PJ3[:, :, PJ_WI:PJ_WI + 8], 64 ** -0.5 * 8 ** -0.5, None, ALU.mult))

            def apply_heads(per_tile, gain, count=True):
                for t in range(TT):
                    view, c = per_tile(t)
                    ins = scale_heads(view, c, view.shape[1])
                link(ins)
                for t in range(TT):
                    view, c = per_tile(t)
                    ins = gain_heads(view, gain)
                ins.then_inc(heads_normed, 1)

            norm_heads(SQ[:, 0:1536], 16, 96, lambda: apply_heads(lambda t: (hv(QB[:, t, :], 8), 8 * t), GB_B), 1)
            norm_heads(SQ[:, 0:1536], 16, 96, lambda: apply_heads(lambda t: (KB[:, t, :, :], 8 * t), GB_B + 96), 1)
            for n in range(8):
                t = n // 4
                nk = keys_of(t)
                wait_drained(dve, ("dots", n))
                for i in range(2):
                    h = 2 * (n % 4) + i
                    r = buf(SM, n)[:, i * nk:(i + 1) * nk]
                    acc_ = IX3[:, t, 0:nk]
                    if h == 0:
                        ins = v.tensor_scalar(acc_, r, WI[:, t, h:h + 1], None, ALU.mult)
                    else:
                        ins = v.scalar_tensor_tensor(out=acc_, in0=r, scalar=WI[:, t, h:h + 1], in1=acc_,
                                                     op0=ALU.mult, op1=ALU.add)
                    if i == 0:
                        link(ins)
                ins.then_inc(relu_used, 1)
                dve.wait_ge(relu_used, n + 1)
            for t in range(TT):
                nk = keys_of(t)
                ins = v.tensor_tensor(IX3[:, t, 0:nk], IX3[:, t, 0:nk], causal[:, S - nk:S], ALU.add)
            link(ins)
            best = NW[:, 0:16].rearrange("p (t n) -> p t n", t=TT)
            for k in range(TOPK // 8):
                for t in range(TT):
                    ins = v.max(best[:, t, :], IX3[:, t, 0:keys_of(t)])
                link(ins)
                for t in range(TT):
                    ins = v.match_replace(IX3[:, t, 0:keys_of(t)], best[:, t, :], IX3[:, t, 0:keys_of(t)], TAKEN)
                link(ins)
            for t in range(TT):
                nk = keys_of(t)
                ins = v.tensor_scalar(IX3[:, t, 0:nk], IX3[:, t, 0:nk], -2e38, NEG, ALU.is_gt, ALU.mult)
            link(ins)
            for t in range(TT):
                nk = keys_of(t)
                ins = v.tensor_tensor(SEL3[:, t, 0:nk], IX3[:, t, 0:nk], causal[:, S - nk:S], ALU.add)
            link(ins)

            def apply_a(q, k, g0):
                def go():
                    for t in range(TT):
                        ins = scale_heads(q(t), 16 * t, 16) if k is None else None
                        if k is not None:
                            scale_heads(q(t), 8 * t, 8)
                            ins = scale_heads(k(t), 16 + 8 * t, 8)
                    link(ins)
                    for t in range(TT):
                        if k is None:
                            gain_heads(q(t)[:, 0:8, :], g0)
                            ins = gain_heads(q(t)[:, 8:16, :], g0 + 64)
                        else:
                            gain_heads(q(t), g0)
                            ins = gain_heads(k(t), g0 + 64)
                    ins.then_inc(heads_normed, 1)
                return go

            norm_heads(SQ[:, :], 32, 64, apply_a(lambda t: hv(PJ3[:, t, 0:1024], 16), None, GB_A), 2)
            silu_t("za", ZT[:, 0:1024])
            attention("A", 0, 9)
            silu_t("zb", ZT[:, 1024:2048])
            attention("A", 9)
            norm_heads(SQ[:, 0:1024], 8, 128,
                       lambda: apply_heads(lambda t: (hv(PJ3[:, t, PJ_QM:PJ_QM + 512], 4), 4 * t), GB_M), 1)
            attention("B", 0, 9)
            silu_t("zm", ZT[:, 2048:3072])
            attention("B", 9)
            attention("M")
            for n in range(3):
                for h in range(2):
                    dst = R1v[:, :, h * 512:(h + 1) * 512]
                    tmp = R4[:, 0:1024].rearrange("p (t n) -> p t n", t=TT)
                    key = f"wb{n}{h}"
                    wait_drained(dve, f"gate{n}{h}")
                    bank = wait_full(dve, key)
                    ins = v.scalar_tensor_tensor(out=dst if n == 0 else tmp, in0=TH[h], scalar=1.0,
                                                 in1=bank[:, :].rearrange("p (t n) -> p t n", t=TT), op0=ALU.add, op1=ALU.mult)
                    ins.then_inc(free_sem(key), 1)
                    if n:
                        wait_drained(dve, key)
                        ins = v.tensor_tensor(dst, dst, tmp, ALU.add)
                        if n == 2:
                            ins.then_inc(merged_ready, 1)
                            dve.wait_ge(merged_ready, h + 1)
                        else:
                            link(ins)
            for t in range(TT):
                for h in range(2):
                    key = ("merged", t, h)
                    bank = wait_full(dve, key)
                    v.tensor_copy(XT3[:, 4 * h:4 * h + 4, t * P:(t + 1) * P],
                                  bank[:, :].rearrange("p (k q) -> p k q", k=4)).then_inc(free_sem(key), 1)

            def add_to_x(key, h, factor):
                bank = wait_full(dve, key)
                x = X3[:, :, h * 512:(h + 1) * 512]
                v.scalar_tensor_tensor(out=x, in0=bank[:, :].rearrange("p (t n) -> p t n", t=TT), scalar=factor, in1=x,
                                       op0=ALU.mult, op1=ALU.add).then_inc(free_sem(key), 1)
                wait_drained(dve, key)

            norm_rows(2, R1v, R3v, 4)
            add_to_x("wout0", 0, 0.25)
            drain_rows("mem2", R2T, GC_MEM2)
            add_to_x("wout1", 1, 0.25)
            norm_rows(3, X3, ZTv, 5)
            drain_rows("x1", XT3, GC_MIX)
            lam = GB[:, GB_LAM:GB_LAM + 256].rearrange("p (a b d) -> p a b d", a=2, b=2)
            link(v.tensor_tensor(lam[:, :, 0, :], lam[:, :, 0, :], lam[:, :, 1, :], ALU.mult))
            v.tensor_reduce(SMALL[:, 48:50], lam[:, :, 0, :], AX_X, ALU.add).then_inc(lambda_dots, 1)
            dve.wait_ge(decay_a, 1)
            link(v.tensor_scalar(LZ, LZ, 0.0, 1 / 16, ALU.min, ALU.mult))
            link(v.scalar_tensor_tensor(out=LG_, in0=LA, scalar=-1 / 16, in1=LZ, op0=ALU.mult, op1=ALU.add))
            for c in range(8):
                one = slice(64 * c, 64 * c + 64)
                ins = v.tensor_tensor_scan(LSUM[:, one], ones[:, 0:64], LG_[:, one], 0.0, ALU.mult, ALU.add)
            link(ins)
            chunked_ = lambda ap: ap.rearrange("p (c i) -> p c i", i=CHUNK)
            ls = chunked_(LSUM)
            v.tensor_tensor(chunked_(LC), ls, ls[:, :, 31:32].broadcast_to([P, 8, CHUNK]), ALU.subtract)
            v.tensor_tensor(chunked_(LE), ls[:, :, 63:64].broadcast_to([P, 8, CHUNK]), ls, ALU.subtract).then_inc(decay_a, 1)
            dve.wait_ge(decay_e, 1)
            dve.wait_ge(pads_cleared, 4)
            link(v.tensor_copy(DEC, chunked_(EL)[:, :, 63]))
            for dst, a, b in ((KNZ, GK, EN), (KPZ, GK, EP), (QLZ, GQ, EL)):
                for i in range(2):
                    r = slice(64 * i, 64 * i + 64)
                    ins = v.tensor_tensor(dst.rearrange("p (h i) q -> p h i q", i=2)[r, :, i, :], kt(a, 2)[r], kt(b, 2)[r],
                                          ALU.mult)
            ins.then_inc(gla_padded, 1)
            norm_heads(SQ[:, :], 32, 64, apply_a(lambda t: hv(DQ[:, t, :], 8), lambda t: hv(DK[:, t, :], 8), GB_DA), 2)
            for t in range(TT):
                bank = wait_full(dve, ("intra", t))
                pb = bank[:, :].rearrange("p (a h q) -> p a h q", a=2, h=4)
                link(v.copy_predicated(ATT[:, t, :, :], past[:, :].bitcast(U32).unsqueeze(1).broadcast_to([P, 4, P]), pb[:, 0]))
                v.copy_predicated(ATT[:, t, :, :], future[:, :].bitcast(U32).unsqueeze(1).broadcast_to([P, 4, P]),
                                  pb[:, 1]).then_inc(free_sem(("intra", t)), 1)
            bank = wait_full(dve, "kend")
            kb_ = bank[:, :].rearrange("p (n d) -> p n d", n=4)
            v.tensor_copy(KEN[0:64, 0, :, :], kb_[0:64])
            v.tensor_copy(KEN[64:128, 1, :, :], kb_[64:128]).then_inc(free_sem("kend"), 1)
            dve.wait_ge(tanh_ready, 4)
            bank = wait_full(dve, "gg")
            v.scalar_tensor_tensor(out=GG, in0=GG, scalar=1.0, in1=bank[:, :].rearrange("p (t n) -> p t n", t=TT),
                                   op0=ALU.add, op1=ALU.mult).then_inc(free_sem("gg"), 1)
            for c in range(3):
                bank = wait_full(dve, ("state", c))
                for h in range(2):
                    for i in range(2):
                        r = slice(64 * i, 64 * i + 64)
                        u_ = bank[r, h * 256 + i * P:h * 256 + (i + 1) * P]
                        if c == 0:
                            ins = v.tensor_copy(ST[r, c, h, :], u_)
                        else:
                            ins = v.scalar_tensor_tensor(out=ST[r, c, h, :], in0=ST[r, c - 1, h, :],
                                                         scalar=DEC[r, 4 * h + c:4 * h + c + 1], in1=u_, op0=ALU.mult, op1=ALU.add)
                ins.then_inc(free_sem(("state", c)), 1)
                wait_drained(dve, ("state", c))
            dve.wait_ge(lambda_exp, 1)
            link(v.tensor_tensor(SMALL[:, 53:54], SMALL[:, 51:52], SMALL[:, 50:51], ALU.subtract))
            link(v.tensor_scalar(SMALL[:, 54:55], SMALL[:, 53:54], -LAM_INIT, None, ALU.add))

            def apply_out(view, gain, factor):
                def go():
                    for t in range(TT):
                        ins = scale_heads(hv(view[:, t, :], 4), 4 * t, 4)
                    link(ins)
                    for t in range(TT):
                        ins = gain_heads(hv(view[:, t, :], 4), gain, factor)
                    ins.then_inc(heads_normed, 1)
                return go

            attention("DA", 0, 2)
            norm_heads(SQ[:, 0:1024], 8, 128, apply_out(OG, GB_GLAO, 0.5), 1)
            dve.wait_ge(heads_normed, 7)
            v.tensor_tensor(GG, GG, OG, ALU.mult).then_inc(mix_ready, 1)
            attention("DA", 2)
            norm_heads(SQ[:, 0:1024], 8, 128, apply_out(MIXA, GB_DAO, 1.0 - LAM_INIT), 1)

            def apply_cross(T, gain, drained=None):
                def go():
                    if drained:
                        wait_drained(dve, drained)
                    for h in range(T.shape[1] // 256):
                        head = T[:, 256 * h:256 * h + 256]
                        ins = v.scalar_tensor_tensor(out=head, in0=head, scalar=RS[:, h:h + 1], in1=GB[:, gain:gain + 256],
                                                     op0=ALU.mult, op1=ALU.mult)
                    ins.then_inc(heads_normed, 1)
                return go

            norm_heads(SQ[:, :], 8, 256, apply_cross(R1[:, :], GB_X + 256), 1)

            def add_tile(key, t):
                bank = wait_full(dve, (key, t))
                v.tensor_tensor(X3[:, t, :], bank[:, :], X3[:, t, :], ALU.add).then_inc(free_sem((key, t)), 1)
                wait_drained(dve, (key, t))

            for t in range(TT):
                add_tile("wo", t)
                norm_tile(t, X3, ZTv, 6 + t)
                drain_rows("x2", XT3, GC_CROSS, [t])
            for t in range(TT):
                for h in range(2):
                    c = slice(t * D + h * 512, t * D + h * 512 + 512)
                    norm_heads(SQ[:, c], 2, 256, apply_cross(R2[:, c], GB_X, ("wcq", t, h)), 1)
            attention("C")
            for t in range(TT):
                add_tile("wco", t)
                norm_tile(t, X3, ZTv, 8 + t)
                drain_rows("x3", XT3, GC_FFN, [t])

            b4 = lambda ap, n: ap.unsqueeze(2).broadcast_to([P, TT, n])
            bank = wait_full(dve, "router")
            v.tensor_tensor(R_log, bank[:, 0:72].rearrange("p (t n) -> p t n", t=TT),
                            GB[:, GB_ROUTE:GB_ROUTE + 36].unsqueeze(1).broadcast_to([P, TT, 36]),
                            ALU.add).then_inc(free_sem("router"), 1)
            wait_drained(dve, "router")
            lg, le = R_log[:, :, 0:4], R_log[:, :, 4:36].rearrange("p t (g j) -> p t g j", g=4)

            def first_best(x, n, m, w, one, pr):
                link(v.tensor_reduce(m, x, AX_X, ALU.max))
                link(v.tensor_tensor(w, x, b4(m, n), ALU.is_equal))
                link(v.tensor_tensor(w, w, pr.unsqueeze(1).broadcast_to([P, TT, n]), ALU.mult))
                link(v.tensor_reduce(R_m, w, AX_X, ALU.max))
                link(v.tensor_tensor(one, w, b4(R_m, n), ALU.is_equal))

            first_best(lg, 4, R_m1, R_w4, R_gs, pref[:, 8:12])
            link(v.tensor_tensor(R_dif4, lg, b4(R_m1, 4), ALU.subtract))
            link(v.tensor_tensor(R_big, le, R_gs.unsqueeze(3).broadcast_to([P, TT, 4, 8]), ALU.mult))
            link(v.tensor_reduce(R_el, R_big.rearrange("p t g j -> p t j g"), AX_X, ALU.add))
            first_best(R_el, 8, R_m1, R_w8, R_s1, pref[:, 0:8])
            link(v.scalar_tensor_tensor(out=R_el, in0=R_s1, scalar=NEG, in1=R_el, op0=ALU.mult, op1=ALU.add))
            first_best(R_el, 8, R_m2, R_w8, R_s2, pref[:, 0:8])
            v.tensor_tensor(R_dif2, R_m2, R_m1, ALU.subtract).then_inc(route_exp, 1)
            dve.wait_ge(route_exp, 2)
            link(v.tensor_reduce(R_m1, R_exp4, AX_X, ALU.add))
            link(v.scalar_tensor_tensor(out=R_m2, in0=R_exp2, scalar=1.0, in1=R_m1, op0=ALU.add, op1=ALU.mult))
            link(v.reciprocal(R_m1, R_m2))
            link(v.tensor_tensor(R_m2, R_m1, R_exp2, ALU.mult))
            link(v.tensor_tensor(R_w8, R_s1, b4(R_m1, 8), ALU.mult))
            link(v.tensor_tensor(R_el, R_s2, b4(R_m2, 8), ALU.mult))
            link(v.tensor_tensor(R_w8, R_w8, R_el, ALU.add))
            link(v.tensor_tensor(R_s1, R_s1, R_s2, ALU.add))
            for t in range(TT):
                for dst, src in ((R_gate[:, t, 0:32], R_w8), (R_sel[:, t, :], R_s1)):
                    ins = v.tensor_tensor(hv(dst, 4), R_gs[:, t, :].unsqueeze(2).broadcast_to([P, 4, 8]),
                                          src[:, t, :].unsqueeze(1).broadcast_to([P, 4, 8]), ALU.mult)
            v.memset(R_gate[:, :, 32:34], 0.0)
            v.memset(R_rank[:, :, 32:34], -1.0)
            ins.then_inc(route_ready, 1)
            bank = wait_full(dve, "ranks")
            link(v.tensor_reduce(R_m[:, 0:1], bank[:, 64:96], AX_X, ALU.max))
            v.tensor_copy(FLAG[:, :], R_m[:, 0:1]).then_inc(flag_ready, 1)
            rk = R_rank[:, :, 0:32]
            link(v.scalar_tensor_tensor(out=rk, in0=bank[:, 0:64].rearrange("p (t n) -> p t n", t=TT), scalar=1.0,
                                        in1=R_sel, op0=ALU.add, op1=ALU.mult))
            link(v.tensor_scalar(rk, rk, -1.0, None, ALU.add))
            link(v.tensor_scalar(R_over, rk, CAP - 0.5, 0.5, ALU.is_gt, ALU.mult))
            v.tensor_tensor(R_over, R_over, R_gate[:, :, 0:32], ALU.mult).then_inc(free_sem("ranks"), 1)
            wait_drained(dve, "ranks")

            pl = iota[:, :].unsqueeze(1).broadcast_to([P, 2, CAP])

            def picks(dst, t, first):
                return v.tensor_tensor(dst[:, t, :].rearrange("p (e c) -> p e c", e=2), pl,
                                       R_rank[:, t, first].unsqueeze(2).broadcast_to([P, 2, CAP]), ALU.is_equal)

            def take_input():
                for h in range(2):
                    ins = v.tensor_tensor(M_xt[:, 4 * h:4 * h + 4, :], AUX[h][:, :].rearrange("p (k c) -> p k c", k=4),
                                          GC[:, GC_FFN + 4 * h:GC_FFN + 4 * h + 4].unsqueeze(2).broadcast_to([P, 4, P]), ALU.mult)
                ins.then_inc(moe_input, 1)

            picks(M_pick, 0, slice(0, 2))
            picks(M_pick, 1, slice(0, 2)).then_inc(moe_picks, 1)
            dve.wait_ge(moe_rows_turned, 1)
            take_input()

            def gate_pair(after, first, last=False):
                dve.wait_ge(moe_picks_turned, after(1))
                picks(M_gpick, 0, first(0))
                picks(M_gpick, 1, first(0)).then_inc(moe_weighting, 1)
                dve.wait_ge(moe_weighting, after(0) * 2 + 1)
                for t in range(TT):
                    ins = v.tensor_tensor(M_gpick[:, t, :].rearrange("p (e c) -> p e c", e=2),
                                          M_gpick[:, t, :].rearrange("p (e c) -> p e c", e=2),
                                          R_gate[:, t, first(0)].unsqueeze(2).broadcast_to([P, 2, CAP]), ALU.mult)
                ins.then_inc(moe_weighting, 1)
                if not last:
                    dve.wait_ge(moe_gathered, after(1))
                    picks(M_pick, 0, first(2))
                    picks(M_pick, 1, first(2)).then_inc(moe_picks, 1)
                dve.wait_ge(moe_tanh, after(1))
                v.scalar_tensor_tensor(out=M_hid, in0=M_th, scalar=1.0, in1=AUX[2][:, :], op0=ALU.add,
                                       op1=ALU.mult).then_inc(moe_gated, 1)
                dve.wait_ge(moe_gated, after(1))
                dve.wait_ge(moe_up, after(1))
                v.scalar_tensor_tensor(out=M_hid, in0=M_hid, scalar=0.5, in1=AUX[3][:, :], op0=ALU.mult,
                                       op1=ALU.mult).then_inc(moe_hidden, 1)
                dve.wait_ge(moe_turned, after(1))
                v.tensor_copy(M_hidt, AUX[2][:, :].rearrange("p (k c) -> p k c", k=4)).then_inc(moe_hidden_t, 1)
                if not last:
                    dve.wait_ge(moe_rows_turned, after(2))
                    take_input()

            with dve.Fori(0, PAIRS - 1) as i:
                gate_pair(lambda k: i + k, lambda k: bass.ds(i * 2 + k, 2))
            gate_pair(lambda k: PAIRS - 1 + k, lambda k: slice(N_EXPERTS - 2, N_EXPERTS), last=True)
            dve.wait_ge(flag_ready, 1)
            fullest = dve.value_load(FLAG[0:1, 0:1])
            with dve.If(fullest > CAP):
                dve.wait_ge(all_rows_turned, 1)
                for t in range(TT):
                    for h in range(2):
                        ins = v.tensor_tensor(XT3[:, 4 * h:4 * h + 4, t * P:(t + 1) * P],
                                              AUX[2 * t + h][:, :].rearrange("p (k q) -> p k q", k=4),
                                              GC[:, GC_FFN + 4 * h:GC_FFN + 4 * h + 4].unsqueeze(2).broadcast_to([P, 4, P]),
                                              ALU.mult)
                ins.then_inc(all_input, 1)
                with dve.Fori(0, N_EXPERTS) as e:
                    for t in range(TT):
                        dve.wait_ge(all_tanh, e * 2 + t + 1)
                        v.scalar_tensor_tensor(out=M_hid, in0=M_th, scalar=1.0, in1=AUX[0][:, :], op0=ALU.add,
                                               op1=ALU.mult).then_inc(all_gated, 1)
                        dve.wait_ge(all_gated, e * 2 + t + 1)
                        v.scalar_tensor_tensor(out=M_hid, in0=M_hid, scalar=R_over[:, t, bass.ds(e, 1)], in1=AUX[1][:, :],
                                               op0=ALU.mult, op1=ALU.mult).then_inc(all_hidden, 1)
                        dve.wait_ge(all_turned, e * 2 + t + 1)
                        v.tensor_copy(M_hidt, AUX[2][:, :].rearrange("p (k c) -> p k c", k=4)).then_inc(all_hidden_t, 1)
            dve.wait_ge(y_done, 1)
            v.tensor_copy(OUT[:, 0, :], ACC[0][:, :]).then_inc(out_ready, 1)


_INS = ["x", "mem", "positions", "g_norm", "w_in", "g_qn_a", "g_kn_a", "g_cq", "g_ckv", "w_uq", "w_ukv", "g_qn_b",
        "g_kn_b", "g_mem", "w_mem_kv", "g_qn_m", "g_kn_m", "w_branch", "w_out", "mem_2", "norm_mix_2", "w_in_2",
        "da_q_norm_2", "da_k_norm_2", "lambda_q1_2", "lambda_k1_2", "lambda_q2_2", "lambda_k2_2", "da_out_norm_2",
        "gla_gate_w_2", "gla_gate_b_2", "gla_out_norm_2", "w_o_2", "norm_cross_2", "norm_mem_2", "w_cq_2", "w_ckv_2",
        "cross_q_norm_2", "cross_k_norm_2", "w_co_2", "norm_ffn_2", "w_group_2", "b_group_2", "w_expert_2", "b_expert_2",
        "w_e_gate_2", "w_e_up_2", "w_e_down_2"]


def kernel(**inputs):
    import numpy as _np
    import concourse.bacc as _bacc
    from concourse import mybir as _mybir
    from concourse.bass_utils import run_bass_kernel_spmd as _run

    nc = _bacc.Bacc("TRN2", target_bir_lowering=False, num_devices=1)
    arrays, args = {}, {}
    for name in _INS:
        a = _np.ascontiguousarray(inputs[name])
        arrays[f"in_{name}_dram"] = a
        args[name] = nc.dram_tensor(f"in_{name}_dram", a.shape, _mybir.dt.from_np(a.dtype), kind="ExternalInput").ap()
    out = nc.dram_tensor("out_0_dram", (1, S, D), F32, kind="ExternalOutput").ap()
    two_block_layer(nc, args, out)
    r = _run(nc, [arrays], core_ids=[0])
    return r.results[0]["out_0_dram"]
```
